# Optimizing a Trainium2 kernel written in Bass

```python
import jax, jax.numpy as jnp
from jax import lax
import numpy as np

D_MODEL = 1024
BATCH = 1
SEQ = 1024
DEPTH = 1
DEC_BATCH = 1
DEC_SEQ = 512
PAST_LEN = 128

N_HEADS_M = 4
DH_M = 256
W_M = N_HEADS_M * DH_M
CHUNK = 64
N_HEADS_A = 16
N_KV_A = 4
GROUP_A = N_HEADS_A // N_KV_A
DH_A = 64
W_A = N_HEADS_A * DH_A
Q_BLOCK = 128
GRID_W = 64
AXIS_DIM = DH_A // 2
ROPE_THETA = 10000.0
EPS = 1e-6

SPLIT_SIZES = (W_M, W_M, W_M, W_M, W_M, 4 * N_HEADS_M,
               W_A, N_KV_A * DH_A, N_KV_A * DH_A, W_A, D_MODEL, D_MODEL)
N_IN_COLS = sum(SPLIT_SIZES)

kernel_name = "hybrid_mlstm_gqa_axial_encoder"

def _rmsnorm(x, g):
    xf = x.astype(jnp.float32)
    y = xf * lax.rsqrt(jnp.mean(xf * xf, axis=-1, keepdims=True) + EPS) * g.astype(jnp.float32)
    return y.astype(x.dtype)

def _mlstm_dir(q, k, v, ig, lf):
    B, H, S, Dh = q.shape
    NC = S // CHUNK

    def chunks(t):
        return jnp.moveaxis(t.reshape(B, H, NC, CHUNK, *t.shape[3:]), 2, 0)

    lower = jnp.tril(jnp.ones((CHUNK, CHUNK), dtype=bool))

    def step(carry, xs):
        C, n, m = carry
        qc, kc, vc, ic, fc = xs
        b = jnp.cumsum(fc, axis=-1)
        dlog = jnp.where(lower, b[..., :, None] - b[..., None, :] + ic[..., None, :], -jnp.inf)
        g = b + m[..., None]
        mt = jnp.maximum(g, jnp.max(dlog, axis=-1))
        s = jnp.einsum('bhtd,bhsd->bhts', qc, kc) * jnp.exp(dlog - mt[..., None])
        inter = jnp.exp(g - mt)
        num = jnp.einsum('bhts,bhsd->bhtd', s, vc) + inter[..., None] * jnp.einsum('bhek,bhtk->bhte', C, qc)
        den = jnp.sum(s, axis=-1) + inter * jnp.einsum('bhk,bhtk->bht', n, qc)
        h = num / jnp.maximum(jnp.abs(den), jnp.exp(-mt))[..., None]
        bL = b[..., -1]
        wl = bL[..., None] - b + ic
        m_new = jnp.maximum(bL + m, jnp.max(wl, axis=-1))
        decay = jnp.exp(bL + m - m_new)
        ws = jnp.exp(wl - m_new[..., None])
        C_new = decay[..., None, None] * C + jnp.einsum('bhse,bhsk->bhek', vc * ws[..., None], kc)
        n_new = decay[..., None] * n + jnp.einsum('bhs,bhsk->bhk', ws, kc)
        return (C_new, n_new, m_new), h

    init = (jnp.zeros((B, H, Dh, Dh), jnp.float32), jnp.zeros((B, H, Dh), jnp.float32),
            jnp.zeros((B, H), jnp.float32))
    _, hs = lax.scan(step, init, (chunks(q), chunks(k), chunks(v), chunks(ig), chunks(lf)))
    return jnp.moveaxis(hs, 0, 2).reshape(B, H, S, Dh)

def _rope_axis(seg, pos):
    half = AXIS_DIM // 2
    freqs = ROPE_THETA ** (-jnp.arange(0, AXIS_DIM, 2, dtype=jnp.float32) / AXIS_DIM)
    ang = pos.astype(jnp.float32)[:, None] * freqs[None, :]
    cos = jnp.cos(ang)[None, :, None, :]
    sin = jnp.sin(ang)[None, :, None, :]
    x1, x2 = seg[..., :half], seg[..., half:]
    return jnp.concatenate([x1 * cos - x2 * sin, x2 * cos + x1 * sin], axis=-1)

def _rope_2d(x, rows, cols):
    return jnp.concatenate([_rope_axis(x[..., :AXIS_DIM], rows), _rope_axis(x[..., AXIS_DIM:], cols)], axis=-1)

def _head_rms(x, g):
    return x * lax.rsqrt(jnp.mean(x * x, axis=-1, keepdims=True) + EPS) * g.astype(jnp.float32)

def _encoder_layer(x, w_in, b_if, norm_pre, q_gain, k_gain, w_mo, w_ao, w_out):
    B, S, _ = x.shape
    f32 = jnp.float32
    h = _rmsnorm(x, norm_pre)
    p = h @ w_in
    idx = [int(i) for i in np.cumsum(SPLIT_SIZES)[:-1]]
    q_m, k_m, v_m, o_m, z_m, if_raw, q_a, k_a, v_a, z_a, g_m, g_a = jnp.split(p, idx, axis=-1)

    if_pre = if_raw.astype(f32).reshape(B, S, 2, 2, N_HEADS_M) + b_if.astype(f32)
    ig = jnp.transpose(if_pre[:, :, :, 0], (2, 0, 3, 1))
    lf = jnp.transpose(jax.nn.log_sigmoid(if_pre[:, :, :, 1]), (2, 0, 3, 1))

    def to_heads(t):
        return t.astype(f32).reshape(B, S, N_HEADS_M, DH_M).transpose(0, 2, 1, 3)

    qm, km, vm = to_heads(q_m), to_heads(k_m) * (DH_M ** -0.5), to_heads(v_m)
    h_f = _mlstm_dir(qm, km, vm, ig[0], lf[0])
    flip = lambda t: jnp.flip(t, axis=2)
    h_b = flip(_mlstm_dir(flip(qm), flip(km), flip(vm), flip(ig[1]), flip(lf[1])))
    h_mem = (h_f + h_b).transpose(0, 2, 1, 3).reshape(B, S, W_M)
    y_m = (h_mem * jax.nn.sigmoid(o_m.astype(f32)) * jax.nn.silu(z_m.astype(f32))).astype(x.dtype) @ w_mo

    ROWS = S // GRID_W
    rows = jnp.broadcast_to(jnp.arange(ROWS)[:, None], (ROWS, GRID_W)).reshape(-1)
    cols = jnp.broadcast_to(jnp.arange(GRID_W)[None, :], (ROWS, GRID_W)).reshape(-1)
    qa = _rope_2d(_head_rms(q_a.astype(f32).reshape(B, S, N_HEADS_A, DH_A), q_gain), rows, cols)
    ka = _rope_2d(_head_rms(k_a.astype(f32).reshape(B, S, N_KV_A, DH_A), k_gain), rows, cols)
    va = v_a.astype(f32).reshape(B, S, N_KV_A, DH_A)
    nqb = S // Q_BLOCK
    qblocks = jnp.moveaxis(qa.reshape(B, nqb, Q_BLOCK, N_KV_A, GROUP_A, DH_A), 1, 0)
    scale = DH_A ** -0.5

    def attend(qb):
        sc = jnp.einsum('bqkgd,bskd->bkgqs', qb, ka) * scale
        pr = jax.nn.softmax(sc, axis=-1)
        return jnp.einsum('bkgqs,bskd->bqkgd', pr, va)

    att = jnp.moveaxis(lax.map(attend, qblocks), 0, 1).reshape(B, S, W_A)
    y_a = (att * jax.nn.silu(z_a.astype(f32))).astype(x.dtype) @ w_ao

    merged = jax.nn.sigmoid(g_m) * y_m + jax.nn.sigmoid(g_a) * y_a
    return x + merged @ w_out

def setup_inputs(seed: int = 0) -> dict:
    key = jax.random.key(seed)
    ks = jax.random.split(key, 14)
    nrm = jax.random.normal
    x_prompt = nrm(ks[0], (BATCH, SEQ, D_MODEL), jnp.float32)
    x_sample = nrm(ks[1], (DEC_BATCH, DEC_SEQ, D_MODEL), jnp.float32)
    w_in = nrm(ks[2], (DEPTH, D_MODEL, N_IN_COLS), jnp.float32) * D_MODEL ** -0.5
    ib = 0.1 * nrm(ks[3], (DEPTH, 2, 1, N_HEADS_M), jnp.float32)
    fb = jnp.linspace(3.0, 6.0, N_HEADS_M, dtype=jnp.float32) + 0.1 * nrm(ks[4], (DEPTH, 2, 1, N_HEADS_M), jnp.float32)
    b_if = jnp.concatenate([ib, fb], axis=2)
    norm_pre = 1.0 + 0.05 * nrm(ks[5], (DEPTH, D_MODEL), jnp.float32)
    q_gain = 1.0 + 0.05 * nrm(ks[6], (DEPTH, DH_A), jnp.float32)
    k_gain = 1.0 + 0.05 * nrm(ks[7], (DEPTH, DH_A), jnp.float32)
    w_mo = nrm(ks[8], (DEPTH, W_M, D_MODEL), jnp.float32) * W_M ** -0.5
    w_ao = nrm(ks[9], (DEPTH, W_A, D_MODEL), jnp.float32) * W_A ** -0.5
    w_out = nrm(ks[10], (DEPTH, D_MODEL, D_MODEL), jnp.float32) * D_MODEL ** -0.5
    norm_final = 1.0 + 0.05 * nrm(ks[11], (D_MODEL,), jnp.float32)
    return {"x_prompt": x_prompt, "x_sample": x_sample, "w_in": w_in, "b_if": b_if,
            "norm_pre": norm_pre, "q_gain": q_gain, "k_gain": k_gain, "w_mo": w_mo,
            "w_ao": w_ao, "w_out": w_out, "norm_final": norm_final}

def reference(x_prompt, x_sample, w_in, b_if, norm_pre, q_gain, k_gain, w_mo, w_ao, w_out, norm_final):
    xp, xs = x_prompt, x_sample
    for l in range(DEPTH):
        xp = _encoder_layer(xp, w_in[l], b_if[l], norm_pre[l], q_gain[l], k_gain[l], w_mo[l], w_ao[l], w_out[l])
        xs = _encoder_layer(xs, w_in[l], b_if[l], norm_pre[l], q_gain[l], k_gain[l], w_mo[l], w_ao[l], w_out[l])
    y_prompt = _rmsnorm(xp, norm_final)
    y_sample = _rmsnorm(xs, norm_final)
    return (y_prompt, y_sample)


_drawn_inputs = setup_inputs


def setup_inputs(seed=0):
    import zlib

    import numpy as np

    out = dict(_drawn_inputs(seed))
    spreads = {}
    factors = {'q_gain': 8.0, 'k_gain': 8.0, 'w_ao': 2.946}
    for name, (base, spread) in spreads.items():
        noise = np.random.default_rng([zlib.crc32(name.encode()), seed]).standard_normal(out[name].shape)
        drawn = base * np.exp(spread * noise) if base else spread * noise
        out[name] = __import__('jax').numpy.asarray(drawn.astype(out[name].dtype))
    for name, factor in factors.items():
        out[name] = (out[name] * factor).astype(out[name].dtype)
    return out
```

```python
import concourse.bass as bass
from concourse import mybir
from contextlib import ExitStack

F32 = mybir.dt.float32
F32R = mybir.dt.float32r
ALU = mybir.AluOpType
ACT = mybir.ActivationFunctionType
AX = mybir.AxisListType

P = 128
D = 1024
SEQS = (1024, 512)
T = sum(SEQS)
TT = T // P
CH = 512
NCH = T // CH
KT = D // P
HM, DM = 4, 256
HA, KVA, DA = 16, 4, 64
GRP = HA // KVA
EPS = 1e-6
W_M, W_A, W_KV = HM * DM, HA * DA, KVA * DA
C_QM, C_VM, C_OM, C_ZM = 0, 2 * W_M, 3 * W_M, 4 * W_M
C_IF = 5 * W_M
C_QA = C_IF + 4 * HM
C_KVA = C_QA + W_A
C_ZA = C_KVA + 2 * W_KV
C_GM = C_ZA + W_A
R_QM, R_OM, R_ZM, R_ZA, R_GM, R_END = 0, 2 * W_M, 3 * W_M, 4 * W_M, 4 * W_M + W_A, 4 * W_M + W_A + 2 * D
S_VM, S_QA, S_KVA, S_END = 0, W_M, W_M + W_A, W_M + W_A + 2 * W_KV

UNIT = 512
CB = UNIT // P
NB = 6
NG = 12
QUADS = NG // 4


class Scope(ExitStack):

    def __init__(self, nc, tag):
        super().__init__()
        self.nc, self.tag, self.used = nc, tag, []
        self.callback(self.clear)

    def clear(self):
        self.nc.clear_and_free_semaphores(self.used)
        self.nc.all_engine_barrier()

    def sb(self, name, shape, dt=F32):
        return self.enter_context(self.nc.sbuf_tensor(f"{self.tag}_{name}", shape, dt))

    def pb(self, name, shape, dt=F32):
        return self.enter_context(self.nc.psum_tensor(f"{self.tag}_{name}", shape, dt))

    def sem(self, name):
        self.used.append(self.nc.alloc_semaphore(f"{self.tag}_{name}"))
        return self.used[-1]

    def sems(self, name, n):
        return [self.sem(f"{name}{i}") for i in range(n)]


def make_identity(nc, pool, ident, sem):
    nc.gpsimd.memset(ident[:], 0.0).then_inc(sem, 1)
    pool.wait_ge(sem, 1)
    nc.gpsimd.affine_select(out=ident[:], in_=ident[:], compare_op=ALU.not_equal, fill=1.0,
                            base=0, pattern=[[-1, P]], channel_multiplier=1).then_inc(sem, 1)


class Gemm:

    def __init__(self, sc):
        self.act_hi = sc.sb("act_hi", [P, KT, T], F32R)
        self.act_lo = sc.sb("act_lo", [P, KT, T], F32R)
        self.w_hi = sc.sb("w_hi", [P, 2, KT, UNIT], F32R)
        self.w_lo = sc.sb("w_lo", [P, 2, KT, UNIT], F32R)
        self.raw = sc.sb("raw", [P, KT, UNIT])
        self.stage = sc.sb("stage", [P, QUADS, 4, CH])
        self.acc = [sc.pb(f"acc{b}", [P, CH]) for b in range(NB)]
        self.raw_loaded = sc.sem("raw_loaded")
        self.hi_split = sc.sems("hi_split", 2)
        self.lo_split = sc.sems("lo_split", 2)
        self.acc_full = sc.sems("acc_full", 2)
        self.evacuated = sc.sems("evacuated", NB)
        self.stored = sc.sems("stored", QUADS)


def load_unit(sp, g, w_cols, slot, pair, width=UNIT):
    sp.wait_ge(g.lo_split[1 - slot], KT * (pair + slot))
    sp.dma_start(g.raw[:, :, 0:width], w_cols).then_inc(g.raw_loaded, 16)


def split_hi_unit(nc, dve, g, slot, pair, width=UNIT):
    dve.wait_ge(g.raw_loaded, 16 * (2 * pair + slot + 1))
    dve.wait_ge(g.acc_full[slot], NG * pair)
    for k in range(KT):
        nc.vector.tensor_copy(g.w_hi[:, slot, k, 0:width], g.raw[:, k, 0:width]).then_inc(g.hi_split[slot], 1)


def split_lo_unit(nc, pool, g, slot, pair, width=UNIT):
    for k in range(KT):
        pool.wait_ge(g.hi_split[slot], KT * pair + k + 1)
        nc.gpsimd.tensor_sub(g.w_lo[:, slot, k, 0:width], g.raw[:, k, 0:width],
                             g.w_hi[:, slot, k, 0:width].bitcast(F32)).then_inc(g.lo_split[slot], 1)


def product(nc, pe, out, stat_hi, stat_lo, mov_hi, mov_lo, before_k=None):
    for k in range(KT):
        if before_k:
            before_k(k)
        nc.tensor.matmul(out, stat_hi(k), mov_hi(k), start=(k == 0), stop=False)
        nc.tensor.matmul(out, stat_hi(k), mov_lo(k), start=False, stop=False)
        last = nc.tensor.matmul(out, stat_lo(k), mov_hi(k), start=False, stop=(k == KT - 1))
    return last


def multiply_unit(nc, pe, g, slot, pair, features, groups=NG, act_ready=None):
    for n in range(groups):
        b = n % NB
        pe.wait_ge(g.evacuated[b], 2 * (2 * pair + slot) + n // NB)

        def before_k(k, n=n):
            if n == 0:
                pe.wait_ge(g.hi_split[slot], KT * pair + k + 1)
                pe.wait_ge(g.lo_split[slot], KT * pair + k + 1)
            if act_ready:
                act_ready(n, k)

        if features:
            c, cb = (n // CB, n % CB) if groups == NG else (n, 0)
            t, m = slice(c * CH, (c + 1) * CH), slice(cb * P, (cb + 1) * P)
            last = product(nc, pe, g.acc[b][:], lambda k: g.w_hi[:, slot, k, m], lambda k: g.w_lo[:, slot, k, m],
                           lambda k: g.act_hi[:, k, t], lambda k: g.act_lo[:, k, t], before_k)
        else:
            t = slice(n * P, (n + 1) * P)
            last = product(nc, pe, g.acc[b][:], lambda k: g.act_hi[:, k, t], lambda k: g.act_lo[:, k, t],
                           lambda k: g.w_hi[:, slot, k, :], lambda k: g.w_lo[:, slot, k, :], before_k)
        last.then_inc(g.acc_full[slot], 1)


def drain_unit(nc, act, g, slot, pair, func, out_quad):
    unit = 2 * pair + slot
    for q in range(QUADS):
        act.wait_ge(g.stored[q], 16 * unit)
        for j in range(4):
            n = 4 * q + j
            act.wait_ge(g.acc_full[slot], NG * pair + n + 1)
            nc.scalar.activation(g.stage[:, q, j, :], g.acc[n % NB][:], func).then_inc(g.evacuated[n % NB], 1)
        for j in range(4):
            n = 4 * q + j
            act.wait_ge(g.evacuated[n % NB], 2 * unit + n // NB + 1)
        act.dma_start(out_quad(q), g.stage[:, q]).then_inc(g.stored[q], 16)


def project(nc, x, w_in, norm_pre, p_feat, p_tok, gate_rows):
    with Scope(nc, "a") as sc:
        g = Gemm(sc)
        gain = sc.sb("gain", [P, D])
        ident = sc.sb("ident", [P, P])
        stat = sc.sb("stat", [P, 3, 4])
        flip = [sc.pb(f"flip{i}", [P, 4, P]) for i in range(2)]
        room = g.stage[:].rearrange("p a b c -> p (a b c)")
        xt = [room[:, j * D:(j + 1) * D] for j in range(3)]
        ht = [room[:, (3 + j) * D:(4 + j) * D] for j in range(3)]
        x_loaded = sc.sems("x_loaded", 3)
        gain_loaded = sc.sem("gain_loaded")
        ident_made = sc.sem("ident_made")
        squared = sc.sem("squared")
        mean_made = sc.sem("mean_made")
        root_made = sc.sem("root_made")
        rstd_made = sc.sem("rstd_made")
        h_made = sc.sem("h_made")
        flipped_a = sc.sem("flipped_a")
        flipped_b = sc.sems("flipped_b", 3)
        act_hi_made = sc.sems("act_hi_made", 2)
        act_lo_made = sc.sems("act_lo_made", 2)
        w_cols = w_in.rearrange("(k p) n -> p k n", p=P)

        feature_runs = [(C_QM, 2, ACT.Copy, R_QM), (C_OM, 1, ACT.Sigmoid, R_OM), (C_ZM, 1, ACT.Silu, R_ZM),
                        (C_ZA, 1, ACT.Silu, R_ZA), (C_GM, 2, ACT.Sigmoid, R_GM)]
        token_runs = [(C_VM, S_VM), (C_QA, S_QA)]
        runs = [(True, *r) for r in feature_runs] + [(False, c, 1, ACT.Copy, s) for c, s in token_runs]

        def over_pairs(eng, body):
            pair = 0
            for run in runs:
                if run[2] > 1:
                    with eng.Fori(0, run[2]) as i:
                        body(run, i + pair, i)
                else:
                    body(run, pair, 0)
                pair += run[2]
            return pair

        with nc.Block() as block:

            @block.sync
            def _(sp):
                sp.dma_start(gain[:], norm_pre.to_broadcast([P, D])).then_inc(gain_loaded, 16)
                with sp.Fori(0, TT // 3) as i:
                    for j in range(3):
                        sp.wait_ge(flipped_b[j], i)
                        sp.dma_start(xt[j], x[bass.ds(i * 3 * P + j * P, P), :]).then_inc(x_loaded[j], 16)

                def body(run, pair, i):
                    for slot in range(2):
                        load_unit(sp, g, w_cols[:, :, bass.ds(i * 2 * UNIT + run[1] + slot * UNIT, UNIT)], slot, pair)

                last = over_pairs(sp, body)
                load_unit(sp, g, w_cols[:, :, C_KVA:C_KVA + UNIT], 0, last)
                load_unit(sp, g, w_cols[:, :, C_IF:C_IF + P], 1, last, P)

            @block.gpsimd
            def _(pool):
                make_identity(nc, pool, ident, ident_made)

                def body(run, pair, i):
                    for slot in range(2):
                        split_lo_unit(nc, pool, g, slot, pair)

                last = over_pairs(pool, body)
                split_lo_unit(nc, pool, g, 0, last)
                split_lo_unit(nc, pool, g, 1, last, P)

            @block.vector
            def _(dve):
                dve.wait_ge(gain_loaded, 16)
                with dve.Fori(0, TT // 3) as i:
                    for j in range(3):
                        t = i * 3 + j
                        dve.wait_ge(squared, t + 1)
                        nc.vector.tensor_scalar(stat[:, j, 1:2], stat[:, j, 0:1], 1.0 / D, EPS, ALU.mult, ALU.add)\
                            .then_inc(mean_made, 1)
                        dve.wait_ge(root_made, t + 1)
                        nc.vector.reciprocal(stat[:, j, 3:4], stat[:, j, 2:3]).then_inc(rstd_made, 1)
                        dve.wait_ge(rstd_made, t + 1)
                        dve.wait_ge(x_loaded[j], 16 * (i + 1))
                        nc.vector.scalar_tensor_tensor(out=ht[j], in0=xt[j], scalar=stat[:, j, 3:4], in1=gain[:],
                                                       op0=ALU.mult, op1=ALU.mult).then_inc(h_made, 1)
                        for half in range(2):
                            dve.wait_ge(act_hi_made[half], t + 1)
                            cols = bass.ds(i * 3 * P + j * P, P)
                            nc.vector.tensor_sub(g.act_lo[:, 4 * half:4 * half + 4, cols], flip[half][:],
                                                 g.act_hi[:, 4 * half:4 * half + 4, cols].bitcast(F32))\
                                .then_inc(act_lo_made[half], 1)

                def body(run, pair, i):
                    for slot in range(2):
                        split_hi_unit(nc, dve, g, slot, pair)

                last = over_pairs(dve, body)
                split_hi_unit(nc, dve, g, 0, last)
                split_hi_unit(nc, dve, g, 1, last, P)

            @block.scalar
            def _(act):
                with act.Fori(0, TT // 3) as i:
                    for j in range(3):
                        t = i * 3 + j
                        act.wait_ge(x_loaded[j], 16 * (i + 1))
                        act.wait_ge(flipped_b[j], i)
                        nc.scalar.activation(ht[j], xt[j], ACT.Square, accum_out=stat[:, j, 0:1]).then_inc(squared, 1)
                        act.wait_ge(mean_made, t + 1)
                        nc.scalar.activation(stat[:, j, 2:3], stat[:, j, 1:2], ACT.Sqrt).then_inc(root_made, 1)
                        for half in range(2):
                            if half:
                                act.wait_ge(flipped_b[j], i + 1)
                            else:
                                act.wait_ge(flipped_a, t + 1)
                            nc.scalar.activation(g.act_hi[:, 4 * half:4 * half + 4, bass.ds(i * 3 * P + j * P, P)],
                                                 flip[half][:], ACT.Copy).then_inc(act_hi_made[half], 1)

                def body(run, pair, i):
                    features, _, _, func, at = run
                    for slot in range(2):
                        if features:
                            rows = p_feat[bass.ds(i * 2 * UNIT + at + slot * UNIT, UNIT), :]
                            rows = rows.rearrange("(b p) t -> p b t", p=P)
                            drain_unit(nc, act, g, slot, pair, func, lambda q: rows[:, :, q * CH:(q + 1) * CH])
                        else:
                            cols = p_tok[:, at + slot * UNIT:at + (slot + 1) * UNIT]
                            cols = cols.rearrange("(b p) c -> p b c", p=P)
                            drain_unit(nc, act, g, slot, pair, func, lambda q: cols[:, 4 * q:4 * q + 4, :])

                last = over_pairs(act, body)
                cols = p_tok[:, S_KVA:S_END].rearrange("(b p) c -> p b c", p=P)
                drain_unit(nc, act, g, 0, last, ACT.Copy, lambda q: cols[:, 4 * q:4 * q + 4, :])
                act.wait_ge(g.stored[0], 16 * (2 * last + 1))
                for c in range(NCH):
                    act.wait_ge(g.acc_full[1], NG * last + c + 1)
                    nc.scalar.activation(g.stage[0:4 * HM, 0, c, :], g.acc[c][0:4 * HM, :], ACT.Copy)\
                        .then_inc(g.evacuated[c], 1)
                for c in range(NCH):
                    act.wait_ge(g.evacuated[c], 2 * (2 * last + 1) + 1)
                act.dma_start(gate_rows.rearrange("r (c t) -> r c t", t=CH),
                              g.stage[0:4 * HM, 0, 0:NCH, :]).then_inc(g.stored[0], 16)
                act.wait_ge(g.stored[0], 16 * (2 * last + 2))
                for q in range(1, QUADS):
                    act.wait_ge(g.stored[q], 16 * (2 * last + 1))

            @block.tensor
            def _(pe):
                pe.wait_ge(ident_made, 2)
                with pe.Fori(0, TT // 3) as i:
                    for j in range(3):
                        t = i * 3 + j
                        pe.wait_ge(h_made, t + 1)
                        for half in range(2):
                            pe.wait_ge(act_lo_made[half], t)
                            for k in range(4):
                                col = (4 * half + k) * P
                                last = nc.tensor.transpose(flip[half][:, k, :], ht[j][:, col:col + P], ident[:])
                            last.then_inc(flipped_b[j] if half else flipped_a, 1)
                for half in range(2):
                    pe.wait_ge(act_lo_made[half], TT)

                def body(run, pair, i):
                    for slot in range(2):
                        multiply_unit(nc, pe, g, slot, pair, run[0])

                last = over_pairs(pe, body)
                multiply_unit(nc, pe, g, 0, last, False)
                multiply_unit(nc, pe, g, 1, last, True, NCH)


NDIR = 2
HALF = 32


def prepare_gates(nc, gate_rows, b_if, neg_max, floor, a_cols):
    with Scope(nc, "g") as sc:
        rows = 2 * HALF
        i_raw, f_raw = sc.sb("i_raw", [rows, T]), sc.sb("f_raw", [rows, T])
        i_bias, f_bias = sc.sb("i_bias", [rows, 1]), sc.sb("f_bias", [rows, 1])
        i_pre, f_pre = sc.sb("i_pre", [rows, T]), sc.sb("f_pre", [rows, T])
        soft = sc.sb("soft", [rows, T])
        ones = sc.sb("ones", [rows, T])
        cum, a_run, m_run, shift = (sc.sb(n, [rows, T]) for n in ("cum", "a_run", "m_run", "shift"))
        a_out, m_out, f_out = (sc.sb(n, [rows, T]) for n in ("a_out", "m_out", "f_out"))
        cols = sc.sb("cols", [P, HM, NDIR, TT])
        ident = sc.sb("ident", [P, P])
        flip = [sc.pb(f"flip{i}", [P, TT // 2, rows]) for i in range(2)]
        ident_made, zeroed, loaded, chain, acts = (sc.sem(n) for n in
                                                   ("ident_made", "zeroed", "loaded", "chain", "acts"))
        a_final, m_final, f_final, flipped, cols_made, stored = (sc.sem(n) for n in (
            "a_final", "m_final", "f_final", "flipped", "cols_made", "stored"))
        fwd, bwd = slice(0, HALF), slice(HALF, rows)
        seqs, at = [], 0
        for n in SEQS:
            seqs.append(slice(at, at + n))
            at += n
        src = gate_rows.rearrange("(d g h) t -> d g h t", d=2, g=2)
        b_v = b_if.rearrange("l d g h -> (l d) g h")

        with nc.Block() as block:

            @block.sync
            def _(sp):
                sp.wait_ge(zeroed, 4)
                for d, r in ((0, 0), (1, HALF)):
                    sp.dma_start(i_raw[r:r + HM, :], src[d, 0]).then_inc(loaded, 16)
                    sp.dma_start(f_raw[r:r + HM, :], src[d, 1]).then_inc(loaded, 16)
                    sp.dma_start(i_bias[r:r + HM, :], b_v[d, 0].rearrange("(h o) -> h o", o=1)).then_inc(loaded, 16)
                    sp.dma_start(f_bias[r:r + HM, :], b_v[d, 1].rearrange("(h o) -> h o", o=1)).then_inc(loaded, 16)
                sp.wait_ge(m_final, 3)
                for d, r in ((0, HALF), (1, 0)):
                    sp.dma_start(neg_max[:, d, :], m_out[r:r + HM, :]).then_inc(stored, 16)
                sp.wait_ge(f_final, 3)
                for d, r in ((0, HALF), (1, 0)):
                    sp.dma_start(floor[:, d, :], f_out[r:r + HM, :]).then_inc(stored, 16)
                sp.wait_ge(cols_made, 4)
                sp.dma_start(a_cols.rearrange("h p d t -> p h d t"), cols[:]).then_inc(stored, 16)
                sp.wait_ge(stored, 16 * 5)

            @block.gpsimd
            def _(pool):
                for tile in (i_raw, f_raw, i_bias, f_bias):
                    nc.gpsimd.memset(tile[:], 0.0).then_inc(zeroed, 1)
                make_identity(nc, pool, ident, ident_made)

            @block.vector
            def _(dve):
                done = [0]

                def link(ins):
                    done[0] += 1
                    ins.then_inc(chain, 1)
                    dve.wait_ge(chain, done[0])

                nc.vector.memset(ones[:], 1.0)
                dve.wait_ge(loaded, 16 * 8)
                for raw, bias, pre in ((f_raw, f_bias, f_pre), (i_raw, i_bias, i_pre)):
                    nc.vector.tensor_scalar_add(pre[fwd, :], raw[fwd, :], bias[fwd, :])
                    for s in seqs:
                        last = nc.vector.tensor_scalar_add(pre[bwd, s], raw[bwd, s][:, ::-1], bias[bwd, :])
                    link(last)
                dve.wait_ge(acts, 3)
                link(nc.vector.scalar_tensor_tensor(out=soft[:], in0=f_pre[:], scalar=0.0, in1=soft[:],
                                                    op0=ALU.min, op1=ALU.subtract))
                for s in seqs:
                    last = nc.vector.tensor_tensor_scan(out=cum[:, s], data0=ones[:, s], data1=soft[:, s], initial=0.0,
                                                        op0=ALU.mult, op1=ALU.add)
                link(last)
                link(nc.vector.tensor_sub(a_run[:], i_pre[:], cum[:]))
                for s in seqs:
                    last = nc.vector.tensor_tensor_scan(out=m_run[:, s], data0=a_run[:, s], data1=a_run[:, s],
                                                        initial=0.0, op0=ALU.max, op1=ALU.max)
                link(last)
                link(nc.vector.tensor_add(shift[:], cum[:], m_run[:]))
                nc.vector.tensor_copy(a_out[fwd, :], a_run[fwd, :]).then_inc(a_final, 1)
                for s in seqs:
                    nc.vector.tensor_copy(a_out[bwd, s], a_run[bwd, s][:, ::-1]).then_inc(a_final, 1)
                nc.vector.tensor_scalar_mul(m_out[fwd, :], m_run[fwd, :], -1.0).then_inc(m_final, 1)
                for s in seqs:
                    nc.vector.tensor_scalar_mul(m_out[bwd, s], m_run[bwd, s][:, ::-1], -1.0).then_inc(m_final, 1)
                for b in range(2):
                    dve.wait_ge(flipped, b + 1)
                    for d, r in ((0, HALF), (1, 0)):
                        nc.vector.tensor_copy(cols[:, :, d, b * TT // 2:(b + 1) * TT // 2],
                                              flip[b][:, :, r:r + HM].rearrange("p t h -> p h t"))\
                            .then_inc(cols_made, 1)

            @block.scalar
            def _(act):
                act.wait_ge(chain, 1)
                nc.scalar.activation(soft[:], f_pre[:], ACT.Abs).then_inc(acts, 1)
                act.wait_ge(acts, 1)
                nc.scalar.activation(soft[:], soft[:], ACT.Exp, scale=-1.0).then_inc(acts, 1)
                act.wait_ge(acts, 2)
                nc.scalar.activation(soft[:], soft[:], ACT.Ln, bias=1.0).then_inc(acts, 1)
                act.wait_ge(chain, 7)
                nc.scalar.activation(f_out[fwd, :], shift[fwd, :], ACT.Exp, scale=-1.0).then_inc(f_final, 1)
                for s in seqs:
                    nc.scalar.activation(f_out[bwd, s], shift[bwd, s][:, ::-1], ACT.Exp, scale=-1.0).then_inc(f_final, 1)

            @block.tensor
            def _(pe):
                pe.wait_ge(ident_made, 2)
                pe.wait_ge(a_final, 3)
                for b in range(2):
                    for t in range(TT // 2):
                        tok = (b * TT // 2 + t) * P
                        last = nc.tensor.transpose(flip[b][:, t, :], a_out[:, tok:tok + P], ident[0:rows, 0:rows])
                    last.then_inc(flipped, 1)


CHUNKS = [(0, 8, 0), (0, 8, 4), (8, 4, 8)]
BLK = CH // P
UNITS = sum(n for _, n, _ in CHUNKS)


def chunk_units(c):
    first, n, own = CHUNKS[c]
    base = sum(m for _, m, _ in CHUNKS[:c])
    for i in range(n):
        s = first + i
        yield base + i, s, i, (s - own if own <= s < own + BLK else None), s < own


def head_steps():
    def scores(c):
        return [("scores", c, u) for u in chunk_units(c)]

    def values(c):
        return [("values", c, u) for u in chunk_units(c)]

    def norm(c, steps):
        return steps[:2] + [("norm", c, None)] + steps[2:]

    def out(c):
        return [("out", c, None)]

    return (scores(0) + norm(0, scores(1)) + norm(1, values(0)) + out(0) + scores(2)
            + norm(2, values(1)) + out(1) + values(2) + out(2))


PIECES = [("k", 0), ("q", 0), ("k", 1), ("q", 1), ("v", 0), ("v", 1), ("k", 2), ("q", 2), ("v", 2)]
NPC = len(PIECES)


def pieces_before(kind, c, s):
    if kind == "scores":
        return {0: 2 if s < BLK else 3, 1: 4, 2: NPC}[c]
    return {0: 5 if s < BLK else 6, 1: 6, 2: 9}[c]


def mlstm(nc, p_feat, p_tok, neg_max, floor, a_cols, g_mem):
    with Scope(nc, "m") as sc:
        raw = {n: sc.sb(f"raw_{n}", [P, 2, T] if n != "v" else [P, TT, DM]) for n in "qkv"}
        hi = {n: sc.sb(f"hi_{n}", [P, 2, T] if n != "v" else [P, TT, DM], F32R) for n in "qkv"}
        lo = {n: sc.sb(f"lo_{n}", [P, 2, T] if n != "v" else [P, TT, DM], F32R) for n in "qkv"}
        a_col = sc.sb("a_col", [P, NDIR, TT])
        nmax = [sc.sb(f"nmax{b}", [P, NDIR, CH]) for b in range(2)]
        norm = [sc.sb(f"norm{b}", [P, NDIR, CH]) for b in range(2)]
        wsum = [sc.sb(f"wsum{b}", [P, NDIR, CH]) for b in range(2)]
        wbuf = [sc.sb(f"wbuf{b}", [P, 8, CH + P]) for b in range(2)]
        dec = [sc.sb(f"dec{b}", [P, BLK + 1, P]) for b in range(2)]
        arg = [sc.sb(f"arg{b}", [P, NDIR, P]) for b in range(2)]
        w_hi = [sc.sb(f"w_hi{b}", [P, CH], F32R) for b in range(2)]
        w_lo = [sc.sb(f"w_lo{b}", [P, CH], F32R) for b in range(2)]
        gate_o, gate_z, out_s = (sc.sb(n, [P, 2, CH]) for n in ("gate_o", "gate_z", "out_s"))
        mask = sc.sb("mask", [P, NDIR, P])
        ones = sc.sb("ones", [P, P])
        scr = [sc.pb(f"scr{b}", [P, CH]) for b in range(4)]
        den = sc.pb("den", [P, NDIR, CH])
        hout = sc.pb("hout", [P, 2, CH])

        mask_made, ones_made = sc.sem("mask_made"), sc.sem("ones_made")
        raw_loaded = {n: sc.sem(f"raw_loaded_{n}") for n in "qkv"}
        col_loaded = sc.sem("col_loaded")
        nmax_loaded, norm_loaded = sc.sems("nmax_loaded", 2), sc.sems("norm_loaded", 2)
        gates_loaded = sc.sem("gates_loaded")
        piece_hi, piece_lo = sc.sem("piece_hi"), sc.sem("piece_lo")
        scored = sc.sem("scored")
        arg_made = sc.sem("arg_made")
        dec_made = sc.sems("dec_made", 2)
        weighed = sc.sems("weighed", 4)
        wsum_zeroed = sc.sem("wsum_zeroed")
        wsum_step = sc.sem("wsum_step")
        den_full = sc.sem("den_full")
        abs_made = sc.sem("abs_made")
        max_made, norm_made = sc.sem("max_made"), sc.sem("norm_made")
        scaled_part, scaled = sc.sem("scaled_part"), sc.sem("scaled")
        whi_made, wlo_made = sc.sems("whi_made", 2), sc.sems("wlo_made", 2)
        valued = sc.sems("valued", 2)
        out_read, out_made, out_stored = sc.sem("out_read"), sc.sem("out_made"), sc.sem("out_stored")

        steps = head_steps()
        own_no = {u: n for n, u in enumerate(u for c in range(3) for u, _, _, j, _ in chunk_units(c) if j is not None)}
        OWN = len(own_no)
        half = UNITS // 2
        wsum_count, n_w = {}, 0
        for kind, c, u in steps:
            if kind == "scores":
                n_w += 1 if u[3] is None else (3 if u[3] < BLK - 1 else 2)
                wsum_count[c] = n_w
        WS = n_w

        def feat(row, h, c):
            v = p_feat[bass.ds(h * DM + row, DM), c * CH:(c + 1) * CH]
            return v.rearrange("(b p) t -> p b t", p=P)

        with nc.Block() as block:

            @block.sync
            def _(sp):
                def load_raw(h):
                    sp.wait_ge(piece_lo, h * NPC)
                    for n, row in (("k", R_QM + W_M), ("q", R_QM)):
                        v = p_feat[bass.ds(h * DM + row, DM), :].rearrange("(b p) t -> p b t", p=P)
                        sp.dma_start(raw[n][:], v).then_inc(raw_loaded[n], 16)
                    v = p_tok[:, bass.ds(h * DM + S_VM, DM)].rearrange("(b p) c -> p b c", p=P)
                    sp.dma_start(raw["v"][:], v).then_inc(raw_loaded["v"], 16)

                def load_rows(h, c):
                    t = slice(c * CH, (c + 1) * CH)
                    for par in range(2):
                        sp.wait_ge(dec_made[par], h * half + (4 if c == 2 else 0))
                    sp.dma_start(nmax[c % 2][:], neg_max[bass.ds(h, 1), :, t].to_broadcast([P, NDIR, CH]))\
                        .then_inc(nmax_loaded[c % 2], 16)
                    sp.wait_ge(scaled, h * UNITS + (8 if c == 2 else 0))
                    sp.dma_start(norm[c % 2][:], floor[bass.ds(h, 1), :, t].to_broadcast([P, NDIR, CH]))\
                        .then_inc(norm_loaded[c % 2], 16)

                def load_gates(h, c):
                    sp.wait_ge(out_made, h * NCH + c)
                    sp.dma_start(gate_o[:], feat(R_OM, h, c)).then_inc(gates_loaded, 16)
                    sp.dma_start(gate_z[:], feat(R_ZM, h, c)).then_inc(gates_loaded, 16)

                def head(h, more):
                    for par in range(2):
                        sp.wait_ge(dec_made[par], h * half)
                    sp.dma_start(a_col[:], a_cols[bass.ds(h, 1)].rearrange("o p d t -> (o p) d t"))\
                        .then_inc(col_loaded, 16)
                    load_rows(h, 0)
                    load_rows(h, 1)
                    load_gates(h, 0)
                    load_rows(h, 2)
                    load_gates(h, 1)
                    if more:
                        load_raw(h + 1)
                    load_gates(h, 2)

                load_raw(0)
                with sp.Fori(0, HM - 1) as h:
                    head(h, True)
                head(HM - 1, False)

            @block.gpsimd
            def _(pool):
                nc.gpsimd.memset(ones[:], 1.0).then_inc(ones_made, 1)
                nc.gpsimd.memset(mask[:], 0.0).then_inc(mask_made, 1)
                pool.wait_ge(mask_made, 1)
                for d, sign in ((0, 1), (1, -1)):
                    nc.gpsimd.affine_select(out=mask[:, d, :], in_=mask[:, d, :], compare_op=ALU.is_ge, fill=-1e30,
                                            base=0, pattern=[[-sign, P]], channel_multiplier=sign)\
                        .then_inc(mask_made, 1)

                with pool.Fori(0, HM) as h:
                    at, w_at = 0, 0
                    for kind, c, u in steps:
                        need = pieces_before(kind, c, u[1]) if u else 0
                        while at < need:
                            pool.wait_ge(piece_hi, h * NPC + at + 1)
                            n, pc = PIECES[at]
                            cut = (slice(None), slice(None), slice(pc * CH, (pc + 1) * CH)) if n != "v" else \
                                (slice(None), slice(pc * BLK, (pc + 1) * BLK), slice(None))
                            nc.gpsimd.tensor_sub(lo[n][cut], raw[n][cut], hi[n][cut].bitcast(F32)).then_inc(piece_lo, 1)
                            at += 1
                        if kind == "scores":
                            n, s, i, j, fwd = u
                            buf = c % 2
                            w = wbuf[buf][:, i, :]
                            if i == 0:
                                pool.wait_ge(wsum_zeroed, h * NCH + c + 1)
                            pool.wait_ge(weighed[n % 4], h * (UNITS // 4) + n // 4 + 1)
                            if j is None:
                                parts = [(int(fwd), slice(0, CH), slice(0, CH))]
                            else:
                                own, past = slice(j * P, (j + 1) * P), (j + 1) * P
                                parts = [(0, slice(0, past), slice(0, past)), (1, own, slice(CH, CH + P))]
                                if past < CH:
                                    parts.append((1, slice(past, CH), slice(past, CH)))
                            pool.wait_ge(wsum_step, h * WS + w_at)
                            for d, dst, src in parts:
                                nc.gpsimd.tensor_add(wsum[buf][:, d, dst], wsum[buf][:, d, dst], w[:, src])\
                                    .then_inc(wsum_step, 1)
                                w_at += 1
                        elif kind == "values":
                            n, s, i, j, fwd = u
                            par = n % 2
                            pool.wait_ge(whi_made[par], h * half + n // 2 + 1)
                            pool.wait_ge(valued[par], h * half + n // 2)
                            nc.gpsimd.tensor_sub(w_lo[par][:], wbuf[c % 2][:, i, 0:CH], w_hi[par][:].bitcast(F32))\
                                .then_inc(wlo_made[par], 1)
                        elif kind == "out":
                            pool.wait_ge(out_read, h * NCH + c + 1)
                            nc.gpsimd.tensor_mul(out_s[:], out_s[:], gate_z[:]).then_inc(out_made, 1)
                            pool.wait_ge(out_made, h * NCH + c + 1)
                            v = g_mem[bass.ds(h * DM, DM), c * CH:(c + 1) * CH].rearrange("(b p) t -> p b t", p=P)
                            pool.dma_start(v, out_s[:]).then_inc(out_stored, 16)
                pool.wait_ge(out_stored, 16 * HM * NCH)

            @block.scalar
            def _(act):
                with act.Fori(0, HM) as h:
                    at = 0
                    for kind, c, u in steps:
                        need = pieces_before(kind, c, u[1]) if u else 0
                        while at < need:
                            n, pc = PIECES[at]
                            act.wait_ge(raw_loaded[n], h * 16 + 16)
                            if n == "v":
                                for par in range(2):
                                    act.wait_ge(valued[par], h * half)
                            else:
                                act.wait_ge(scored, h * UNITS)
                            cut = (slice(None), slice(None), slice(pc * CH, (pc + 1) * CH)) if n != "v" else \
                                (slice(None), slice(pc * BLK, (pc + 1) * BLK), slice(None))
                            nc.scalar.activation(hi[n][cut], raw[n][cut], ACT.Copy).then_inc(piece_hi, 1)
                            at += 1
                        if kind == "scores":
                            n, s, i, j, fwd = u
                            par, buf = n % 2, c % 2
                            if n == 0:
                                act.wait_ge(col_loaded, h * 16 + 16)
                            if i == 0:
                                act.wait_ge(nmax_loaded[buf], h * (32 if buf == 0 else 16) + (32 if c == 2 else 16))
                            act.wait_ge(weighed[(n - 2) % 4], h * (UNITS // 4) + (n - 2) // 4 + 1)
                            flat = dec[par][:].rearrange("p b t -> p (b t)")
                            todo = []
                            if j is None:
                                d = int(fwd)
                                todo.append((flat[:, 0:CH], nmax[buf][:, d, :], a_col[:, d, s:s + 1]))
                            else:
                                if j:
                                    todo.append((flat[:, 0:j * P], nmax[buf][:, 0, 0:j * P], a_col[:, 0, s:s + 1]))
                                if j < BLK - 1:
                                    x = slice((j + 1) * P, CH)
                                    todo.append((flat[:, x], nmax[buf][:, 1, x], a_col[:, 1, s:s + 1]))
                                todo.append((dec[par][:, j::BLK - j, :], arg[par][:], 0.0))
                            for m, (dst, src, bias) in enumerate(todo):
                                if j is not None and m == len(todo) - 1:
                                    act.wait_ge(arg_made, h * OWN + own_no[n] + 1)
                                ins = nc.scalar.activation(dst, src, ACT.Exp, bias=bias)
                            ins.then_inc(dec_made[par], 1)
                        elif kind == "norm":
                            act.wait_ge(den_full, h * NCH + c + 1)
                            nc.scalar.activation(wsum[c % 2][:], den[:], ACT.Abs).then_inc(abs_made, 1)
                        elif kind == "values":
                            n, s, i, j, fwd = u
                            par = n % 2
                            act.wait_ge(valued[par], h * half + n // 2)
                            act.wait_ge(scaled, h * UNITS + n + 1)
                            nc.scalar.activation(w_hi[par][:], wbuf[c % 2][:, i, 0:CH], ACT.Copy)\
                                .then_inc(whi_made[par], 1)

            @block.vector
            def _(dve):
                dve.wait_ge(mask_made, 3)
                with dve.Fori(0, HM) as h:
                    part = 0
                    for kind, c, u in steps:
                        buf = c % 2
                        if kind == "scores":
                            n, s, i, j, fwd = u
                            par = n % 2
                            if n == 0:
                                dve.wait_ge(col_loaded, h * 16 + 16)
                            if i == 0:
                                dve.wait_ge(nmax_loaded[buf], h * (32 if buf == 0 else 16) + (32 if c == 2 else 16))
                                for q in range(2):
                                    dve.wait_ge(wlo_made[q], h * half + (4 if c == 2 else 0))
                                dve.wait_ge(norm_made, h * NCH + (1 if c == 2 else 0))
                                nc.vector.memset(wsum[buf][:], 0.0).then_inc(wsum_zeroed, 1)
                            if j is not None:
                                dve.wait_ge(dec_made[par], h * half + n // 2)
                                for d in range(NDIR):
                                    ins = nc.vector.scalar_tensor_tensor(
                                        out=arg[par][:, d, :], in0=nmax[buf][:, d, j * P:(j + 1) * P],
                                        scalar=a_col[:, d, s:s + 1], in1=mask[:, d, :], op0=ALU.add, op1=ALU.min)
                                ins.then_inc(arg_made, 1)
                            dve.wait_ge(scored, h * UNITS + n + 1)
                            dve.wait_ge(dec_made[par], h * half + n // 2 + 1)
                            flat = dec[par][:].rearrange("p b t -> p (b t)")
                            w = wbuf[buf][:, i, :]
                            ins = nc.vector.scalar_tensor_tensor(
                                out=w[:, 0:CH], in0=scr[n % 4][:], scalar=DM ** -0.5, in1=flat[:, 0:CH],
                                op0=ALU.mult, op1=ALU.mult)
                            if j is not None:
                                ins = nc.vector.scalar_tensor_tensor(
                                    out=w[:, CH:], in0=scr[n % 4][:, j * P:(j + 1) * P], scalar=DM ** -0.5,
                                    in1=flat[:, CH:], op0=ALU.mult, op1=ALU.mult)
                            ins.then_inc(weighed[n % 4], 1)
                        elif kind == "norm":
                            dve.wait_ge(abs_made, h * NCH + c + 1)
                            dve.wait_ge(norm_loaded[buf], h * (32 if buf == 0 else 16) + (32 if c == 2 else 16))
                            nc.vector.tensor_max(norm[buf][:], norm[buf][:], wsum[buf][:]).then_inc(max_made, 1)
                            dve.wait_ge(max_made, h * NCH + c + 1)
                            nc.vector.reciprocal(norm[buf][:], norm[buf][:]).then_inc(norm_made, 1)
                        elif kind == "values":
                            n, s, i, j, fwd = u
                            if i == 0:
                                dve.wait_ge(norm_made, h * NCH + c + 1)
                            dve.wait_ge(wsum_step, h * WS + wsum_count[c])
                            w = wbuf[buf][:, i, :]
                            if j is None:
                                nc.vector.tensor_mul(w[:, 0:CH], w[:, 0:CH], norm[buf][:, int(fwd), :])\
                                    .then_inc(scaled, 1)
                            else:
                                own, past = slice(j * P, (j + 1) * P), (j + 1) * P
                                if past < CH:
                                    nc.vector.tensor_mul(w[:, past:CH], w[:, past:CH], norm[buf][:, 1, past:CH])
                                nc.vector.tensor_mul(w[:, 0:past], w[:, 0:past], norm[buf][:, 0, 0:past])
                                nc.vector.tensor_mul(w[:, CH:], w[:, CH:], norm[buf][:, 1, own]).then_inc(scaled_part, 1)
                                part += 1
                                dve.wait_ge(scaled_part, h * OWN + part)
                                nc.vector.tensor_add(w[:, own], w[:, own], w[:, CH:]).then_inc(scaled, 1)
                        elif kind == "out":
                            last = sum(m for _, m, _ in CHUNKS[:c + 1])
                            dve.wait_ge(valued[1], h * half + last // 2)
                            dve.wait_ge(gates_loaded, 32 * (h * NCH + c + 1))
                            dve.wait_ge(out_stored, 16 * (h * NCH + c))
                            nc.vector.tensor_mul(out_s[:], hout[:], gate_o[:]).then_inc(out_read, 1)

            @block.tensor
            def _(pe):
                pe.wait_ge(ones_made, 1)
                with pe.Fori(0, HM) as h:
                    for kind, c, u in steps:
                        t = slice(c * CH, (c + 1) * CH)
                        if kind == "scores":
                            n, s, i, j, fwd = u
                            src = slice(s * P, (s + 1) * P)
                            pe.wait_ge(piece_lo, h * NPC + pieces_before(kind, c, s))
                            pe.wait_ge(weighed[n % 4], h * (UNITS // 4) + n // 4)
                            for d in range(2):
                                nc.tensor.matmul(scr[n % 4][:], hi["k"][:, d, src], hi["q"][:, d, t], start=(d == 0), stop=False)
                                nc.tensor.matmul(scr[n % 4][:], hi["k"][:, d, src], lo["q"][:, d, t], start=False, stop=False)
                                ins = nc.tensor.matmul(scr[n % 4][:], lo["k"][:, d, src], hi["q"][:, d, t], start=False, stop=(d == 1))
                            ins.then_inc(scored, 1)
                        elif kind == "norm":
                            pe.wait_ge(wsum_step, h * WS + wsum_count[c])
                            pe.wait_ge(norm_made, h * NCH + c)
                            for d in range(NDIR):
                                ins = nc.tensor.matmul(den[:, d, :], ones[:], wsum[c % 2][:, d, :], start=True, stop=True)
                            ins.then_inc(den_full, 1)
                        elif kind == "values":
                            n, s, i, j, fwd = u
                            par = n % 2
                            if i == 0:
                                pe.wait_ge(out_read, h * NCH + c)
                            pe.wait_ge(piece_lo, h * NPC + pieces_before(kind, c, s))
                            pe.wait_ge(wlo_made[par], h * half + n // 2 + 1)
                            end = i == CHUNKS[c][1] - 1
                            for d in range(2):
                                f = slice(d * P, (d + 1) * P)
                                nc.tensor.matmul(hout[:, d, :], hi["v"][:, s, f], w_hi[par][:], start=(i == 0), stop=False)
                                nc.tensor.matmul(hout[:, d, :], hi["v"][:, s, f], w_lo[par][:], start=False, stop=False)
                                ins = nc.tensor.matmul(hout[:, d, :], lo["v"][:, s, f], w_hi[par][:], start=False, stop=end)
                            ins.then_inc(valued[par], 1)


QK = HA + KVA
NST = HA + 2 * KVA


def rotate(nc, p_tok, rope, q_gain, k_gain, stacks, v_stacks):
    with Scope(nc, "r") as sc:
        x = [sc.sb(f"x{b}", [P, QK + KVA, DA]) for b in range(2)]
        trig = [sc.sb(f"trig{b}", [P, 2, DA]) for b in range(2)]
        sq = [sc.sb(f"sq{b}", [P, QK, DA]) for b in range(2)]
        turn = [sc.sb(f"turn{b}", [P, QK, DA]) for b in range(2)]
        stat = [sc.sb(f"stat{b}", [P, 3, QK]) for b in range(2)]
        tab = [sc.sb(f"tab{b}", [P, 2, 2, DA]) for b in range(2)]
        st = [sc.sb(f"st{b}", [P, NST, 2, DA]) for b in range(2)]
        vst = [sc.sb(f"vst{b}", [P, KVA, 2, DA]) for b in range(2)]
        flat = [sc.sb(f"flat{b}", [P, NST, P]) for b in range(2)]
        gain = sc.sb("gain", [P, 2, 2, DA])
        ident = sc.sb("ident", [P, P])
        flip = [sc.pb(f"flip{i}", [P, 4, P]) for i in range(6)]
        ident_made, gain_loaded, gain_step = sc.sem("ident_made"), sc.sem("gain_loaded"), sc.sem("gain_step")
        loaded = sc.sems("loaded", 2)
        squared, summed, eps_added, rooted, rstd_made = (sc.sem(n) for n in (
            "squared", "summed", "eps_added", "rooted", "rstd_made"))
        tab_made, cos_made, sin_made, turned, normed = (sc.sem(n) for n in (
            "tab_made", "cos_made", "sin_made", "turned", "normed"))
        hi_made, stacked, doubled = sc.sem("hi_made"), sc.sem("stacked"), sc.sem("doubled")
        flipped = sc.sems("flipped", 6)
        emptied = sc.sems("emptied", 6)
        stored = sc.sems("stored", 2)
        halves = "p h (a b c) -> p h a b c"

        def each_tile(eng, body):
            with eng.Fori(0, TT // 2) as i:
                for b in range(2):
                    body(i * 2 + b, b, i)

        with nc.Block() as block:

            @block.sync
            def _(sp):
                for n, src in enumerate((q_gain, k_gain)):
                    sp.dma_start(gain[:, n, 0, :], src.to_broadcast([P, DA])).then_inc(gain_loaded, 16)

                def body(t, b, i):
                    sp.wait_ge(stored[b], 32 * i)
                    rows = bass.ds(t * P, P)
                    sp.dma_start(x[b][:], p_tok[rows, S_QA:S_END].rearrange("p (h d) -> p h d", d=DA))\
                        .then_inc(loaded[b], 16)
                    sp.dma_start(trig[b][:], rope[rows].rearrange("p (s d) -> p s d", d=DA)).then_inc(loaded[b], 16)

                each_tile(sp, body)

            @block.gpsimd
            def _(pool):
                make_identity(nc, pool, ident, ident_made)
                pool.wait_ge(gain_loaded, 32)
                for n in range(2):
                    g_in = gain[:, n, 0, :].rearrange("p (a b c) -> p a b c", a=2, b=2)
                    g_out = gain[:, n, 1, :].rearrange("p (a b c) -> p a b c", a=2, b=2)
                    for h in range(2):
                        nc.gpsimd.tensor_copy(g_out[:, :, h, :], g_in[:, :, 1 - h, :]).then_inc(gain_step, 1)

                def body(t, b, i):
                    pool.wait_ge(tab_made, 4 * t + 4)
                    pool.wait_ge(squared, t + 1)
                    pool.wait_ge(summed, t + 1)
                    xv, sv = x[b][:, 0:QK, :].rearrange(halves, a=2, b=2), sq[b][:].rearrange(halves, a=2, b=2)
                    for n, heads in ((0, slice(0, HA)), (1, slice(HA, QK))):
                        m = heads.stop - heads.start
                        tv = tab[b][:, n:n + 1, 1, :].rearrange(halves, a=2, b=2)
                        for h in range(2):
                            nc.gpsimd.tensor_mul(sv[:, heads, :, h, :], xv[:, heads, :, 1 - h, :],
                                                 tv[:, :, :, h, :].to_broadcast([P, m, 2, DA // 4]))\
                                .then_inc(sin_made, 1)

                each_tile(pool, body)

            @block.vector
            def _(dve):
                dve.wait_ge(gain_step, 4)

                def body(t, b, i):
                    dve.wait_ge(loaded[b], 32 * (i + 1))
                    for n, s in ((0, DA ** -0.5), (1, 1.0)):
                        for k in range(2):
                            nc.vector.scalar_tensor_tensor(out=tab[b][:, n, k, :], in0=trig[b][:, k, :], scalar=s,
                                                           in1=gain[:, n, k, :], op0=ALU.mult, op1=ALU.mult)\
                                .then_inc(tab_made, 1)
                    dve.wait_ge(squared, t + 1)
                    nc.vector.tensor_reduce(out=stat[b][:, 0, :], in_=sq[b][:], axis=AX.X, op=ALU.add).then_inc(summed, 1)
                    dve.wait_ge(summed, t + 1)
                    nc.vector.tensor_scalar(stat[b][:, 1, :], stat[b][:, 0, :], 1.0 / DA, EPS, ALU.mult, ALU.add)\
                        .then_inc(eps_added, 1)
                    dve.wait_ge(tab_made, 4 * t + 4)
                    for n, heads in ((0, slice(0, HA)), (1, slice(HA, QK))):
                        m = heads.stop - heads.start
                        nc.vector.tensor_mul(turn[b][:, heads, :], x[b][:, heads, :],
                                             tab[b][:, n:n + 1, 0, :].to_broadcast([P, m, DA])).then_inc(cos_made, 1)
                    dve.wait_ge(cos_made, 2 * t + 2)
                    dve.wait_ge(sin_made, 4 * t + 4)
                    nc.vector.tensor_add(turn[b][:], turn[b][:], sq[b][:]).then_inc(turned, 1)
                    dve.wait_ge(rooted, t + 1)
                    nc.vector.reciprocal(stat[b][:, 2, :], stat[b][:, 1, :]).then_inc(rstd_made, 1)
                    dve.wait_ge(rstd_made, t + 1)
                    dve.wait_ge(turned, t + 1)
                    nc.vector.tensor_mul(turn[b][:], turn[b][:],
                                         stat[b][:, 2, :].rearrange("p (h o) -> p h o", o=1).to_broadcast([P, QK, DA]))\
                        .then_inc(normed, 1)
                    dve.wait_ge(hi_made, 3 * t + 3)
                    nc.vector.tensor_sub(st[b][:, 0:HA, 1, :], turn[b][:, 0:HA, :], st[b][:, 0:HA, 0, :])\
                        .then_inc(stacked, 1)
                    nc.vector.tensor_sub(st[b][:, QK:NST, 0, :], turn[b][:, HA:QK, :], st[b][:, HA:QK, 0, :])\
                        .then_inc(stacked, 1)
                    nc.vector.tensor_sub(vst[b][:, :, 1, :], x[b][:, QK:, :], vst[b][:, :, 0, :]).then_inc(stacked, 1)
                    dve.wait_ge(stacked, 3 * t + 3)
                    nc.vector.tensor_copy(st[b][:, HA:NST, 1, :], st[b][:, HA:NST, 0, :]).then_inc(doubled, 1)
                    for f in range(3, 6):
                        dve.wait_ge(flipped[f], t + 1)
                        nc.vector.tensor_copy(flat[b][:, 4 * f:4 * f + 4, :], flip[f][:]).then_inc(emptied[f], 1)

                each_tile(dve, body)

            @block.scalar
            def _(act):
                def body(t, b, i):
                    act.wait_ge(loaded[b], 32 * (i + 1))
                    nc.scalar.activation(sq[b][:], x[b][:, 0:QK, :], ACT.Square).then_inc(squared, 1)
                    act.wait_ge(eps_added, t + 1)
                    nc.scalar.activation(stat[b][:, 1, :], stat[b][:, 1, :], ACT.Sqrt).then_inc(rooted, 1)
                    act.wait_ge(normed, t + 1)
                    nc.scalar.activation(st[b][:, 0:HA, 0, :].bitcast(F32R), turn[b][:, 0:HA, :], ACT.Copy).then_inc(hi_made, 1)
                    nc.scalar.activation(st[b][:, HA:QK, 0, :].bitcast(F32R), turn[b][:, HA:QK, :], ACT.Copy)\
                        .then_inc(hi_made, 1)
                    nc.scalar.activation(vst[b][:, :, 0, :].bitcast(F32R), x[b][:, QK:, :], ACT.Copy).then_inc(hi_made, 1)
                    for f in range(3):
                        act.wait_ge(flipped[f], t + 1)
                        nc.scalar.activation(flat[b][:, 4 * f:4 * f + 4, :], flip[f][:], ACT.Copy).then_inc(emptied[f], 1)
                    for f in range(6):
                        act.wait_ge(emptied[f], t + 1)
                    act.wait_ge(stacked, 3 * t + 3)
                    cols = bass.ds(t * P, P)
                    act.dma_start(stacks[:, :, cols].rearrange("n p t -> p n t"), flat[b][:]).then_inc(stored[b], 16)
                    act.dma_start(v_stacks[cols], vst[b][:].rearrange("p h s d -> p h (s d)")).then_inc(stored[b], 16)

                each_tile(act, body)
                for b in range(2):
                    act.wait_ge(stored[b], 32 * (TT // 2))

            @block.tensor
            def _(pe):
                pe.wait_ge(ident_made, 2)

                def body(t, b, i):
                    pe.wait_ge(doubled, t + 1)
                    pe.wait_ge(stacked, 3 * t + 3)
                    for f in range(6):
                        pe.wait_ge(emptied[f], t)
                        for n in range(4):
                            src = st[b][:, 4 * f + n, :, :].rearrange("p s d -> p (s d)")
                            last = nc.tensor.transpose(flip[f][:, n, :], src, ident[:])
                        last.then_inc(flipped[f], 1)

                each_tile(pe, body)


NU = TT
HEADS_IT = 4
UIT = NU * HEADS_IT


def keys_of(q_tile):
    at = 0
    for n in SEQS:
        if q_tile * P < at + n:
            return at // P, n // P
        at += n


def attend(nc, p_feat, stacks, v_stacks, g_att):
    with Scope(nc, "t") as sc:
        q_t = [sc.sb(f"q{s}", [P, 2, T], F32R) for s in range(2)]
        k_t = [sc.sb(f"k{s}", [P, 2, T], F32R) for s in range(2)]
        v_t = [sc.sb(f"v{s}", [P, TT, P], F32R) for s in range(2)]
        gate = [sc.sb(f"gate{s}", [DA, 2, T]) for s in range(2)]
        prob = [sc.sb(f"prob{r}", [P, SEQS[0]]) for r in range(3)]
        nmax, rsum = sc.sb("nmax", [P, 4]), sc.sb("rsum", [P, 2, 4])
        pt_hi = [sc.sb(f"pt_hi{b}", [P, SEQS[0] // P, CH], F32R) for b in range(2)]
        pt_lo = [sc.sb(f"pt_lo{b}", [P, SEQS[0] // P, CH], F32R) for b in range(2)]
        low = [sc.sb(f"low{b}", [DA, CH]) for b in range(2)]
        att = [sc.sb(f"att{b}", [DA, CH]) for b in range(2)]
        ident = sc.sb("ident", [P, P])
        scr = [sc.pb(f"scr{b}", [P, SEQS[0]]) for b in range(2)]
        flip = [sc.pb(f"flip{b}", [P, 4, P]) for b in range(2)]
        out = [sc.pb(f"out{b}", [P, CH]) for b in range(2)]

        ident_made = sc.sem("ident_made")
        loaded = sc.sems("loaded", 2)
        scored = sc.sem("scored")
        max_made = sc.sem("max_made")
        exp_made = sc.sems("exp_made", 2)
        inv_made = sc.sem("inv_made")
        normed = sc.sem("normed")
        flipped = sc.sems("flipped", 3)
        hi_made, lo_made = sc.sems("hi_made", 2), sc.sems("lo_made", 2)
        multiplied = sc.sems("multiplied", 2)
        low_made = sc.sem("low_made")
        summed = sc.sems("summed", 2)
        gated, stored = sc.sem("gated"), sc.sems("stored", 2)

        units, groups = [], 0
        for hd in range(HEADS_IT):
            for q in range(NU):
                first, n = keys_of(q)
                gs = list(range(groups, groups + n // 4))
                groups += n // 4
                units.append((hd, q, first, n, gs))
        upto, per_slot = [], [0, 0, 0]
        for m, u in enumerate(units):
            upto.append((m % 3, per_slot[m % 3]))
            per_slot[m % 3] += len(u[4])
        NCI = HEADS_IT * NCH
        LAG = 2
        turn = range(UIT + LAG + 1)

        def complete(k):
            m = k - LAG - 1
            return m // 4 if m >= 0 and m % 4 == 3 else None

        with nc.Block() as block:

            @block.sync
            def _(sp):
                def load(slot, g):
                    a = loaded[slot]
                    hd = g * HEADS_IT + 2 * slot
                    sp.dma_start(q_t[slot][:].bitcast(F32), stacks[bass.ds(hd, 2)].rearrange("n p t -> p n t"))\
                        .then_inc(a, 16)
                    for s in range(2):
                        sp.dma_start(k_t[slot][:, s:s + 1, :].bitcast(F32),
                                     stacks[bass.ds(g + HA + s * KVA, 1)].rearrange("n p t -> p n t")).then_inc(a, 16)
                    v = v_stacks[:, bass.ds(g, 1), :].rearrange("(t p) o d -> p t (o d)", p=P)
                    sp.dma_start(v_t[slot][:].bitcast(F32), v).then_inc(a, 16)
                    rows = p_feat[bass.ds(g * (HEADS_IT * DA) + (R_ZA + 2 * slot * DA), 2 * DA), :]
                    sp.dma_start(gate[slot][:], rows.rearrange("(n p) t -> p n t", p=DA)).then_inc(a, 16)

                load(0, 0)
                load(1, 0)
                with sp.Fori(0, KVA - 1) as g:
                    for slot in range(2):
                        sp.wait_ge(gated, g * NCI + (slot + 1) * NCI // 2)
                        load(slot, g + 1)

            @block.gpsimd
            def _(pool):
                make_identity(nc, pool, ident, ident_made)
                with pool.Fori(0, KVA) as g:
                    for k in turn:
                        if 0 <= k - 1 < UIT:
                            m = k - 1
                            n = units[m][3] * P
                            pool.wait_ge(inv_made, g * UIT + m + 1)
                            nc.gpsimd.tensor_mul(prob[m % 3][:, 0:n], prob[m % 3][:, 0:n],
                                                 rsum[:, 1, m % 4:m % 4 + 1].to_broadcast([P, n])).then_inc(normed, 1)
                        ci = complete(k)
                        if ci is not None:
                            hd, c = ci // NCH, ci % NCH
                            pool.wait_ge(summed[ci % 2], g * (NCI // 2) + ci // 2 + 1)
                            t = slice(c * CH, (c + 1) * CH)
                            nc.gpsimd.tensor_mul(att[ci % 2][:], att[ci % 2][:], gate[hd // 2][:, hd % 2, t])\
                                .then_inc(gated, 1)
                            pool.wait_ge(gated, g * NCI + ci + 1)
                            pool.dma_start(g_att[bass.ds(g * (HEADS_IT * DA) + hd * DA, DA), t], att[ci % 2][:])\
                                .then_inc(stored[ci % 2], 16)
                for b in range(2):
                    pool.wait_ge(stored[b], 16 * KVA * NCI // 2)

            @block.vector
            def _(dve):
                with dve.Fori(0, KVA) as g:
                    for k in turn:
                        if k < UIT:
                            n = units[k][3] * P
                            dve.wait_ge(scored, g * UIT + k + 1)
                            nc.vector.tensor_reduce(out=nmax[:, k % 4:k % 4 + 1], in_=scr[k % 2][:, 0:n], axis=AX.X,
                                                    op=ALU.max, negate=True).then_inc(max_made, 1)
                        if 0 <= k - 1 < UIT:
                            m = k - 1
                            dve.wait_ge(exp_made[m % 2], g * (UIT // 2) + m // 2 + 1)
                            nc.vector.reciprocal(rsum[:, 1, m % 4:m % 4 + 1], rsum[:, 0, m % 4:m % 4 + 1])\
                                .then_inc(inv_made, 1)
                        if 0 <= k - LAG < UIT:
                            m = k - LAG
                            hd, q, first, n, gs = units[m]
                            buf = (m // 4) % 2
                            for i, x in enumerate(gs):
                                dve.wait_ge(hi_made[x % 2], g * (groups // 2) + x // 2 + 1)
                                cut = (slice(None), slice(4 * i, 4 * i + 4), slice((m % 4) * P, (m % 4 + 1) * P))
                                nc.vector.tensor_sub(pt_lo[buf][cut], flip[x % 2][:], pt_hi[buf][cut].bitcast(F32))\
                                    .then_inc(lo_made[x % 2], 1)
                        ci = complete(k)
                        if ci is not None:
                            dve.wait_ge(low_made, g * NCI + ci + 1)
                            dve.wait_ge(stored[ci % 2], 16 * (g * (NCI // 2) + ci // 2))
                            nc.vector.tensor_add(att[ci % 2][:], out[ci % 2][0:DA, :], low[ci % 2][:])\
                                .then_inc(summed[ci % 2], 1)

            @block.scalar
            def _(act):
                with act.Fori(0, KVA) as g:
                    for k in turn:
                        if k < UIT:
                            n = units[k][3] * P
                            act.wait_ge(max_made, g * UIT + k + 1)
                            r, cnt = upto[k]
                            act.wait_ge(flipped[r], g * per_slot[r] + cnt)
                            act.wait_ge(inv_made, g * UIT + max(k - 3, 0))
                            nc.scalar.activation(prob[k % 3][:, 0:n], scr[k % 2][:, 0:n], ACT.Exp,
                                                 bias=nmax[:, k % 4:k % 4 + 1], accum_out=rsum[:, 0, k % 4:k % 4 + 1])\
                                .then_inc(exp_made[k % 2], 1)
                        if 0 <= k - LAG < UIT:
                            m = k - LAG
                            hd, q, first, n, gs = units[m]
                            ci = m // 4
                            if m % 4 == 0:
                                act.wait_ge(multiplied[ci % 2], g * (NCI // 2) + ci // 2)
                            r, cnt = upto[m]
                            for i, x in enumerate(gs):
                                act.wait_ge(flipped[r], g * per_slot[r] + cnt + i + 1)
                                cut = (slice(None), slice(4 * i, 4 * i + 4), slice((m % 4) * P, (m % 4 + 1) * P))
                                nc.scalar.activation(pt_hi[ci % 2][cut], flip[x % 2][:], ACT.Copy)\
                                    .then_inc(hi_made[x % 2], 1)
                        ci = complete(k)
                        if ci is not None:
                            act.wait_ge(multiplied[ci % 2], g * (NCI // 2) + ci // 2 + 1)
                            act.wait_ge(summed[ci % 2], g * (NCI // 2) + ci // 2)
                            nc.scalar.activation(low[ci % 2][:], out[ci % 2][DA:P, :], ACT.Copy).then_inc(low_made, 1)

            @block.tensor
            def _(pe):
                pe.wait_ge(ident_made, 2)
                with pe.Fori(0, KVA) as g:
                    for k in turn:
                        if k < UIT:
                            hd, q, first, n, gs = units[k]
                            slot = hd // 2
                            if k % (UIT // 2) == 0:
                                pe.wait_ge(loaded[slot], 80 * (g + 1))
                            pe.wait_ge(exp_made[k % 2], g * (UIT // 2) + k // 2)
                            for i in range(len(gs)):
                                keys = slice(first * P + i * CH, first * P + (i + 1) * CH)
                                for s in range(2):
                                    ins = nc.tensor.matmul(scr[k % 2][:, i * CH:(i + 1) * CH],
                                                           q_t[slot][:, hd % 2, q * P:(q + 1) * P],
                                                           k_t[slot][:, s, keys], start=(s == 0), stop=(s == 1))
                            ins.then_inc(scored, 1)
                        if 0 <= k - LAG < UIT:
                            m = k - LAG
                            gs = units[m][4]
                            pe.wait_ge(normed, g * UIT + m + 1)
                            for i, x in enumerate(gs):
                                pe.wait_ge(lo_made[x % 2], g * (groups // 2) + x // 2)
                                for j in range(4):
                                    ins = nc.tensor.transpose(flip[x % 2][:, j, :],
                                                              prob[m % 3][:, (4 * i + j) * P:(4 * i + j + 1) * P], ident[:])
                                ins.then_inc(flipped[m % 3], 1)
                        ci = complete(k)
                        if ci is not None:
                            hd, c = ci // NCH, ci % NCH
                            m = 4 * ci + 3
                            first, n = units[m][2:4]
                            x = units[m][4][-1]
                            for y in (x - 1, x):
                                pe.wait_ge(lo_made[y % 2], g * (groups // 2) + y // 2 + 1)
                            pe.wait_ge(summed[ci % 2], g * (NCI // 2) + ci // 2)
                            for i in range(n):
                                for s, pt in enumerate((pt_hi, pt_lo)):
                                    ins = nc.tensor.matmul(out[ci % 2][:], v_t[hd // 2][:, first + i, :],
                                                           pt[ci % 2][:, i, :], start=(i == 0 and s == 0),
                                                           stop=(i == n - 1 and s == 1))
                            ins.then_inc(multiplied[ci % 2], 1)


STAGES = 3
ACT_PCS = KT // 2


def finish(nc, x, p_feat, g_mem, g_att, w_mo, w_ao, w_out, norm_final, part, merged, y):
    with Scope(nc, "f") as sc:
        act_hi = sc.sb("act_hi", [P, KT, T], F32R)
        act_lo = sc.sb("act_lo", [P, KT, T], F32R)
        w_hi = sc.sb("w_hi", [P, 2, KT, UNIT], F32R)
        w_lo = sc.sb("w_lo", [P, 2, KT, UNIT], F32R)
        raw = sc.sb("raw", [P, KT // 2, UNIT])
        act_raw = [sc.sb(f"act_raw{b}", [P, 2, CH]) for b in range(2)]
        add = [sc.sb(f"add{b}", [P, CH]) for b in range(2)]
        stage = sc.sb("stage", [P, QUADS, 4, CH])
        stat = sc.sb("stat", [P, 2, 4])
        acc = [sc.pb(f"acc{b}", [P, CH]) for b in range(NB)]
        room = stage[:].rearrange("p a b c -> p (a b c)")
        xt = [room[:, j * D:(j + 1) * D] for j in range(2)]
        yt = [room[:, (2 + j) * D:(3 + j) * D] for j in range(2)]
        gain, junk = room[:, 4 * D:5 * D], room[:, 5 * D:6 * D]

        raw_loaded = sc.sem("raw_loaded")
        w_hi_made, w_lo_made = sc.sem("w_hi_made"), sc.sem("w_lo_made")
        act_loaded = sc.sems("act_loaded", 2)
        act_hi_made = sc.sem("act_hi_made")
        act_lo_made = sc.sems("act_lo_made", 2)
        acc_full = sc.sems("acc_full", 2)
        evacuated = sc.sems("evacuated", NB)
        gate_loaded = sc.sems("gate_loaded", QUADS)
        add_loaded, gated, stored = sc.sems("add_loaded", 2), sc.sem("gated"), sc.sems("stored", QUADS)
        x_loaded, gain_loaded = sc.sems("x_loaded", 2), sc.sem("gain_loaded")
        summed, squared, mean_made, root_made, rstd_made, normed = (sc.sem(n) for n in (
            "summed", "squared", "mean_made", "root_made", "rstd_made", "normed"))
        y_stored = sc.sems("y_stored", 2)
        UNITS_F = 2 * STAGES
        PIECES_F = NCH * ACT_PCS
        weights = (w_mo, w_ao, w_out)
        sources = (g_mem, g_att, merged)

        def fview(ap):
            return ap.rearrange("(b p) t -> p b t", p=P)

        with nc.Block() as block:

            @block.sync
            def _(sp):
                def load_half(n, h):
                    s, slot = n // 2, n % 2
                    if 2 * n + h > 0:
                        sp.wait_ge(w_lo_made, (2 * n + h) * KT // 2)
                    v = weights[s].rearrange("(k p) n -> p k n", p=P)
                    sp.dma_start(raw[:], v[:, h * KT // 2:(h + 1) * KT // 2, slot * UNIT:(slot + 1) * UNIT])\
                        .then_inc(raw_loaded, 16)

                def load_act(s, c):
                    v = fview(sources[s])
                    for i in range(ACT_PCS):
                        pc = (s * NCH + c) * ACT_PCS + i
                        if pc >= 2:
                            sp.wait_ge(act_lo_made[pc % 2], pc // 2)
                        sp.dma_start(act_raw[pc % 2][:], v[:, 2 * i:2 * i + 2, c * CH:(c + 1) * CH])\
                            .then_inc(act_loaded[pc % 2], 16)

                load_half(0, 0)
                load_half(0, 1)
                load_act(0, 0)
                load_half(1, 0)
                load_act(0, 1)
                load_act(0, 2)
                for n in range(UNITS_F - 2):
                    s, slot = n // 2, n % 2
                    load_half(n + 1, 1)
                    load_half(n + 2, 0)
                    for c in range(NCH):
                        if n:
                            sp.wait_ge(stored[c], 16 * n)
                        v = fview(p_feat[R_GM + s * D + slot * UNIT:R_GM + s * D + (slot + 1) * UNIT, :])
                        sp.dma_start(stage[:, c], v[:, :, c * CH:(c + 1) * CH]).then_inc(gate_loaded[c], 16)
                    for c in range(NCH):
                        t = slice(c * CH, (c + 1) * CH)
                        rows = slice(slot * UNIT, (slot + 1) * UNIT)
                        if s == 1:
                            if slot == 0 and c == 0:
                                for q in range(QUADS):
                                    sp.wait_ge(stored[q], 16 * 2)
                            for j in range(4):
                                m = (slot * NCH + c) * 4 + j
                                if m >= 2:
                                    sp.wait_ge(gated, 2 * NG + m - 1)
                                at = slot * UNIT + j * P
                                sp.dma_start(add[m % 2][:], part[at:at + P, t]).then_inc(add_loaded[m % 2], 16)
                        sp.wait_ge(gated, n * NG + 4 * c + 4)
                        dst = (part, merged)[s]
                        sp.dma_start(fview(dst[rows, :])[:, :, t], stage[:, c]).then_inc(stored[c], 16)
                        if slot == 1:
                            if s == 1:
                                sp.wait_ge(stored[c], 16 * 4)
                            load_act(s + 1, c)
                load_half(UNITS_F - 1, 1)
                for q in range(QUADS):
                    sp.wait_ge(stored[q], 16 * 4)
                sp.dma_start(gain, norm_final.to_broadcast([P, D])).then_inc(gain_loaded, 16)
                for t in range(TT):
                    b = t % 2
                    if t >= 2:
                        sp.wait_ge(summed, t - 1)
                    sp.dma_start(xt[b], x[t * P:(t + 1) * P, :]).then_inc(x_loaded[b], 16)
                    if t:
                        sp.wait_ge(normed, t)
                        sp.dma_start(y[(t - 1) * P:t * P, :], yt[1 - b]).then_inc(y_stored[1 - b], 16)
                sp.wait_ge(normed, TT)
                sp.dma_start(y[(TT - 1) * P:, :], yt[(TT - 1) % 2]).then_inc(y_stored[(TT - 1) % 2], 16)
                for b in range(2):
                    sp.wait_ge(y_stored[b], 16 * TT // 2)

            def split_order(stage_no):
                yield from (("w", 2 * stage_no, k) for k in range(KT))
                if stage_no == 0:
                    yield from (("a", 0, i) for i in range(ACT_PCS))
                    yield from (("w", 1, k) for k in range(KT // 2))
                    yield from (("a", c, i) for c in (1, 2) for i in range(ACT_PCS))
                    yield from (("w", 1, k) for k in range(KT // 2, KT))
                else:
                    yield from (("a", c, i) for c in range(NCH) for i in range(ACT_PCS))
                    yield from (("w", 2 * stage_no + 1, k) for k in range(KT))

            @block.gpsimd
            def _(pool):
                for s in range(STAGES):
                    for kind, n, k in split_order(s):
                        if kind == "w":
                            pool.wait_ge(w_hi_made, n * KT + k + 1)
                            cut = (slice(None), n % 2, k, slice(None))
                            nc.gpsimd.tensor_sub(w_lo[cut], raw[:, k % (KT // 2), :], w_hi[cut].bitcast(F32))\
                                .then_inc(w_lo_made, 1)
                        else:
                            pc = (s * NCH + n) * ACT_PCS + k
                            pool.wait_ge(act_hi_made, pc + 1)
                            cut = (slice(None), slice(2 * k, 2 * k + 2), slice(n * CH, (n + 1) * CH))
                            nc.gpsimd.tensor_sub(act_lo[cut], act_raw[pc % 2][:], act_hi[cut].bitcast(F32))\
                                .then_inc(act_lo_made[pc % 2], 1)

            @block.scalar
            def _(act):
                for s in range(STAGES):
                    for kind, n, k in split_order(s):
                        if kind == "w":
                            act.wait_ge(raw_loaded, 16 * (2 * n + k // (KT // 2) + 1))
                            if n >= 2:
                                act.wait_ge(acc_full[n % 2], NG * (n // 2))
                            nc.scalar.activation(w_hi[:, n % 2, k, :], raw[:, k % (KT // 2), :], ACT.Copy)\
                                .then_inc(w_hi_made, 1)
                        else:
                            pc = (s * NCH + n) * ACT_PCS + k
                            act.wait_ge(act_loaded[pc % 2], 16 * (pc // 2 + 1))
                            if s:
                                act.wait_ge(acc_full[1], NG * (s - 1) + 4 * n + 4)
                            cut = (slice(None), slice(2 * k, 2 * k + 2), slice(n * CH, (n + 1) * CH))
                            nc.scalar.activation(act_hi[cut], act_raw[pc % 2][:], ACT.Copy).then_inc(act_hi_made, 1)
                for t in range(TT):
                    b = t % 2
                    act.wait_ge(summed, t + 1)
                    nc.scalar.activation(junk, yt[b], ACT.Square, accum_out=stat[:, b, 0:1]).then_inc(squared, 1)
                    act.wait_ge(mean_made, t + 1)
                    nc.scalar.activation(stat[:, b, 2:3], stat[:, b, 1:2], ACT.Sqrt).then_inc(root_made, 1)

            @block.vector
            def _(dve):
                for n in range(UNITS_F - 2):
                    s, slot = n // 2, n % 2
                    for m in range(NG):
                        c, j = m // 4, m % 4
                        dve.wait_ge(gate_loaded[c], 16 * (n + 1))
                        dve.wait_ge(acc_full[slot], NG * s + m + 1)
                        ins = nc.vector.tensor_mul(stage[:, c, j, :], stage[:, c, j, :], acc[m % NB][:])\
                            .then_inc(evacuated[m % NB], 1)
                        if s == 0:
                            dve.wait_ge(evacuated[m % NB], 2 * n + m // NB + 1)
                            dve.sem_inc(gated, 1)
                        else:
                            a = slot * NG + m
                            dve.wait_ge(add_loaded[a % 2], 16 * (a // 2 + 1))
                            dve.wait_ge(evacuated[m % NB], 2 * n + m // NB + 1)
                            nc.vector.tensor_add(stage[:, c, j, :], stage[:, c, j, :], add[a % 2][:]).then_inc(gated, 1)
                dve.wait_ge(gain_loaded, 16)
                for t in range(TT):
                    b = t % 2
                    dve.wait_ge(x_loaded[b], 16 * (t // 2 + 1))
                    if t >= 2:
                        dve.wait_ge(y_stored[b], 16 * (t // 2))
                    for h in range(2):
                        m = 2 * t + h
                        dve.wait_ge(acc_full[h], NG * 2 + t + 1)
                        cols = slice(h * CH, (h + 1) * CH)
                        nc.vector.tensor_add(yt[b][:, cols], xt[b][:, cols], acc[m % NB][:]).then_inc(evacuated[m % NB], 1)
                    for h in range(2):
                        m = 2 * t + h
                        dve.wait_ge(evacuated[m % NB], 8 + m // NB + 1)
                    dve.sem_inc(summed, 1)
                    dve.wait_ge(squared, t + 1)
                    nc.vector.tensor_scalar(stat[:, b, 1:2], stat[:, b, 0:1], 1.0 / D, EPS, ALU.mult, ALU.add)\
                        .then_inc(mean_made, 1)
                    dve.wait_ge(root_made, t + 1)
                    nc.vector.reciprocal(stat[:, b, 3:4], stat[:, b, 2:3]).then_inc(rstd_made, 1)
                    dve.wait_ge(rstd_made, t + 1)
                    nc.vector.scalar_tensor_tensor(out=yt[b], in0=yt[b], scalar=stat[:, b, 3:4], in1=gain,
                                                   op0=ALU.mult, op1=ALU.mult).then_inc(normed, 1)

            @block.tensor
            def _(pe):
                def act_ready(s, c, k):
                    pc = (s * NCH + c) * ACT_PCS + k // 2
                    pe.wait_ge(act_lo_made[pc % 2], pc // 2 + 1)

                for n in range(UNITS_F - 2):
                    s, slot = n // 2, n % 2
                    for m in range(NG):
                        c, cb = m // 4, m % 4
                        if n or m >= NB:
                            pe.wait_ge(evacuated[m % NB], 2 * n + m // NB)

                        def before_k(k):
                            if m == 0:
                                pe.wait_ge(w_lo_made, n * KT + k + 1)
                            if slot == 0 and cb == 0:
                                act_ready(s, c, k)

                        t, o = slice(c * CH, (c + 1) * CH), slice(cb * P, (cb + 1) * P)
                        product(nc, pe, acc[m % NB][:], lambda k: w_hi[:, slot, k, o], lambda k: w_lo[:, slot, k, o],
                                lambda k: act_hi[:, k, t], lambda k: act_lo[:, k, t], before_k)\
                            .then_inc(acc_full[slot], 1)
                for t in range(TT):
                    for h in range(2):
                        m = 2 * t + h
                        pe.wait_ge(evacuated[m % NB], 8 + m // NB)

                        def before_k(k):
                            if t == 0:
                                pe.wait_ge(w_lo_made, (4 + h) * KT + k + 1)
                            if h == 0 and t % 4 == 0:
                                act_ready(2, t // 4, k)

                        o = slice(t * P, (t + 1) * P)
                        product(nc, pe, acc[m % NB][:], lambda k: act_hi[:, k, o], lambda k: act_lo[:, k, o],
                                lambda k: w_hi[:, h, k, :], lambda k: w_lo[:, h, k, :], before_k)\
                            .then_inc(acc_full[h], 1)


def encoder_layer(nc, x, w_in, b_if, norm_pre, q_gain, k_gain, w_mo, w_ao, w_out, norm_final, rope, y):
    def scratch(name, *shape):
        return nc.dram_tensor(name, shape, F32, kind="Internal").ap()

    p_feat, p_tok = scratch("p_feat", R_END, T), scratch("p_tok", T, S_END)
    gate_rows = scratch("gate_rows", 4 * HM, T)
    neg_max, floor = scratch("neg_max", HM, NDIR, T), scratch("floor", HM, NDIR, T)
    a_cols = scratch("a_cols", HM, P, NDIR, TT)
    stacks, v_stacks = scratch("stacks", NST, P, T), scratch("v_stacks", T, KVA, P)
    g_mem, g_att = scratch("g_mem", W_M, T), scratch("g_att", W_A, T)
    part, merged = scratch("part", D, T), scratch("merged", D, T)
    project(nc, x, w_in, norm_pre, p_feat, p_tok, gate_rows)
    prepare_gates(nc, gate_rows, b_if, neg_max, floor, a_cols)
    mlstm(nc, p_feat, p_tok, neg_max, floor, a_cols, g_mem)
    rotate(nc, p_tok, rope, q_gain, k_gain, stacks, v_stacks)
    attend(nc, p_feat, stacks, v_stacks, g_att)
    finish(nc, x, p_feat, g_mem, g_att, w_mo, w_ao, w_out, norm_final, part, merged, y)


def rope_table(np):
    grid_w, half, theta = 64, DA // 4, 10000.0
    pos = np.concatenate([np.arange(n) for n in SEQS])
    freqs = theta ** (-np.arange(0, DA // 2, 2, dtype=np.float32) / np.float32(DA // 2))
    out = np.zeros((T, 2, 2, 2, half), np.float32)
    for axis, at in enumerate((pos // grid_w, pos % grid_w)):
        angle = at.astype(np.float32)[:, None] * freqs.astype(np.float32)
        out[:, 0, axis, :] = np.cos(angle)[:, None]
        out[:, 1, axis, 0], out[:, 1, axis, 1] = -np.sin(angle), np.sin(angle)
    return out.reshape(T, 2 * DA)


def kernel(x_prompt, x_sample, w_in, b_if, norm_pre, q_gain, k_gain, w_mo, w_ao, w_out, norm_final):
    import numpy as np
    import concourse.bacc as bacc
    from concourse.bass_utils import run_bass_kernel_spmd

    a = np.ascontiguousarray
    arrays = {
        "x": a(np.concatenate([np.asarray(x_prompt)[0], np.asarray(x_sample)[0]])),
        "w_in": a(np.asarray(w_in)[0]), "b_if": a(b_if), "norm_pre": a(norm_pre), "q_gain": a(q_gain),
        "k_gain": a(k_gain), "w_mo": a(np.asarray(w_mo)[0]), "w_ao": a(np.asarray(w_ao)[0]),
        "w_out": a(np.asarray(w_out)[0]), "norm_final": a(np.asarray(norm_final)[None, :]),
        "rope": rope_table(np),
    }
    nc = bacc.Bacc("TRN2", target_bir_lowering=False, num_devices=1)
    aps = {n: nc.dram_tensor(n, v.shape, F32, kind="ExternalInput").ap() for n, v in arrays.items()}
    y = nc.dram_tensor("y", (T, D), F32, kind="ExternalOutput").ap()
    encoder_layer(nc, y=y, **aps)
    r = run_bass_kernel_spmd(nc, [arrays], core_ids=[0])
    out = r.results[0]["y"]
    return out[None, 0:SEQS[0]], out[None, SEQS[0]:T]
```

```python
import concourse.bass as bass
from concourse import mybir
from contextlib import ExitStack

F32 = mybir.dt.float32
F32R = mybir.dt.float32r
ALU = mybir.AluOpType
ACT = mybir.ActivationFunctionType
AX = mybir.AxisListType

P = 128
D = 1024
SEQS = (1024, 512)
T = sum(SEQS)
TT = T // P
CH = 512
NCH = T // CH
KT = D // P
HM, DM = 4, 256
HA, KVA, DA = 16, 4, 64
GRP = HA // KVA
EPS = 1e-6
CREDIT = 1
W_M, W_A, W_KV = HM * DM, HA * DA, KVA * DA
C_QM, C_VM, C_OM, C_ZM = 0, 2 * W_M, 3 * W_M, 4 * W_M
C_IF = 5 * W_M
C_QA = C_IF + 4 * HM
C_KVA = C_QA + W_A
C_ZA = C_KVA + 2 * W_KV
C_GM = C_ZA + W_A
R_QM, R_OM, R_ZM, R_ZA, R_GM, R_END = 0, 2 * W_M, 3 * W_M, 4 * W_M, 4 * W_M + W_A, 4 * W_M + W_A + 2 * D
S_QA, S_KVA, S_VM, S_END = 0, W_A, W_A + 2 * W_KV, W_A + 2 * W_KV + W_M

UNIT = 512
CB = UNIT // P
NB = 6
NG = 12
QUADS = NG // 4


class Scope(ExitStack):

    def __init__(self, nc, tag):
        super().__init__()
        self.nc, self.tag, self.used = nc, tag, []
        self.callback(self.clear)

    def clear(self):
        self.nc.clear_and_free_semaphores(self.used)
        self.nc.all_engine_barrier()

    def sb(self, name, shape, dt=F32):
        return self.enter_context(self.nc.sbuf_tensor(f"{self.tag}_{name}", shape, dt))

    def pb(self, name, shape, dt=F32):
        return self.enter_context(self.nc.psum_tensor(f"{self.tag}_{name}", shape, dt))

    def sem(self, name):
        self.used.append(self.nc.alloc_semaphore(f"{self.tag}_{name}"))
        self.nc.gpsimd.sem_inc(self.used[-1], CREDIT)
        return self.used[-1]

    def sems(self, name, n):
        return [self.sem(f"{name}{i}") for i in range(n)]


def make_identity(nc, pool, ident, sem):
    nc.gpsimd.memset(ident[:], 0.0).then_inc(sem, 1)
    pool.wait_ge(sem, CREDIT + 1)
    nc.gpsimd.affine_select(out=ident[:], in_=ident[:], compare_op=ALU.not_equal, fill=1.0,
                            base=0, pattern=[[-1, P]], channel_multiplier=1).then_inc(sem, 1)


class Gemm:

    def __init__(self, sc):
        self.act_hi = sc.sb("act_hi", [P, KT, T], F32R)
        self.act_lo = sc.sb("act_lo", [P, KT, T], F32R)
        self.w_hi = sc.sb("w_hi", [P, 2, KT, UNIT], F32R)
        self.w_lo = sc.sb("w_lo", [P, 2, KT, UNIT], F32R)
        self.raw = sc.sb("raw", [P, KT, UNIT])
        self.stage = sc.sb("stage", [P, QUADS, 4, CH])
        self.acc = [sc.pb(f"acc{b}", [P, CH]) for b in range(NB)]
        self.raw_loaded = sc.sem("raw_loaded")
        self.hi_split = sc.sems("hi_split", 2)
        self.lo_split = sc.sems("lo_split", 2)
        self.acc_full = sc.sems("acc_full", 2)
        self.evacuated = sc.sems("evacuated", NB)
        self.stored = sc.sems("stored", QUADS)


def over_turns(eng, steps, step, count, ticks):
    first, last = (int(f(t for t, _, _ in steps) // ticks) for f in (min, max))
    order = sorted((t % ticks, t // ticks, kind, n) for t, kind, n in steps)

    def ticks_of(i):
        for _, late, kind, n in order:
            turn = i - int(late)
            if not isinstance(turn, int) or 0 <= turn < count:
                step(kind, n, turn)

    for i in range(first, last):
        ticks_of(i)
    with eng.Fori(last, count + first) as i:
        ticks_of(i)
    for i in range(count + first, count + last):
        ticks_of(i)


def load_unit(sp, g, w_cols, slot, pair, width=UNIT):
    sp.wait_ge(g.lo_split[1 - slot], CREDIT + KT * (pair + slot))
    sp.dma_start(g.raw[:, :, 0:width], w_cols).then_inc(g.raw_loaded, 16)


def split_hi_unit(nc, dve, g, slot, pair, width=UNIT):
    dve.wait_ge(g.raw_loaded, CREDIT + 16 * (2 * pair + slot + 1))
    dve.wait_ge(g.acc_full[slot], CREDIT + NG * pair)
    for k in range(KT):
        nc.vector.tensor_copy(g.w_hi[:, slot, k, 0:width], g.raw[:, k, 0:width]).then_inc(g.hi_split[slot], 1)


def split_lo_unit(nc, pool, g, slot, pair, width=UNIT):
    for k in range(KT):
        pool.wait_ge(g.hi_split[slot], CREDIT + KT * pair + k + 1)
        nc.gpsimd.tensor_sub(g.w_lo[:, slot, k, 0:width], g.raw[:, k, 0:width],
                             g.w_hi[:, slot, k, 0:width].bitcast(F32)).then_inc(g.lo_split[slot], 1)


def product(nc, pe, out, stat_hi, stat_lo, mov_hi, mov_lo, before_k=None):
    for k in range(KT):
        if before_k:
            before_k(k)
        nc.tensor.matmul(out, stat_hi(k), mov_hi(k), start=(k == 0), stop=False)
        nc.tensor.matmul(out, stat_hi(k), mov_lo(k), start=False, stop=False)
        last = nc.tensor.matmul(out, stat_lo(k), mov_hi(k), start=False, stop=(k == KT - 1))
    return last


def multiply_unit(nc, pe, g, slot, pair, features, groups=NG, act_ready=None, before_group=None):
    for n in range(groups):
        b = n % NB
        if before_group:
            before_group(n)
        pe.wait_ge(g.evacuated[b], CREDIT + 2 * (2 * pair + slot) + n // NB)

        def before_k(k, n=n):
            if n == 0:
                pe.wait_ge(g.hi_split[slot], CREDIT + KT * pair + k + 1)
                pe.wait_ge(g.lo_split[slot], CREDIT + KT * pair + k + 1)
            if act_ready:
                act_ready(n, k)

        if features:
            c, cb = (n // CB, n % CB) if groups == NG else (n, 0)
            t, m = slice(c * CH, (c + 1) * CH), slice(cb * P, (cb + 1) * P)
            last = product(nc, pe, g.acc[b][:], lambda k: g.w_hi[:, slot, k, m], lambda k: g.w_lo[:, slot, k, m],
                           lambda k: g.act_hi[:, k, t], lambda k: g.act_lo[:, k, t], before_k)
        else:
            t = slice(n * P, (n + 1) * P)
            last = product(nc, pe, g.acc[b][:], lambda k: g.act_hi[:, k, t], lambda k: g.act_lo[:, k, t],
                           lambda k: g.w_hi[:, slot, k, :], lambda k: g.w_lo[:, slot, k, :], before_k)
        last.then_inc(g.acc_full[slot], 1)


def drain_unit(nc, act, g, slot, pair, func, out_quad):
    unit = 2 * pair + slot
    for q in range(QUADS):
        act.wait_ge(g.stored[q], CREDIT + 16 * unit)
        for j in range(4):
            n = 4 * q + j
            act.wait_ge(g.acc_full[slot], CREDIT + NG * pair + n + 1)
            nc.scalar.activation(g.stage[:, q, j, :], g.acc[n % NB][:], func).then_inc(g.evacuated[n % NB], 1)
        for j in range(4):
            n = 4 * q + j
            act.wait_ge(g.evacuated[n % NB], CREDIT + 2 * unit + n // NB + 1)
        act.dma_start(out_quad(q), g.stage[:, q]).then_inc(g.stored[q], 16)


def project(nc, x, w_in, norm_pre, p_feat, p_tok, gate_rows):
    with Scope(nc, "a") as sc:
        g = Gemm(sc)
        gain = sc.sb("gain", [P, D])
        ident = sc.sb("ident", [P, P])
        stat = sc.sb("stat", [P, 3, 4])
        flip = [sc.pb(f"flip{i}", [P, 4, P]) for i in range(2)]
        room = g.stage[:].rearrange("p a b c -> p (a b c)")
        xt = [room[:, j * D:(j + 1) * D] for j in range(3)]
        ht = [room[:, (3 + j) * D:(4 + j) * D] for j in range(3)]
        x_loaded = sc.sems("x_loaded", 3)
        gain_loaded = sc.sem("gain_loaded")
        ident_made = sc.sem("ident_made")
        squared = sc.sem("squared")
        mean_made = sc.sem("mean_made")
        root_made = sc.sem("root_made")
        rstd_made = sc.sem("rstd_made")
        h_made = sc.sem("h_made")
        flipped_a = sc.sem("flipped_a")
        flipped_b = sc.sems("flipped_b", 3)
        act_hi_made = sc.sems("act_hi_made", 2)
        act_lo_made = sc.sems("act_lo_made", 2)
        w_cols = w_in.rearrange("(k p) n -> p k n", p=P)

        feature_runs = [(C_OM, 1, ACT.Sigmoid, R_OM), (C_QM, 2, ACT.Copy, R_QM), (C_ZM, 1, ACT.Silu, R_ZM),
                        (C_ZA, 1, ACT.Silu, R_ZA), (C_GM, 2, ACT.Sigmoid, R_GM)]
        token_runs = [(C_VM, S_VM), (C_QA, S_QA)]
        runs = [(True, *r) for r in feature_runs] + [(False, c, 1, ACT.Copy, s) for c, s in token_runs]

        tile_plan = {"act": [], "dve": []}
        for j in range(3):
            for engine, tick, kind in (("act", 0.0, "square"), ("dve", 0.2, "mean"), ("act", 0.3, "root"),
                                       ("dve", 0.5, "normalise"), ("act", 1.6, "high"), ("dve", 1.75, "low")):
                tile_plan[engine].append((tick + j, kind, j))

        def over_pairs(eng, body):
            pair = 0
            for run in runs:
                if run[2] > 1:
                    with eng.Fori(0, run[2]) as i:
                        body(run, i + pair, i)
                else:
                    body(run, pair, 0)
                pair += run[2]
            return pair

        with nc.Block() as block:

            @block.sync
            def _(sp):
                sp.dma_start(gain[:], norm_pre.to_broadcast([P, D])).then_inc(gain_loaded, 16)
                for j in range(3):
                    sp.dma_start(xt[j], x[j * P:(j + 1) * P, :]).then_inc(x_loaded[j], 16)
                sp.dma_start(g.raw[:], w_cols[:, :, runs[0][1]:runs[0][1] + UNIT]).then_inc(g.raw_loaded, 16)
                with sp.Fori(1, TT // 3) as i:
                    for j in range(3):
                        sp.wait_ge(flipped_b[j], CREDIT + i)
                        sp.dma_start(xt[j], x[bass.ds(i * 3 * P + j * P, P), :]).then_inc(x_loaded[j], 16)

                def body(run, pair, i):
                    for slot in range(2):
                        if run is runs[0] and slot == 0:
                            continue
                        load_unit(sp, g, w_cols[:, :, bass.ds(i * 2 * UNIT + run[1] + slot * UNIT, UNIT)], slot, pair)

                last = over_pairs(sp, body)
                load_unit(sp, g, w_cols[:, :, C_KVA:C_KVA + UNIT], 0, last)
                load_unit(sp, g, w_cols[:, :, C_IF:C_IF + P], 1, last, P)

            @block.gpsimd
            def _(pool):
                make_identity(nc, pool, ident, ident_made)
                pool.wait_ge(g.raw_loaded, CREDIT + 16)
                for k in range(KT):
                    nc.gpsimd.tensor_copy(g.w_hi[:, 0, k, :], g.raw[:, k, :]).then_inc(g.hi_split[0], 1)

                def body(run, pair, i):
                    for slot in range(2):
                        split_lo_unit(nc, pool, g, slot, pair)

                last = over_pairs(pool, body)
                split_lo_unit(nc, pool, g, 0, last)
                split_lo_unit(nc, pool, g, 1, last, P)

            @block.vector
            def _(dve):
                def tile_step(kind, j, i):
                    t = i * 3 + j
                    if kind == "mean":
                        dve.wait_ge(squared, CREDIT + t + 1)
                        nc.vector.tensor_scalar(stat[:, j, 1:2], stat[:, j, 0:1], 1.0 / D, EPS, ALU.mult, ALU.add)\
                            .then_inc(mean_made, 1)
                    elif kind == "normalise":
                        dve.wait_ge(root_made, CREDIT + t + 1)
                        nc.vector.reciprocal(stat[:, j, 3:4], stat[:, j, 2:3]).then_inc(rstd_made, 1)
                        dve.wait_ge(rstd_made, CREDIT + t + 1)
                        dve.wait_ge(x_loaded[j], CREDIT + 16 * (i + 1))
                        nc.vector.scalar_tensor_tensor(out=ht[j], in0=xt[j], scalar=stat[:, j, 3:4], in1=gain[:],
                                                       op0=ALU.mult, op1=ALU.mult).then_inc(h_made, 1)
                    elif kind == "low":
                        for half in range(2):
                            dve.wait_ge(act_hi_made[half], CREDIT + t + 1)
                            cols = bass.ds(i * 3 * P + j * P, P)
                            nc.vector.tensor_sub(g.act_lo[:, 4 * half:4 * half + 4, cols], flip[half][:],
                                                 g.act_hi[:, 4 * half:4 * half + 4, cols].bitcast(F32))\
                                .then_inc(act_lo_made[half], 1)

                dve.wait_ge(gain_loaded, CREDIT + 16)
                over_turns(dve, tile_plan["dve"], tile_step, TT // 3, 3)

                def body(run, pair, i):
                    for slot in range(2):
                        if run is runs[0] and slot == 0:
                            continue
                        split_hi_unit(nc, dve, g, slot, pair)

                last = over_pairs(dve, body)
                split_hi_unit(nc, dve, g, 0, last)
                split_hi_unit(nc, dve, g, 1, last, P)

            @block.scalar
            def _(act):
                def tile_step(kind, j, i):
                    t = i * 3 + j
                    if kind == "square":
                        act.wait_ge(x_loaded[j], CREDIT + 16 * (i + 1))
                        act.wait_ge(flipped_b[j], CREDIT + i)
                        nc.scalar.activation(ht[j], xt[j], ACT.Square, accum_out=stat[:, j, 0:1]).then_inc(squared, 1)
                    elif kind == "root":
                        act.wait_ge(mean_made, CREDIT + t + 1)
                        nc.scalar.activation(stat[:, j, 2:3], stat[:, j, 1:2], ACT.Sqrt).then_inc(root_made, 1)
                    elif kind == "high":
                        for half in range(2):
                            if half:
                                act.wait_ge(flipped_b[j], CREDIT + i + 1)
                            else:
                                act.wait_ge(flipped_a, CREDIT + t + 1)
                            nc.scalar.activation(g.act_hi[:, 4 * half:4 * half + 4, bass.ds(i * 3 * P + j * P, P)],
                                                 flip[half][:], ACT.Copy).then_inc(act_hi_made[half], 1)

                over_turns(act, tile_plan["act"], tile_step, TT // 3, 3)

                def body(run, pair, i):
                    features, _, _, func, at = run
                    for slot in range(2):
                        if features:
                            rows = p_feat[bass.ds(i * 2 * UNIT + at + slot * UNIT, UNIT), :]
                            rows = rows.rearrange("(b p) t -> p b t", p=P)
                            drain_unit(nc, act, g, slot, pair, func, lambda q: rows[:, :, q * CH:(q + 1) * CH])
                        else:
                            cols = p_tok[:, at + slot * UNIT:at + (slot + 1) * UNIT]
                            cols = cols.rearrange("(b p) c -> p b c", p=P)
                            drain_unit(nc, act, g, slot, pair, func, lambda q: cols[:, 4 * q:4 * q + 4, :])

                last = over_pairs(act, body)
                cols = p_tok[:, S_KVA:S_VM].rearrange("(b p) c -> p b c", p=P)
                drain_unit(nc, act, g, 0, last, ACT.Copy, lambda q: cols[:, 4 * q:4 * q + 4, :])
                act.wait_ge(g.stored[0], CREDIT + 16 * (2 * last + 1))
                for c in range(NCH):
                    act.wait_ge(g.acc_full[1], CREDIT + NG * last + c + 1)
                    nc.scalar.activation(g.stage[0:4 * HM, 0, c, :], g.acc[c][0:4 * HM, :], ACT.Copy)\
                        .then_inc(g.evacuated[c], 1)
                for c in range(NCH):
                    act.wait_ge(g.evacuated[c], CREDIT + 2 * (2 * last + 1) + 1)
                act.dma_start(gate_rows.rearrange("r (c t) -> r c t", t=CH),
                              g.stage[0:4 * HM, 0, 0:NCH, :]).then_inc(g.stored[0], 16)
                act.wait_ge(g.stored[0], CREDIT + 16 * (2 * last + 2))
                for q in range(1, QUADS):
                    act.wait_ge(g.stored[q], CREDIT + 16 * (2 * last + 1))

            @block.tensor
            def _(pe):
                def transpose_tile(t):
                    pe.wait_ge(h_made, CREDIT + t + 1)
                    for half in range(2):
                        pe.wait_ge(act_lo_made[half], CREDIT + t)
                        for k in range(4):
                            col = (4 * half + k) * P
                            last = nc.tensor.transpose(flip[half][:, k, :], ht[t % 3][:, col:col + P], ident[:])
                        last.then_inc(flipped_b[t % 3] if half else flipped_a, 1)

                def before_group(n):
                    if n < CB:
                        for t in (6 + 2 * n, 7 + 2 * n):
                            if t < TT:
                                transpose_tile(t)
                    if n % CB == 0:
                        for half in range(2):
                            pe.wait_ge(act_lo_made[half], CREDIT + (n // CB + 1) * CH // P)

                pe.wait_ge(ident_made, CREDIT + 2)
                for t in range(6):
                    transpose_tile(t)

                def body(run, pair, i):
                    for slot in range(2):
                        multiply_unit(nc, pe, g, slot, pair, run[0],
                                      before_group=before_group if run is runs[0] and slot == 0 else None)

                last = over_pairs(pe, body)
                multiply_unit(nc, pe, g, 0, last, False)
                multiply_unit(nc, pe, g, 1, last, True, NCH)


NDIR = 2
HALF = 32


def prepare_gates(nc, gate_rows, b_if, neg_max, floor, a_cols):
    with Scope(nc, "g") as sc:
        rows = 2 * HALF
        i_raw, f_raw = sc.sb("i_raw", [rows, T]), sc.sb("f_raw", [rows, T])
        i_bias, f_bias = sc.sb("i_bias", [rows, 1]), sc.sb("f_bias", [rows, 1])
        i_pre, f_pre = sc.sb("i_pre", [rows, T]), sc.sb("f_pre", [rows, T])
        soft = sc.sb("soft", [rows, T])
        ones = sc.sb("ones", [rows, T])
        cum, a_run, m_run, shift = (sc.sb(n, [rows, T]) for n in ("cum", "a_run", "m_run", "shift"))
        a_out, m_out, f_out = (sc.sb(n, [rows, T]) for n in ("a_out", "m_out", "f_out"))
        cols = sc.sb("cols", [P, HM, NDIR, TT])
        ident = sc.sb("ident", [P, P])
        flip = [sc.pb(f"flip{i}", [P, TT // 2, rows]) for i in range(2)]
        ident_made, zeroed, loaded, chain, acts = (sc.sem(n) for n in
                                                   ("ident_made", "zeroed", "loaded", "chain", "acts"))
        a_final, m_final, f_final, flipped, cols_made, stored = (sc.sem(n) for n in (
            "a_final", "m_final", "f_final", "flipped", "cols_made", "stored"))
        fwd, bwd = slice(0, HALF), slice(HALF, rows)
        seqs, at = [], 0
        for n in SEQS:
            seqs.append(slice(at, at + n))
            at += n
        src = gate_rows.rearrange("(d g h) t -> d g h t", d=2, g=2)
        b_v = b_if.rearrange("l d g h -> (l d) g h")

        with nc.Block() as block:

            @block.sync
            def _(sp):
                sp.wait_ge(zeroed, CREDIT + 4)
                for d, r in ((0, 0), (1, HALF)):
                    sp.dma_start(i_raw[r:r + HM, :], src[d, 0]).then_inc(loaded, 16)
                    sp.dma_start(f_raw[r:r + HM, :], src[d, 1]).then_inc(loaded, 16)
                    sp.dma_start(i_bias[r:r + HM, :], b_v[d, 0].rearrange("(h o) -> h o", o=1)).then_inc(loaded, 16)
                    sp.dma_start(f_bias[r:r + HM, :], b_v[d, 1].rearrange("(h o) -> h o", o=1)).then_inc(loaded, 16)
                sp.wait_ge(m_final, CREDIT + 3)
                for d, r in ((0, HALF), (1, 0)):
                    sp.dma_start(neg_max[:, d, :], m_out[r:r + HM, :]).then_inc(stored, 16)
                sp.wait_ge(f_final, CREDIT + 3)
                for d, r in ((0, HALF), (1, 0)):
                    sp.dma_start(floor[:, d, :], f_out[r:r + HM, :]).then_inc(stored, 16)
                sp.wait_ge(cols_made, CREDIT + 4)
                sp.dma_start(a_cols.rearrange("h p d t -> p h d t"), cols[:]).then_inc(stored, 16)
                sp.wait_ge(stored, CREDIT + 16 * 5)

            @block.gpsimd
            def _(pool):
                for tile in (i_raw, f_raw, i_bias, f_bias):
                    nc.gpsimd.memset(tile[:], 0.0).then_inc(zeroed, 1)
                make_identity(nc, pool, ident, ident_made)

            @block.vector
            def _(dve):
                done = [0]

                def link(ins):
                    done[0] += 1
                    ins.then_inc(chain, 1)
                    dve.wait_ge(chain, CREDIT + done[0])

                nc.vector.memset(ones[:], 1.0)
                dve.wait_ge(loaded, CREDIT + 16 * 8)
                for raw, bias, pre in ((f_raw, f_bias, f_pre), (i_raw, i_bias, i_pre)):
                    nc.vector.tensor_scalar_add(pre[fwd, :], raw[fwd, :], bias[fwd, :])
                    for s in seqs:
                        last = nc.vector.tensor_scalar_add(pre[bwd, s], raw[bwd, s][:, ::-1], bias[bwd, :])
                    link(last)
                dve.wait_ge(acts, CREDIT + 3)
                link(nc.vector.scalar_tensor_tensor(out=soft[:], in0=f_pre[:], scalar=0.0, in1=soft[:],
                                                    op0=ALU.min, op1=ALU.subtract))
                for s in seqs:
                    last = nc.vector.tensor_tensor_scan(out=cum[:, s], data0=ones[:, s], data1=soft[:, s], initial=0.0,
                                                        op0=ALU.mult, op1=ALU.add)
                link(last)
                link(nc.vector.tensor_sub(a_run[:], i_pre[:], cum[:]))
                for s in seqs:
                    last = nc.vector.tensor_tensor_scan(out=m_run[:, s], data0=a_run[:, s], data1=a_run[:, s],
                                                        initial=0.0, op0=ALU.max, op1=ALU.max)
                link(last)
                link(nc.vector.tensor_add(shift[:], cum[:], m_run[:]))
                nc.vector.tensor_copy(a_out[fwd, :], a_run[fwd, :]).then_inc(a_final, 1)
                for s in seqs:
                    nc.vector.tensor_copy(a_out[bwd, s], a_run[bwd, s][:, ::-1]).then_inc(a_final, 1)
                nc.vector.tensor_scalar_mul(m_out[fwd, :], m_run[fwd, :], -1.0).then_inc(m_final, 1)
                for s in seqs:
                    nc.vector.tensor_scalar_mul(m_out[bwd, s], m_run[bwd, s][:, ::-1], -1.0).then_inc(m_final, 1)
                for b in range(2):
                    dve.wait_ge(flipped, CREDIT + b + 1)
                    for d, r in ((0, HALF), (1, 0)):
                        nc.vector.tensor_copy(cols[:, :, d, b * TT // 2:(b + 1) * TT // 2],
                                              flip[b][:, :, r:r + HM].rearrange("p t h -> p h t"))\
                            .then_inc(cols_made, 1)

            @block.scalar
            def _(act):
                act.wait_ge(chain, CREDIT + 1)
                nc.scalar.activation(soft[:], f_pre[:], ACT.Abs).then_inc(acts, 1)
                act.wait_ge(acts, CREDIT + 1)
                nc.scalar.activation(soft[:], soft[:], ACT.Exp, scale=-1.0).then_inc(acts, 1)
                act.wait_ge(acts, CREDIT + 2)
                nc.scalar.activation(soft[:], soft[:], ACT.Ln, bias=1.0).then_inc(acts, 1)
                act.wait_ge(chain, CREDIT + 7)
                nc.scalar.activation(f_out[fwd, :], shift[fwd, :], ACT.Exp, scale=-1.0).then_inc(f_final, 1)
                for s in seqs:
                    nc.scalar.activation(f_out[bwd, s], shift[bwd, s][:, ::-1], ACT.Exp, scale=-1.0).then_inc(f_final, 1)

            @block.tensor
            def _(pe):
                pe.wait_ge(ident_made, CREDIT + 2)
                pe.wait_ge(a_final, CREDIT + 3)
                for b in range(2):
                    for t in range(TT // 2):
                        tok = (b * TT // 2 + t) * P
                        last = nc.tensor.transpose(flip[b][:, t, :], a_out[:, tok:tok + P], ident[0:rows, 0:rows])
                    last.then_inc(flipped, 1)


CHUNKS = [(0, 8, 0), (0, 8, 4), (8, 4, 8)]
BLK = CH // P
UNITS = sum(n for _, n, _ in CHUNKS)
FIRST = [sum(m for _, m, _ in CHUNKS[:c]) for c in range(NCH + 1)]


def units_of_head():
    return [(c, first + i, (first + i - own if own <= first + i < own + BLK else None), first + i < own)
            for c, (first, n, own) in enumerate(CHUNKS) for i in range(n)]


KQ_PIECES = [("k", 0), ("q", 0), ("k", 1), ("q", 1), ("k", 2), ("q", 2)]
NKQ = len(KQ_PIECES)
KQ_RING = 3
TICKS = UNITS


def head_plan():
    plan = {e: [] for e in ("sp", "pool", "act", "dve", "pe")}

    def at(engine, tick, kind, n):
        plan[engine].append((tick, kind, n))

    units = units_of_head()
    start = [2 + FIRST[c] for c in range(NCH)]
    end = [1 + FIRST[c + 1] for c in range(NCH)]
    for n, (c, s, j, _) in enumerate(units):
        score, value = 2 + n, VALUES_AFTER + n
        if j is not None:
            at("dve", score - 1.0, "argument", n)
        at("act", score - 0.2, "decay", n)
        at("pe", score, "scores", n)
        at("dve", score + 0.9, "weigh", n)
        at("pool", score + 1.2, "sum", n)
        at("dve", value - 1.6, "scale", n)
        at("act", value - 1.1, "high", n)
        at("pool" if j is None else "dve", value - 0.7, "low", n)
        at("pe", value, "values", n)
    for c in range(NCH):
        at("dve", start[c] - 1.5, "zero", c)
        for k, (engine, kind) in enumerate((("pe", "den"), ("act", "abs"), ("sp", "move"), ("dve", "invert"),
                                            ("sp", "keep"), ("sp", "spread"))):
            at(engine, end[c] + (2.3, 3.0, 3.1, 4.2, 4.3, 5.0)[k], kind, c)
        out = VALUES_AFTER + FIRST[c + 1] - 1 + 0.4
        at("dve", out, "gate", c)
        at("pool", out + 0.8, "gate", c)
        at("sp", out + 1.7, "store", c)
        at("sp", (15.5 + 4, out - 6, out - 2.3)[c], "load gates", c)
        at("sp", (-6, 2, 5)[c], "load nmax", c)
        at("sp", (3, 4, 7)[c], "load floor", c)
        at("act", (13.3, 17.3, 21.3)[c], "v high", c)
        at("pool", (13.8, 17.8, 21.8)[c], "v low", c)
        at("sp", (10, 14.5, 18.5)[c], "load v", c)
    for m in range(NKQ):
        tick = (0.2, 0.8, 3.3, 6.3, 12.3, 14.3)[m]
        at("act", tick, "kq high", m)
        at("dve", tick + 0.5, "kq low", m)
        at("sp", (-11, -6.5, -4.5, 1.5, 2.5, 5)[m], "load kq", m)
    return plan


VALUES_AFTER = 17.0


def mlstm(nc, p_feat, p_tok, neg_max, floor, a_cols, inverse, g_mem):
    with Scope(nc, "m") as sc:
        units, plan = units_of_head(), head_plan()
        own_no = {n: k for k, n in enumerate(n for n, u in enumerate(units) if u[2] is not None)}
        OWN = len(own_no)
        half = UNITS // 2
        raw_kq = [sc.sb(f"raw_kq{b}", [P, 2, CH]) for b in range(KQ_RING)]
        raw_v = sc.sb("raw_v", [P, BLK, DM])
        hi = {n: sc.sb(f"hi_{n}", [P, 2, T] if n != "v" else [P, TT, DM], F32R) for n in "qkv"}
        lo = {n: sc.sb(f"lo_{n}", [P, 2, T] if n != "v" else [P, TT, DM], F32R) for n in "qkv"}
        a_col = [sc.sb(f"a_col{c}", [P, NDIR, TT]) for c in range(NCH)]
        nmax = [sc.sb(f"nmax{c}", [P, NDIR, CH]) for c in range(NCH)]
        norm = [sc.sb(f"norm{c}", [P, NDIR, CH]) for c in range(NCH)]
        wsum = [sc.sb(f"wsum{c}", [P, NDIR, CH]) for c in range(NCH)]
        wbuf = sc.sb("wbuf", [P, UNITS, CH])
        wfwd = sc.sb("wfwd", [P, OWN, P])
        dec = [sc.sb(f"dec{b}", [P, BLK + 1, P]) for b in range(2)]
        arg = [sc.sb(f"arg{b}", [P, NDIR, P]) for b in range(2)]
        w_hi = [sc.sb(f"w_hi{b}", [P, CH], F32R) for b in range(2)]
        w_lo = [sc.sb(f"w_lo{b}", [P, CH], F32R) for b in range(2)]
        gate_o, gate_z, out_s = (sc.sb(n, [P, 2, CH]) for n in ("gate_o", "gate_z", "out_s"))
        mask = sc.sb("mask", [P, NDIR, P])
        ones = sc.sb("ones", [P, 1])
        den_row = sc.sb("den_row", [1, NDIR * CH])
        DC = NDIR * CH // P
        den_col = sc.sb("den_col", [P, DC])
        floor_col = [sc.sb(f"floor_col{c}", [P, DC]) for c in range(NCH)]
        scr = [sc.pb(f"scr{b}", [P, CH]) for b in range(4)]
        den = sc.pb("den", [1, NDIR, CH])
        hout = sc.pb("hout", [P, 2, CH])

        mask_made, ones_made = sc.sem("mask_made"), sc.sem("ones_made")
        kq_loaded = sc.sems("kq_loaded", KQ_RING)
        v_loaded = sc.sem("v_loaded")
        nmax_loaded = sc.sems("nmax_loaded", NCH)
        gates_loaded = sc.sem("gates_loaded")
        kq_hi, kq_lo, v_hi, v_lo = (sc.sem(n) for n in ("kq_hi", "kq_lo", "v_hi", "v_lo"))
        scored = sc.sem("scored")
        arg_made = sc.sem("arg_made")
        dec_made = sc.sems("dec_made", 2)
        weighed = sc.sems("weighed", 4)
        wsum_zeroed = sc.sem("wsum_zeroed")
        wsum_step = sc.sem("wsum_step")
        den_full, abs_made, den_moved = (sc.sem(n) for n in ("den_full", "abs_made", "den_moved"))
        floor_loaded = sc.sems("floor_loaded", NCH)
        max_made, inv_made, inv_stored = sc.sem("max_made"), sc.sem("inv_made"), sc.sem("inv_stored")
        norm_spread = sc.sems("norm_spread", NCH)
        scaled_part, scaled = sc.sem("scaled_part"), sc.sem("scaled")
        whi_made, wlo_made = sc.sems("whi_made", 2), sc.sems("wlo_made", 2)
        valued = sc.sems("valued", 2)
        out_read, out_made, out_stored = sc.sem("out_read"), sc.sem("out_made"), sc.sem("out_stored")

        wsum_count, n_w = {}, 0
        for n, (_, _, j, _) in enumerate(units):
            n_w += 1 if j is None else (3 if j < BLK - 1 else 2)
            wsum_count[n] = n_w
        WS = n_w

        def once_more(h):
            return not (isinstance(h, int) and h == 0)

        def piece(n, pc):
            return (slice(None), slice(None), slice(pc * CH, (pc + 1) * CH)) if n != "v" else \
                (slice(None), slice(pc * BLK, (pc + 1) * BLK), slice(None))

        def feat(row, h, c):
            v = p_feat[bass.ds(h * DM + row, DM), c * CH:(c + 1) * CH]
            return v.rearrange("(b p) t -> p b t", p=P)

        with nc.Block() as block:

            @block.sync
            def _(sp):
                def step(kind, c, h):
                    t = slice(c * CH, (c + 1) * CH)
                    if kind == "load kq":
                        m, (name, pc) = c, KQ_PIECES[c]
                        if m >= KQ_RING:
                            sp.wait_ge(kq_lo, CREDIT + h * NKQ + m - KQ_RING + 1)
                        elif once_more(h):
                            sp.wait_ge(kq_lo, CREDIT + h * NKQ + m - KQ_RING + 1)
                        sp.dma_start(raw_kq[m % KQ_RING][:], feat(R_QM + (W_M if name == "k" else 0), h, pc))\
                            .then_inc(kq_loaded[m % KQ_RING], 16)
                    elif kind == "load v":
                        v = p_tok[t, bass.ds(h * DM + S_VM, DM)].rearrange("(b p) c -> p b c", p=P)
                        sp.wait_ge(v_lo, CREDIT + h * NCH + c)
                        sp.dma_start(raw_v[:], v).then_inc(v_loaded, 16)
                    elif kind == "load nmax":
                        if once_more(h):
                            for q in range(2):
                                sp.wait_ge(dec_made[q], CREDIT + h * half - half + FIRST[c + 1] // 2)
                        sp.dma_start(nmax[c][:], neg_max[bass.ds(h, 1), :, t].to_broadcast([P, NDIR, CH]))\
                            .then_inc(nmax_loaded[c], 16)
                        sp.dma_start(a_col[c][:], a_cols[bass.ds(h, 1)].rearrange("o p d t -> (o p) d t"))\
                            .then_inc(nmax_loaded[c], 16)
                    elif kind == "load floor":
                        if once_more(h):
                            sp.wait_ge(max_made, CREDIT + h * NCH - NCH + c + 1)
                        for d in range(NDIR):
                            v = floor[bass.ds(h, 1), d, t].rearrange("o (p k) -> (o p) k", k=DC)
                            sp.dma_start(floor_col[c][d * CH // DC:(d + 1) * CH // DC, :], v)\
                                .then_inc(floor_loaded[c], 16)
                    elif kind == "load gates":
                        sp.wait_ge(out_made, CREDIT + h * NCH + c)
                        sp.dma_start(gate_o[:], feat(R_OM, h, c)).then_inc(gates_loaded, 16)
                        sp.dma_start(gate_z[:], feat(R_ZM, h, c)).then_inc(gates_loaded, 16)
                    elif kind == "store":
                        sp.wait_ge(out_made, CREDIT + h * NCH + c + 1)
                        v = g_mem[bass.ds(h * DM, DM), t].rearrange("(b p) t -> p b t", p=P)
                        sp.dma_start(v, out_s[:]).then_inc(out_stored, 16)
                    elif kind == "move":
                        sp.wait_ge(abs_made, CREDIT + h * NCH + c + 1)
                        sp.wait_ge(inv_stored, CREDIT + 16 * (h * NCH + c))
                        sp.dma_start(den_col[:], den_row[:].rearrange("o (p k) -> o p k", k=DC))\
                            .then_inc(den_moved, 16)
                    elif kind == "keep":
                        sp.wait_ge(inv_made, CREDIT + h * NCH + c + 1)
                        if c:
                            sp.wait_ge(norm_spread[c - 1], CREDIT + h * 16 + 16)
                        elif once_more(h):
                            sp.wait_ge(norm_spread[NCH - 1], CREDIT + h * 16)
                        sp.dma_start(inverse.rearrange("(p k) -> p k", k=DC), den_col[:]).then_inc(inv_stored, 16)
                    elif kind == "spread":
                        sp.wait_ge(inv_stored, CREDIT + 16 * (h * NCH + c + 1))
                        if once_more(h):
                            sp.wait_ge(scaled, CREDIT + h * UNITS - (UNITS - FIRST[1] if c == 0 else 0))
                        sp.dma_start(norm[c][:].rearrange("p d t -> p (d t)"),
                                     inverse.rearrange("(o n) -> o n", o=1).to_broadcast([P, NDIR * CH]))\
                            .then_inc(norm_spread[c], 16)

                over_turns(sp, plan["sp"], step, HM, TICKS)
                sp.wait_ge(out_stored, CREDIT + 16 * HM * NCH)

            @block.gpsimd
            def _(pool):
                nc.gpsimd.memset(ones[:], 1.0).then_inc(ones_made, 1)
                nc.gpsimd.memset(mask[:], 0.0).then_inc(mask_made, 1)
                pool.wait_ge(mask_made, CREDIT + 1)
                for d, sign in ((0, 1), (1, -1)):
                    nc.gpsimd.affine_select(out=mask[:, d, :], in_=mask[:, d, :], compare_op=ALU.is_ge, fill=-1e30,
                                            base=0, pattern=[[-sign, P]], channel_multiplier=sign)\
                        .then_inc(mask_made, 1)

                def step(kind, n, h):
                    if kind == "v low":
                        pool.wait_ge(v_hi, CREDIT + h * NCH + n + 1)
                        cut = piece("v", n)
                        nc.gpsimd.tensor_sub(lo["v"][cut], raw_v[:], hi["v"][cut].bitcast(F32)).then_inc(v_lo, 1)
                    elif kind == "sum":
                        c, s, j, fwd = units[n]
                        if n in FIRST:
                            pool.wait_ge(wsum_zeroed, CREDIT + h * NCH + c + 1)
                        pool.wait_ge(weighed[n % 4], CREDIT + h * (UNITS // 4) + n // 4 + 1)
                        if j is None:
                            parts = [(int(fwd), slice(0, CH), wbuf[:, n, :])]
                        else:
                            own, past = slice(j * P, (j + 1) * P), (j + 1) * P
                            parts = [(0, slice(0, past), wbuf[:, n, 0:past]), (1, own, wfwd[:, own_no[n], :])]
                            if past < CH:
                                parts.append((1, slice(past, CH), wbuf[:, n, past:CH]))
                        pool.wait_ge(wsum_step, CREDIT + h * WS + wsum_count[n] - len(parts))
                        for d, dst, src in parts:
                            nc.gpsimd.tensor_add(wsum[c][:, d, dst], wsum[c][:, d, dst], src).then_inc(wsum_step, 1)
                    elif kind == "low":
                        par = n % 2
                        pool.wait_ge(whi_made[par], CREDIT + h * half + n // 2 + 1)
                        pool.wait_ge(valued[par], CREDIT + h * half + n // 2)
                        nc.gpsimd.tensor_sub(w_lo[par][:], wbuf[:, n, :], w_hi[par][:].bitcast(F32))\
                            .then_inc(wlo_made[par], 1)
                    elif kind == "gate":
                        pool.wait_ge(out_read, CREDIT + h * NCH + n + 1)
                        nc.gpsimd.tensor_mul(out_s[:], out_s[:], gate_z[:]).then_inc(out_made, 1)

                over_turns(pool, plan["pool"], step, HM, TICKS)

            @block.scalar
            def _(act):
                def step(kind, n, h):
                    if kind == "kq high":
                        name, pc = KQ_PIECES[n]
                        act.wait_ge(kq_loaded[n % KQ_RING], CREDIT + h * 32 + n // KQ_RING * 16 + 16)
                        if once_more(h):
                            act.wait_ge(scored, CREDIT + h * UNITS - (UNITS - FIRST[2] if pc < 2 else 0))
                        nc.scalar.activation(hi[name][piece(name, pc)], raw_kq[n % KQ_RING][:], ACT.Copy)\
                            .then_inc(kq_hi, 1)
                    elif kind == "v high":
                        act.wait_ge(v_loaded, CREDIT + 16 * (h * NCH + n + 1))
                        if once_more(h):
                            for q in range(2):
                                act.wait_ge(valued[q], CREDIT + h * half - (half - FIRST[2] // 2 if n < 2 else 0))
                        nc.scalar.activation(hi["v"][piece("v", n)], raw_v[:], ACT.Copy).then_inc(v_hi, 1)
                    elif kind == "decay":
                        c, s, j, fwd = units[n]
                        par = n % 2
                        if n in FIRST:
                            act.wait_ge(nmax_loaded[c], CREDIT + h * 32 + 32)
                        if n >= 2 or once_more(h):
                            act.wait_ge(weighed[(n - 2) % 4], CREDIT + h * (UNITS // 4) + (n - 2) // 4 + 1)
                        flat = dec[par][:].rearrange("p b t -> p (b t)")
                        col = a_col[c][:, :, s:s + 1]
                        todo = []
                        if j is None:
                            d = int(fwd)
                            todo.append((flat[:, 0:CH], nmax[c][:, d, :], col[:, d]))
                        else:
                            if j:
                                todo.append((flat[:, 0:j * P], nmax[c][:, 0, 0:j * P], col[:, 0]))
                            if j < BLK - 1:
                                x = slice((j + 1) * P, CH)
                                todo.append((flat[:, x], nmax[c][:, 1, x], col[:, 1]))
                            todo.append((dec[par][:, j::BLK - j, :], arg[par][:], 0.0))
                        for m, (dst, src, bias) in enumerate(todo):
                            if j is not None and m == len(todo) - 1:
                                act.wait_ge(arg_made, CREDIT + h * OWN + own_no[n] + 1)
                            ins = nc.scalar.activation(dst, src, ACT.Exp, bias=bias)
                        ins.then_inc(dec_made[par], 1)
                    elif kind == "abs":
                        act.wait_ge(den_full, CREDIT + h * NCH + n + 1)
                        act.wait_ge(den_moved, CREDIT + 16 * (h * NCH + n))
                        nc.scalar.activation(den_row[:], den[:].rearrange("o d t -> o (d t)"), ACT.Abs)\
                            .then_inc(abs_made, 1)
                    elif kind == "high":
                        par = n % 2
                        act.wait_ge(valued[par], CREDIT + h * half + n // 2)
                        act.wait_ge(scaled, CREDIT + h * UNITS + n + 1)
                        nc.scalar.activation(w_hi[par][:], wbuf[:, n, :], ACT.Copy).then_inc(whi_made[par], 1)

                over_turns(act, plan["act"], step, HM, TICKS)

            @block.vector
            def _(dve):
                def step(kind, n, h):
                    if kind == "kq low":
                        name, pc = KQ_PIECES[n]
                        dve.wait_ge(kq_hi, CREDIT + h * NKQ + n + 1)
                        cut = piece(name, pc)
                        nc.vector.tensor_sub(lo[name][cut], raw_kq[n % KQ_RING][:], hi[name][cut].bitcast(F32))\
                            .then_inc(kq_lo, 1)
                    elif kind == "zero":
                        if once_more(h):
                            dve.wait_ge(den_full, CREDIT + h * NCH - NCH + n + 1)
                        nc.vector.memset(wsum[n][:], 0.0).then_inc(wsum_zeroed, 1)
                    elif kind == "argument":
                        c, s, j, fwd = units[n]
                        par = n % 2
                        dve.wait_ge(nmax_loaded[c], CREDIT + h * 32 + 32)
                        if n >= 2 or once_more(h):
                            dve.wait_ge(dec_made[par], CREDIT + h * half + n // 2)
                        for d in range(NDIR):
                            ins = nc.vector.scalar_tensor_tensor(
                                out=arg[par][:, d, :], in0=nmax[c][:, d, j * P:(j + 1) * P],
                                scalar=a_col[c][:, d, s:s + 1], in1=mask[:, d, :], op0=ALU.add, op1=ALU.min)
                        ins.then_inc(arg_made, 1)
                    elif kind == "weigh":
                        c, s, j, fwd = units[n]
                        par = n % 2
                        if once_more(h):
                            dve.wait_ge(wlo_made[par], CREDIT + h * half - half + n // 2 + 1)
                        dve.wait_ge(scored, CREDIT + h * UNITS + n + 1)
                        dve.wait_ge(dec_made[par], CREDIT + h * half + n // 2 + 1)
                        flat = dec[par][:].rearrange("p b t -> p (b t)")
                        ins = nc.vector.scalar_tensor_tensor(
                            out=wbuf[:, n, :], in0=scr[n % 4][:], scalar=DM ** -0.5, in1=flat[:, 0:CH],
                            op0=ALU.mult, op1=ALU.mult)
                        if j is not None:
                            ins = nc.vector.scalar_tensor_tensor(
                                out=wfwd[:, own_no[n], :], in0=scr[n % 4][:, j * P:(j + 1) * P], scalar=DM ** -0.5,
                                in1=flat[:, CH:], op0=ALU.mult, op1=ALU.mult)
                        ins.then_inc(weighed[n % 4], 1)
                    elif kind == "invert":
                        dve.wait_ge(den_moved, CREDIT + 16 * (h * NCH + n + 1))
                        dve.wait_ge(floor_loaded[n], CREDIT + 32 * h + 32)
                        nc.vector.tensor_max(den_col[:], den_col[:], floor_col[n][:]).then_inc(max_made, 1)
                        dve.wait_ge(max_made, CREDIT + h * NCH + n + 1)
                        nc.vector.reciprocal(den_col[:], den_col[:]).then_inc(inv_made, 1)
                    elif kind == "scale":
                        c, s, j, fwd = units[n]
                        if n in FIRST:
                            dve.wait_ge(norm_spread[c], CREDIT + 16 * h + 16)
                        dve.wait_ge(wsum_step, CREDIT + h * WS + wsum_count[n])
                        w = wbuf[:, n, :]
                        if j is None:
                            nc.vector.tensor_mul(w, w, norm[c][:, int(fwd), :]).then_inc(scaled, 1)
                        else:
                            own, past = slice(j * P, (j + 1) * P), (j + 1) * P
                            fw = wfwd[:, own_no[n], :]
                            if past < CH:
                                nc.vector.tensor_mul(w[:, past:CH], w[:, past:CH], norm[c][:, 1, past:CH])
                            nc.vector.tensor_mul(w[:, 0:past], w[:, 0:past], norm[c][:, 0, 0:past])
                            nc.vector.tensor_mul(fw, fw, norm[c][:, 1, own]).then_inc(scaled_part, 1)
                            dve.wait_ge(scaled_part, CREDIT + h * OWN + own_no[n] + 1)
                            nc.vector.tensor_add(w[:, own], w[:, own], fw).then_inc(scaled, 1)
                    elif kind == "low":
                        par = n % 2
                        dve.wait_ge(whi_made[par], CREDIT + h * half + n // 2 + 1)
                        dve.wait_ge(valued[par], CREDIT + h * half + n // 2)
                        nc.vector.tensor_sub(w_lo[par][:], wbuf[:, n, :], w_hi[par][:].bitcast(F32))\
                            .then_inc(wlo_made[par], 1)
                    elif kind == "gate":
                        dve.wait_ge(valued[1], CREDIT + h * half + FIRST[n + 1] // 2)
                        dve.wait_ge(gates_loaded, CREDIT + 32 * (h * NCH + n + 1))
                        dve.wait_ge(out_stored, CREDIT + 16 * (h * NCH + n))
                        nc.vector.tensor_mul(out_s[:], hout[:], gate_o[:]).then_inc(out_read, 1)

                dve.wait_ge(mask_made, CREDIT + 3)
                over_turns(dve, plan["dve"], step, HM, TICKS)

            @block.tensor
            def _(pe):
                def kq_before(c, s):
                    return {0: 2 if s < BLK else 3, 1: 4, 2: 6}[c]

                def step(kind, n, h):
                    if kind == "scores":
                        c, s, j, fwd = units[n]
                        t, src = slice(c * CH, (c + 1) * CH), slice(s * P, (s + 1) * P)
                        pe.wait_ge(kq_lo, CREDIT + h * NKQ + kq_before(c, s))
                        pe.wait_ge(weighed[n % 4], CREDIT + h * (UNITS // 4) + n // 4)
                        for d in range(2):
                            nc.tensor.matmul(scr[n % 4][:], hi["k"][:, d, src], hi["q"][:, d, t], start=(d == 0), stop=False)
                            nc.tensor.matmul(scr[n % 4][:], hi["k"][:, d, src], lo["q"][:, d, t], start=False, stop=False)
                            ins = nc.tensor.matmul(scr[n % 4][:], lo["k"][:, d, src], hi["q"][:, d, t], start=False, stop=(d == 1))
                        ins.then_inc(scored, 1)
                    elif kind == "den":
                        pe.wait_ge(wsum_step, CREDIT + h * WS + wsum_count[FIRST[n + 1] - 1])
                        pe.wait_ge(abs_made, CREDIT + h * NCH + n)
                        for d in range(NDIR):
                            ins = nc.tensor.matmul(den[:, d, :], ones[:], wsum[n][:, d, :], start=True, stop=True)
                        ins.then_inc(den_full, 1)
                    elif kind == "values":
                        c, s, j, fwd = units[n]
                        par = n % 2
                        first, last = n == FIRST[c], n == FIRST[c + 1] - 1
                        if first:
                            pe.wait_ge(out_read, CREDIT + h * NCH + c)
                        pe.wait_ge(v_lo, CREDIT + h * NCH + s // BLK + 1)
                        pe.wait_ge(wlo_made[par], CREDIT + h * half + n // 2 + 1)
                        for d in range(2):
                            f = slice(d * P, (d + 1) * P)
                            nc.tensor.matmul(hout[:, d, :], hi["v"][:, s, f], w_hi[par][:], start=first, stop=False)
                            nc.tensor.matmul(hout[:, d, :], hi["v"][:, s, f], w_lo[par][:], start=False, stop=False)
                            ins = nc.tensor.matmul(hout[:, d, :], lo["v"][:, s, f], w_hi[par][:], start=False, stop=last)
                        ins.then_inc(valued[par], 1)

                pe.wait_ge(ones_made, CREDIT + 1)
                over_turns(pe, plan["pe"], step, HM, TICKS)


QK = HA + KVA
NST = HA + 2 * KVA


def rotation_plan():
    plan = {e: [] for e in ("sp", "pool", "act", "dve", "pe")}
    for b in range(2):
        for engine, tick, kind in (
                ("sp", -0.7, "load"), ("dve", 0.0, "tables"), ("act", 0.0, "square"), ("dve", 0.15, "sum squares"),
                ("act", 0.3, "root"), ("dve", 0.35, "cosine"), ("dve", 0.4, "invert"), ("pool", 0.3, "sine"),
                ("dve", 0.75, "add"), ("pool", 0.85, "normalise"), ("act", 1.1, "high"), ("dve", 1.3, "low"),
                ("pe", 1.5, "transpose"), ("act", 1.6, "empty"), ("dve", 1.8, "empty"), ("sp", 2.0, "store")):
            plan[engine].append((tick + b, kind, b))
    return plan


def rotate(nc, p_tok, rope, q_gain, k_gain, stacks, v_stacks):
    with Scope(nc, "r") as sc:
        x = [sc.sb(f"x{b}", [P, QK + KVA, DA]) for b in range(2)]
        trig = [sc.sb(f"trig{b}", [P, 2, DA]) for b in range(2)]
        sq = [sc.sb(f"sq{b}", [P, QK, DA]) for b in range(2)]
        turn = [sc.sb(f"turn{b}", [P, QK, DA]) for b in range(2)]
        stat = [sc.sb(f"stat{b}", [P, 3, QK]) for b in range(2)]
        tab = [sc.sb(f"tab{b}", [P, 2, 2, DA]) for b in range(2)]
        st = [sc.sb(f"st{b}", [P, NST, 2, DA]) for b in range(2)]
        vst = [sc.sb(f"vst{b}", [P, KVA, 2, DA]) for b in range(2)]
        flat = [sc.sb(f"flat{b}", [P, NST, P]) for b in range(2)]
        gain = sc.sb("gain", [P, 2, 2, DA])
        ident = sc.sb("ident", [P, P])
        BANKS, BY_ACT = NST // 4, NST // 4 - 2
        flip = [sc.pb(f"flip{i}", [P, 4, P]) for i in range(BANKS)]
        ident_made, gain_loaded, gain_step = sc.sem("ident_made"), sc.sem("gain_loaded"), sc.sem("gain_step")
        loaded = sc.sems("loaded", 2)
        squared, summed, eps_added, rooted, rstd_made = (sc.sem(n) for n in (
            "squared", "summed", "eps_added", "rooted", "rstd_made"))
        tab_made, cos_made, sin_made, turned, normed = (sc.sem(n) for n in (
            "tab_made", "cos_made", "sin_made", "turned", "normed"))
        hi_made, stacked, doubled = sc.sem("hi_made"), sc.sem("stacked"), sc.sem("doubled")
        flipped = sc.sems("flipped", BANKS)
        emptied = sc.sems("emptied", BANKS)
        stored = sc.sems("stored", 2)
        halves = "p h (a b c) -> p h a b c"
        plan = rotation_plan()
        q_and_k = ((0, slice(0, HA)), (1, slice(HA, QK)))

        def at_start(i):
            return isinstance(i, int) and i == 0

        with nc.Block() as block:

            @block.sync
            def _(sp):
                for n, src in enumerate((q_gain, k_gain)):
                    sp.dma_start(gain[:, n, 0, :], src.to_broadcast([P, DA])).then_inc(gain_loaded, 16)

                def step(kind, b, i):
                    t, rows = i * 2 + b, bass.ds(i * (2 * P) + b * P, P)
                    if kind == "load":
                        if not at_start(i):
                            sp.wait_ge(stacked, CREDIT + 3 * t - 3)
                        sp.dma_start(x[b][:], p_tok[rows, S_QA:S_VM].rearrange("p (h d) -> p h d", d=DA))\
                            .then_inc(loaded[b], 16)
                        sp.dma_start(trig[b][:], rope[rows].rearrange("p (s d) -> p s d", d=DA)).then_inc(loaded[b], 16)
                    elif kind == "store":
                        sp.wait_ge(emptied[BY_ACT - 1], CREDIT + t + 1)
                        sp.wait_ge(emptied[BANKS - 1], CREDIT + t + 1)
                        sp.dma_start(stacks[:, :, rows].rearrange("n p t -> p n t"), flat[b][:]).then_inc(stored[b], 16)
                        sp.dma_start(v_stacks[rows], vst[b][:].rearrange("p h s d -> p h (s d)")).then_inc(stored[b], 16)

                over_turns(sp, plan["sp"], step, TT // 2, 2)
                for b in range(2):
                    sp.wait_ge(stored[b], CREDIT + 32 * (TT // 2))

            @block.gpsimd
            def _(pool):
                make_identity(nc, pool, ident, ident_made)
                pool.wait_ge(gain_loaded, CREDIT + 32)
                for n in range(2):
                    g_in = gain[:, n, 0, :].rearrange("p (a b c) -> p a b c", a=2, b=2)
                    g_out = gain[:, n, 1, :].rearrange("p (a b c) -> p a b c", a=2, b=2)
                    for h in range(2):
                        nc.gpsimd.tensor_copy(g_out[:, :, h, :], g_in[:, :, 1 - h, :]).then_inc(gain_step, 1)

                def step(kind, b, i):
                    t = i * 2 + b
                    if kind == "sine":
                        pool.wait_ge(tab_made, CREDIT + 4 * t + 4)
                        pool.wait_ge(squared, CREDIT + t + 1)
                        pool.wait_ge(summed, CREDIT + t + 1)
                        xv, sv = x[b][:, 0:QK, :].rearrange(halves, a=2, b=2), sq[b][:].rearrange(halves, a=2, b=2)
                        for n, heads in q_and_k:
                            m = heads.stop - heads.start
                            tv = tab[b][:, n:n + 1, 1, :].rearrange(halves, a=2, b=2)
                            for h in range(2):
                                nc.gpsimd.tensor_mul(sv[:, heads, :, h, :], xv[:, heads, :, 1 - h, :],
                                                     tv[:, :, :, h, :].to_broadcast([P, m, 2, DA // 4]))\
                                    .then_inc(sin_made, 1)
                    elif kind == "normalise":
                        pool.wait_ge(rstd_made, CREDIT + t + 1)
                        pool.wait_ge(turned, CREDIT + t + 1)
                        nc.gpsimd.tensor_mul(turn[b][:], turn[b][:],
                                             stat[b][:, 2, :].rearrange("p (h o) -> p h o", o=1).to_broadcast([P, QK, DA]))\
                            .then_inc(normed, 1)

                over_turns(pool, plan["pool"], step, TT // 2, 2)

            @block.vector
            def _(dve):
                dve.wait_ge(gain_step, CREDIT + 4)

                def step(kind, b, i):
                    t = i * 2 + b
                    if kind == "tables":
                        dve.wait_ge(loaded[b], CREDIT + 32 * (i + 1))
                        if not at_start(i):
                            dve.wait_ge(sin_made, CREDIT + 4 * t - 4)
                        for n, s in ((0, DA ** -0.5), (1, 1.0)):
                            for k in range(2):
                                nc.vector.scalar_tensor_tensor(out=tab[b][:, n, k, :], in0=trig[b][:, k, :], scalar=s,
                                                               in1=gain[:, n, k, :], op0=ALU.mult, op1=ALU.mult)\
                                    .then_inc(tab_made, 1)
                    elif kind == "sum squares":
                        dve.wait_ge(squared, CREDIT + t + 1)
                        nc.vector.tensor_reduce(out=stat[b][:, 0, :], in_=sq[b][:], axis=AX.X, op=ALU.add)\
                            .then_inc(summed, 1)
                        dve.wait_ge(summed, CREDIT + t + 1)
                        nc.vector.tensor_scalar(stat[b][:, 1, :], stat[b][:, 0, :], 1.0 / DA, EPS, ALU.mult, ALU.add)\
                            .then_inc(eps_added, 1)
                    elif kind == "cosine":
                        dve.wait_ge(tab_made, CREDIT + 4 * t + 4)
                        if not at_start(i):
                            dve.wait_ge(hi_made, CREDIT + 3 * t - 3)
                        for n, heads in q_and_k:
                            m = heads.stop - heads.start
                            nc.vector.tensor_mul(turn[b][:, heads, :], x[b][:, heads, :],
                                                 tab[b][:, n:n + 1, 0, :].to_broadcast([P, m, DA])).then_inc(cos_made, 1)
                    elif kind == "invert":
                        dve.wait_ge(rooted, CREDIT + t + 1)
                        nc.vector.reciprocal(stat[b][:, 2, :], stat[b][:, 1, :]).then_inc(rstd_made, 1)
                    elif kind == "add":
                        dve.wait_ge(cos_made, CREDIT + 2 * t + 2)
                        dve.wait_ge(sin_made, CREDIT + 4 * t + 4)
                        nc.vector.tensor_add(turn[b][:], turn[b][:], sq[b][:]).then_inc(turned, 1)
                    elif kind == "low":
                        dve.wait_ge(hi_made, CREDIT + 3 * t + 3)
                        nc.vector.tensor_sub(st[b][:, 0:HA, 1, :], turn[b][:, 0:HA, :], st[b][:, 0:HA, 0, :])\
                            .then_inc(stacked, 1)
                        nc.vector.tensor_sub(st[b][:, QK:NST, 0, :], turn[b][:, HA:QK, :], st[b][:, HA:QK, 0, :])\
                            .then_inc(stacked, 1)
                        nc.vector.tensor_sub(vst[b][:, :, 1, :], x[b][:, QK:, :], vst[b][:, :, 0, :]).then_inc(stacked, 1)
                        dve.wait_ge(stacked, CREDIT + 3 * t + 3)
                        nc.vector.tensor_copy(st[b][:, HA:NST, 1, :], st[b][:, HA:NST, 0, :]).then_inc(doubled, 1)
                    elif kind == "empty":
                        for f in range(BY_ACT, BANKS):
                            dve.wait_ge(flipped[f], CREDIT + t + 1)
                            if f == BY_ACT:
                                dve.wait_ge(stored[b], CREDIT + 32 * i)
                            nc.vector.tensor_copy(flat[b][:, 4 * f:4 * f + 4, :], flip[f][:]).then_inc(emptied[f], 1)

                over_turns(dve, plan["dve"], step, TT // 2, 2)

            @block.scalar
            def _(act):
                def step(kind, b, i):
                    t = i * 2 + b
                    if kind == "square":
                        act.wait_ge(loaded[b], CREDIT + 32 * (i + 1))
                        if not at_start(i):
                            act.wait_ge(turned, CREDIT + t - 1)
                        nc.scalar.activation(sq[b][:], x[b][:, 0:QK, :], ACT.Square).then_inc(squared, 1)
                    elif kind == "root":
                        act.wait_ge(eps_added, CREDIT + t + 1)
                        nc.scalar.activation(stat[b][:, 1, :], stat[b][:, 1, :], ACT.Sqrt).then_inc(rooted, 1)
                    elif kind == "high":
                        act.wait_ge(normed, CREDIT + t + 1)
                        if not at_start(i):
                            act.wait_ge(flipped[BANKS - 1], CREDIT + t - 1)
                        act.wait_ge(stored[b], CREDIT + 32 * i)
                        nc.scalar.activation(st[b][:, 0:HA, 0, :].bitcast(F32R), turn[b][:, 0:HA, :], ACT.Copy)\
                            .then_inc(hi_made, 1)
                        nc.scalar.activation(st[b][:, HA:QK, 0, :].bitcast(F32R), turn[b][:, HA:QK, :], ACT.Copy)\
                            .then_inc(hi_made, 1)
                        nc.scalar.activation(vst[b][:, :, 0, :].bitcast(F32R), x[b][:, QK:, :], ACT.Copy)\
                            .then_inc(hi_made, 1)
                    elif kind == "empty":
                        for f in range(BY_ACT):
                            act.wait_ge(flipped[f], CREDIT + t + 1)
                            nc.scalar.activation(flat[b][:, 4 * f:4 * f + 4, :], flip[f][:], ACT.Copy)\
                                .then_inc(emptied[f], 1)

                over_turns(act, plan["act"], step, TT // 2, 2)

            @block.tensor
            def _(pe):
                def step(kind, b, i):
                    t = i * 2 + b
                    pe.wait_ge(doubled, CREDIT + t + 1)
                    pe.wait_ge(stacked, CREDIT + 3 * t + 3)
                    for f in range(BANKS):
                        pe.wait_ge(emptied[f], CREDIT + t)
                        for n in range(4):
                            src = st[b][:, 4 * f + n, :, :].rearrange("p s d -> p (s d)")
                            last = nc.tensor.transpose(flip[f][:, n, :], src, ident[:])
                        last.then_inc(flipped[f], 1)

                pe.wait_ge(ident_made, CREDIT + 2)
                over_turns(pe, plan["pe"], step, TT // 2, 2)


NU = TT
HEADS_IT = 4
UIT = NU * HEADS_IT
NCI = HEADS_IT * NCH
FLIPS = 3
QUARTERS = 4


def keys_of(q_tile):
    at = 0
    for n in SEQS:
        if q_tile * P < at + n:
            return at // P, n // P
        at += n


def attention_units():
    units, groups = [], 0
    for hd in range(HEADS_IT):
        for q in range(NU):
            first, n = keys_of(q)
            units.append((hd, q, first, n, list(range(groups, groups + n // 4))))
            groups += n // 4
    return units, groups


def attention_plan():
    plan = {e: [] for e in ("sp", "pool", "act", "dve", "pe")}

    def at(engine, tick, kind, n):
        plan[engine].append((tick, kind, n))

    for m, (_, _, _, _, gs) in enumerate(attention_units()[0]):
        at("pe", m, "scores", m)
        at("dve", m + MAX_AT, "maximum", m)
        at("act", m + EXP_AT, "exponent", m)
        at("dve", m + INV_AT, "invert", m)
        at("pool", m + NORM_AT, "normalise", m)
        at("pe", m + FLIP_AT, "transpose", m)
        for i in range(len(gs)):
            at("act", m + HIGH_AT[i], "high", (m, i))
            at("dve", m + LOW_AT[i], "low", (m, i))
    for ci in range(NCI):
        done = 4 * ci + 3 + FLIP_AT
        for q in range(QUARTERS):
            at("pe", done + VALUE_AT + q, "values", (ci, q))
        at("act", done + FOLD_AT, "fold", ci)
        at("dve", done + ADD_AT, "add", ci)
        at("pool", done + GATE_AT, "gate", ci)
        at("sp", done + 7, "store", ci)
    half = UIT // 2
    for slot in range(2):
        at("sp", (slot - 1) * half + 1, "load q and k", slot)
        at("sp", (slot - 1) * half + FLIP_AT + 7, "load v and gate", slot)
    return plan


MAX_AT, EXP_AT, INV_AT, NORM_AT, FLIP_AT = 0.6, 1.05, 1.7, 2.0, 3.4
HIGH_AT, LOW_AT = (3.9, 3.95), (4.0, 4.05)
VALUE_AT, FOLD_AT, ADD_AT, GATE_AT = 2.0, 5.2, 5.4, 5.65


def attend(nc, p_feat, stacks, v_stacks, g_att):
    with Scope(nc, "t") as sc:
        units, groups = attention_units()
        plan = attention_plan()
        q_t = [sc.sb(f"q{s}", [P, 2, T], F32R) for s in range(2)]
        k_t = [sc.sb(f"k{s}", [P, 2, T], F32R) for s in range(2)]
        v_t = [sc.sb(f"v{s}", [P, TT, P], F32R) for s in range(2)]
        gate = [sc.sb(f"gate{s}", [DA, 2, T]) for s in range(2)]
        prob = [sc.sb(f"prob{r}", [P, SEQS[0]]) for r in range(3)]
        nmax, rsum = sc.sb("nmax", [P, 4]), sc.sb("rsum", [P, 2, 4])
        pt_hi = [sc.sb(f"pt_hi{b}", [P, SEQS[0] // P, CH], F32R) for b in range(2)]
        pt_lo = [sc.sb(f"pt_lo{b}", [P, SEQS[0] // P, CH], F32R) for b in range(2)]
        low = [sc.sb(f"low{b}", [DA, CH]) for b in range(2)]
        att = [sc.sb(f"att{b}", [DA, CH]) for b in range(2)]
        ident = sc.sb("ident", [P, P])
        scr = [sc.pb(f"scr{b}", [P, SEQS[0]]) for b in range(2)]
        flip = [sc.pb(f"flip{b}", [P, 4, P]) for b in range(FLIPS)]
        out = sc.pb("out", [P, CH])

        ident_made = sc.sem("ident_made")
        qk_loaded = sc.sems("qk_loaded", 2)
        vg_loaded = sc.sems("vg_loaded", 2)
        scored = sc.sem("scored")
        max_made = sc.sem("max_made")
        exp_made = sc.sems("exp_made", 2)
        inv_made = sc.sem("inv_made")
        normed = sc.sem("normed")
        flipped = sc.sems("flipped", 3)
        hi_made, lo_made = sc.sems("hi_made", FLIPS), sc.sems("lo_made", FLIPS)
        multiplied = sc.sem("multiplied")
        low_made = sc.sem("low_made")
        summed = sc.sem("summed")
        gated, stored = sc.sem("gated"), sc.sems("stored", 2)

        before, per_slot = [], [0, 0, 0]
        for m, u in enumerate(units):
            before.append(per_slot[m % 3])
            per_slot[m % 3] += len(u[4])

        per_bank = [len(range(b, groups, FLIPS)) for b in range(FLIPS)]

        def place(m, i):
            return (slice(None), slice(4 * i, 4 * i + 4), slice((m % 4) * P, (m % 4 + 1) * P))

        with nc.Block() as block:

            @block.sync
            def _(sp):
                def step(kind, n, g):
                    first = isinstance(g, int) and g == 0
                    if kind == "load q and k":
                        s = n
                        if not first:
                            sp.wait_ge(scored, CREDIT + g * UIT - (1 - s) * (UIT // 2))
                        hd = g * HEADS_IT + 2 * s
                        sp.dma_start(q_t[s][:].bitcast(F32), stacks[bass.ds(hd, 2)].rearrange("n p t -> p n t"))\
                            .then_inc(qk_loaded[s], 16)
                        for part in range(2):
                            sp.dma_start(k_t[s][:, part:part + 1, :].bitcast(F32),
                                         stacks[bass.ds(g + HA + part * KVA, 1)].rearrange("n p t -> p n t"))\
                                .then_inc(qk_loaded[s], 16)
                    elif kind == "load v and gate":
                        s = n
                        if not first:
                            sp.wait_ge(gated, CREDIT + g * NCI - (1 - s) * (NCI // 2))
                        v = v_stacks[:, bass.ds(g, 1), :].rearrange("(t p) o d -> p t (o d)", p=P)
                        sp.dma_start(v_t[s][:].bitcast(F32), v).then_inc(vg_loaded[s], 16)
                        rows = p_feat[bass.ds(g * (HEADS_IT * DA) + (R_ZA + 2 * s * DA), 2 * DA), :]
                        sp.dma_start(gate[s][:], rows.rearrange("(n p) t -> p n t", p=DA)).then_inc(vg_loaded[s], 16)
                    elif kind == "store":
                        hd, c = n // NCH, n % NCH
                        sp.wait_ge(gated, CREDIT + g * NCI + n + 1)
                        sp.dma_start(g_att[bass.ds(g * (HEADS_IT * DA) + hd * DA, DA), c * CH:(c + 1) * CH],
                                     att[n % 2][:]).then_inc(stored[n % 2], 16)

                over_turns(sp, plan["sp"], step, KVA, UIT)
                for b in range(2):
                    sp.wait_ge(stored[b], CREDIT + 16 * KVA * NCI // 2)

            @block.gpsimd
            def _(pool):
                make_identity(nc, pool, ident, ident_made)

                def step(kind, n, g):
                    if kind == "normalise":
                        w = units[n][3] * P
                        pool.wait_ge(inv_made, CREDIT + g * UIT + n + 1)
                        nc.gpsimd.tensor_mul(prob[n % 3][:, 0:w], prob[n % 3][:, 0:w],
                                             rsum[:, 1, n % 4:n % 4 + 1].to_broadcast([P, w])).then_inc(normed, 1)
                    elif kind == "gate":
                        hd, c = n // NCH, n % NCH
                        pool.wait_ge(summed, CREDIT + g * NCI + n + 1)
                        nc.gpsimd.tensor_mul(att[n % 2][:], att[n % 2][:],
                                             gate[hd // 2][:, hd % 2, c * CH:(c + 1) * CH]).then_inc(gated, 1)

                over_turns(pool, plan["pool"], step, KVA, UIT)

            @block.vector
            def _(dve):
                def step(kind, n, g):
                    if kind == "maximum":
                        w = units[n][3] * P
                        dve.wait_ge(scored, CREDIT + g * UIT + n + 1)
                        nc.vector.tensor_reduce(out=nmax[:, n % 4:n % 4 + 1], in_=scr[n % 2][:, 0:w], axis=AX.X,
                                                op=ALU.max, negate=True).then_inc(max_made, 1)
                    elif kind == "invert":
                        dve.wait_ge(exp_made[n % 2], CREDIT + g * (UIT // 2) + n // 2 + 1)
                        nc.vector.reciprocal(rsum[:, 1, n % 4:n % 4 + 1], rsum[:, 0, n % 4:n % 4 + 1])\
                            .then_inc(inv_made, 1)
                    elif kind == "low":
                        m, i = n
                        x, b = units[m][4][i], (m // 4) % 2
                        dve.wait_ge(hi_made[x % FLIPS], CREDIT + g * per_bank[x % FLIPS] + x // FLIPS + 1)
                        nc.vector.tensor_sub(pt_lo[b][place(m, i)], flip[x % FLIPS][:],
                                             pt_hi[b][place(m, i)].bitcast(F32)).then_inc(lo_made[x % FLIPS], 1)
                    elif kind == "add":
                        dve.wait_ge(low_made, CREDIT + g * NCI + n + 1)
                        dve.wait_ge(stored[n % 2], CREDIT + 16 * (g * (NCI // 2) + n // 2))
                        if n % (NCI // 2) == 0:
                            dve.wait_ge(vg_loaded[n // (NCI // 2)], CREDIT + 32 * (g + 1))
                        nc.vector.tensor_add(att[n % 2][:], out[0:DA, :], low[n % 2][:])\
                            .then_inc(summed, 1)

                over_turns(dve, plan["dve"], step, KVA, UIT)

            @block.scalar
            def _(act):
                def step(kind, n, g):
                    if kind == "exponent":
                        w = units[n][3] * P
                        act.wait_ge(max_made, CREDIT + g * UIT + n + 1)
                        act.wait_ge(flipped[n % 3], CREDIT + g * per_slot[n % 3] + before[n])
                        if n >= 3 or not (isinstance(g, int) and g == 0):
                            act.wait_ge(inv_made, CREDIT + g * UIT + n - 3)
                        nc.scalar.activation(prob[n % 3][:, 0:w], scr[n % 2][:, 0:w], ACT.Exp,
                                             bias=nmax[:, n % 4:n % 4 + 1], accum_out=rsum[:, 0, n % 4:n % 4 + 1])\
                            .then_inc(exp_made[n % 2], 1)
                    elif kind == "high":
                        m, i = n
                        x, ci = units[m][4][i], m // 4
                        if m % 4 == 0 and i == 0:
                            if ci >= 2 or not (isinstance(g, int) and g == 0):
                                act.wait_ge(multiplied, CREDIT + g * NCI + ci - 1)
                        act.wait_ge(flipped[m % 3], CREDIT + g * per_slot[m % 3] + before[m] + i + 1)
                        nc.scalar.activation(pt_hi[ci % 2][place(m, i)], flip[x % FLIPS][:], ACT.Copy)\
                            .then_inc(hi_made[x % FLIPS], 1)
                    elif kind == "fold":
                        act.wait_ge(multiplied, CREDIT + g * NCI + n + 1)
                        if n >= 2 or not (isinstance(g, int) and g == 0):
                            act.wait_ge(summed, CREDIT + g * NCI + n - 1)
                        nc.scalar.activation(low[n % 2][:], out[DA:P, :], ACT.Copy).then_inc(low_made, 1)

                over_turns(act, plan["act"], step, KVA, UIT)

            @block.tensor
            def _(pe):
                def step(kind, n, g):
                    if kind == "scores":
                        hd, q, first, _, gs = units[n]
                        s = hd // 2
                        if n % (UIT // 2) == 0:
                            pe.wait_ge(qk_loaded[s], CREDIT + 48 * (g + 1))
                        pe.wait_ge(exp_made[n % 2], CREDIT + g * (UIT // 2) + n // 2)
                        for i in range(len(gs)):
                            keys = slice(first * P + i * CH, first * P + (i + 1) * CH)
                            for part in range(2):
                                ins = nc.tensor.matmul(scr[n % 2][:, i * CH:(i + 1) * CH],
                                                       q_t[s][:, hd % 2, q * P:(q + 1) * P],
                                                       k_t[s][:, part, keys], start=(part == 0), stop=(part == 1))
                        ins.then_inc(scored, 1)
                    elif kind == "transpose":
                        pe.wait_ge(normed, CREDIT + g * UIT + n + 1)
                        for i, x in enumerate(units[n][4]):
                            pe.wait_ge(lo_made[x % FLIPS], CREDIT + g * per_bank[x % FLIPS] + x // FLIPS)
                            for j in range(4):
                                ins = nc.tensor.transpose(flip[x % FLIPS][:, j, :],
                                                          prob[n % 3][:, (4 * i + j) * P:(4 * i + j + 1) * P], ident[:])
                            ins.then_inc(flipped[n % 3], 1)
                    elif kind == "values":
                        ci, quarter = n
                        hd = ci // NCH
                        _, _, first, tiles, gs = units[4 * ci + 3]
                        if quarter == 0:
                            y = gs[-1]
                            pe.wait_ge(lo_made[y % FLIPS], CREDIT + g * per_bank[y % FLIPS] + y // FLIPS + 1)
                            pe.wait_ge(summed, CREDIT + g * NCI + ci)
                            if ci % (NCI // 2) == 0:
                                pe.wait_ge(vg_loaded[hd // 2], CREDIT + 32 * (g + 1))
                        for i in range(quarter * tiles // QUARTERS, (quarter + 1) * tiles // QUARTERS):
                            for part, pt in enumerate((pt_hi, pt_lo)):
                                ins = nc.tensor.matmul(out[:], v_t[hd // 2][:, first + i, :], pt[ci % 2][:, i, :],
                                                       start=(i == 0 and part == 0),
                                                       stop=(i == tiles - 1 and part == 1))
                        if quarter == QUARTERS - 1:
                            ins.then_inc(multiplied, 1)

                pe.wait_ge(ident_made, CREDIT + 2)
                over_turns(pe, plan["pe"], step, KVA, UIT)


STAGES = 3
ACT_PCS = KT // 2


def finish(nc, x, p_feat, g_mem, g_att, w_mo, w_ao, w_out, norm_final, part, merged, y):
    with Scope(nc, "f") as sc:
        act_hi = sc.sb("act_hi", [P, KT, T], F32R)
        act_lo = sc.sb("act_lo", [P, KT, T], F32R)
        w_hi = sc.sb("w_hi", [P, 2, KT, UNIT], F32R)
        w_lo = sc.sb("w_lo", [P, 2, KT, UNIT], F32R)
        raw = sc.sb("raw", [P, KT // 2, UNIT])
        act_raw = [sc.sb(f"act_raw{b}", [P, 2, CH]) for b in range(2)]
        add = [sc.sb(f"add{b}", [P, CH]) for b in range(2)]
        stage = sc.sb("stage", [P, QUADS, 4, CH])
        stat = sc.sb("stat", [P, 2, 4])
        acc = [sc.pb(f"acc{b}", [P, CH]) for b in range(NB)]
        room = stage[:].rearrange("p a b c -> p (a b c)")
        xt = [room[:, j * D:(j + 1) * D] for j in range(2)]
        yt = [room[:, (2 + j) * D:(3 + j) * D] for j in range(2)]
        gain, junk = room[:, 4 * D:5 * D], room[:, 5 * D:6 * D]

        raw_loaded = sc.sem("raw_loaded")
        w_hi_made, w_lo_made = sc.sem("w_hi_made"), sc.sem("w_lo_made")
        act_loaded = sc.sems("act_loaded", 2)
        act_hi_made = sc.sem("act_hi_made")
        act_lo_made = sc.sems("act_lo_made", 2)
        acc_full = sc.sems("acc_full", 2)
        evacuated = sc.sems("evacuated", NB)
        gate_loaded = sc.sems("gate_loaded", QUADS)
        add_loaded, gated, stored = sc.sems("add_loaded", 2), sc.sem("gated"), sc.sems("stored", QUADS)
        x_loaded, gain_loaded = sc.sems("x_loaded", 2), sc.sem("gain_loaded")
        summed, squared, mean_made, root_made, rstd_made, normed = (sc.sem(n) for n in (
            "summed", "squared", "mean_made", "root_made", "rstd_made", "normed"))
        y_stored = sc.sems("y_stored", 2)
        UNITS_F = 2 * STAGES
        PIECES_F = NCH * ACT_PCS
        weights = (w_mo, w_ao, w_out)
        sources = (g_mem, g_att, merged)

        def fview(ap):
            return ap.rearrange("(b p) t -> p b t", p=P)

        with nc.Block() as block:

            @block.sync
            def _(sp):
                def load_half(n, h):
                    s, slot = n // 2, n % 2
                    if 2 * n + h > 0:
                        sp.wait_ge(w_lo_made, CREDIT + (2 * n + h) * KT // 2)
                    v = weights[s].rearrange("(k p) n -> p k n", p=P)
                    sp.dma_start(raw[:], v[:, h * KT // 2:(h + 1) * KT // 2, slot * UNIT:(slot + 1) * UNIT])\
                        .then_inc(raw_loaded, 16)

                def load_act(s, c):
                    v = fview(sources[s])
                    for i in range(ACT_PCS):
                        pc = (s * NCH + c) * ACT_PCS + i
                        if pc >= 2:
                            sp.wait_ge(act_lo_made[pc % 2], CREDIT + pc // 2)
                        sp.dma_start(act_raw[pc % 2][:], v[:, 2 * i:2 * i + 2, c * CH:(c + 1) * CH])\
                            .then_inc(act_loaded[pc % 2], 16)

                load_half(0, 0)
                load_half(0, 1)
                load_act(0, 0)
                load_half(1, 0)
                load_act(0, 1)
                load_act(0, 2)
                for n in range(UNITS_F - 2):
                    s, slot = n // 2, n % 2
                    load_half(n + 1, 1)
                    load_half(n + 2, 0)
                    for c in range(NCH):
                        if n:
                            sp.wait_ge(stored[c], CREDIT + 16 * n)
                        v = fview(p_feat[R_GM + s * D + slot * UNIT:R_GM + s * D + (slot + 1) * UNIT, :])
                        sp.dma_start(stage[:, c], v[:, :, c * CH:(c + 1) * CH]).then_inc(gate_loaded[c], 16)
                    for c in range(NCH):
                        t = slice(c * CH, (c + 1) * CH)
                        rows = slice(slot * UNIT, (slot + 1) * UNIT)
                        if s == 1:
                            if slot == 0 and c == 0:
                                for q in range(QUADS):
                                    sp.wait_ge(stored[q], CREDIT + 16 * 2)
                            for j in range(4):
                                m = (slot * NCH + c) * 4 + j
                                if m >= 2:
                                    sp.wait_ge(gated, CREDIT + 2 * NG + m - 1)
                                at = slot * UNIT + j * P
                                sp.dma_start(add[m % 2][:], part[at:at + P, t]).then_inc(add_loaded[m % 2], 16)
                        sp.wait_ge(gated, CREDIT + n * NG + 4 * c + 4)
                        dst = (part, merged)[s]
                        sp.dma_start(fview(dst[rows, :])[:, :, t], stage[:, c]).then_inc(stored[c], 16)
                        if slot == 1:
                            if s == 1:
                                sp.wait_ge(stored[c], CREDIT + 16 * 4)
                            load_act(s + 1, c)
                load_half(UNITS_F - 1, 1)
                for q in range(QUADS):
                    sp.wait_ge(stored[q], CREDIT + 16 * 4)
                sp.dma_start(gain, norm_final.to_broadcast([P, D])).then_inc(gain_loaded, 16)
                for t in range(TT):
                    b = t % 2
                    if t >= 2:
                        sp.wait_ge(summed, CREDIT + t - 1)
                    sp.dma_start(xt[b], x[t * P:(t + 1) * P, :]).then_inc(x_loaded[b], 16)
                    if t:
                        sp.wait_ge(normed, CREDIT + t)
                        sp.dma_start(y[(t - 1) * P:t * P, :], yt[1 - b]).then_inc(y_stored[1 - b], 16)
                sp.wait_ge(normed, CREDIT + TT)
                sp.dma_start(y[(TT - 1) * P:, :], yt[(TT - 1) % 2]).then_inc(y_stored[(TT - 1) % 2], 16)
                for b in range(2):
                    sp.wait_ge(y_stored[b], CREDIT + 16 * TT // 2)

            def split_order(stage_no):
                yield from (("w", 2 * stage_no, k) for k in range(KT))
                if stage_no == 0:
                    yield from (("a", 0, i) for i in range(ACT_PCS))
                    yield from (("w", 1, k) for k in range(KT // 2))
                    yield from (("a", c, i) for c in (1, 2) for i in range(ACT_PCS))
                    yield from (("w", 1, k) for k in range(KT // 2, KT))
                else:
                    yield from (("a", c, i) for c in range(NCH) for i in range(ACT_PCS))
                    yield from (("w", 2 * stage_no + 1, k) for k in range(KT))

            @block.gpsimd
            def _(pool):
                for s in range(STAGES):
                    for kind, n, k in split_order(s):
                        if kind == "w":
                            pool.wait_ge(w_hi_made, CREDIT + n * KT + k + 1)
                            cut = (slice(None), n % 2, k, slice(None))
                            nc.gpsimd.tensor_sub(w_lo[cut], raw[:, k % (KT // 2), :], w_hi[cut].bitcast(F32))\
                                .then_inc(w_lo_made, 1)
                        else:
                            pc = (s * NCH + n) * ACT_PCS + k
                            pool.wait_ge(act_hi_made, CREDIT + pc + 1)
                            cut = (slice(None), slice(2 * k, 2 * k + 2), slice(n * CH, (n + 1) * CH))
                            nc.gpsimd.tensor_sub(act_lo[cut], act_raw[pc % 2][:], act_hi[cut].bitcast(F32))\
                                .then_inc(act_lo_made[pc % 2], 1)

            @block.scalar
            def _(act):
                for s in range(STAGES):
                    for kind, n, k in split_order(s):
                        if kind == "w":
                            act.wait_ge(raw_loaded, CREDIT + 16 * (2 * n + k // (KT // 2) + 1))
                            if n >= 2:
                                act.wait_ge(acc_full[n % 2], CREDIT + NG * (n // 2))
                            nc.scalar.activation(w_hi[:, n % 2, k, :], raw[:, k % (KT // 2), :], ACT.Copy)\
                                .then_inc(w_hi_made, 1)
                        else:
                            pc = (s * NCH + n) * ACT_PCS + k
                            act.wait_ge(act_loaded[pc % 2], CREDIT + 16 * (pc // 2 + 1))
                            if s:
                                act.wait_ge(acc_full[1], CREDIT + NG * (s - 1) + 4 * n + 4)
                            cut = (slice(None), slice(2 * k, 2 * k + 2), slice(n * CH, (n + 1) * CH))
                            nc.scalar.activation(act_hi[cut], act_raw[pc % 2][:], ACT.Copy).then_inc(act_hi_made, 1)
                for t in range(TT):
                    b = t % 2
                    act.wait_ge(summed, CREDIT + t + 1)
                    nc.scalar.activation(junk, yt[b], ACT.Square, accum_out=stat[:, b, 0:1]).then_inc(squared, 1)
                    act.wait_ge(mean_made, CREDIT + t + 1)
                    nc.scalar.activation(stat[:, b, 2:3], stat[:, b, 1:2], ACT.Sqrt).then_inc(root_made, 1)

            @block.vector
            def _(dve):
                for n in range(UNITS_F - 2):
                    s, slot = n // 2, n % 2
                    for m in range(NG):
                        c, j = m // 4, m % 4
                        dve.wait_ge(gate_loaded[c], CREDIT + 16 * (n + 1))
                        dve.wait_ge(acc_full[slot], CREDIT + NG * s + m + 1)
                        ins = nc.vector.tensor_mul(stage[:, c, j, :], stage[:, c, j, :], acc[m % NB][:])\
                            .then_inc(evacuated[m % NB], 1)
                        if s == 0:
                            dve.wait_ge(evacuated[m % NB], CREDIT + 2 * n + m // NB + 1)
                            dve.sem_inc(gated, 1)
                        else:
                            a = slot * NG + m
                            dve.wait_ge(add_loaded[a % 2], CREDIT + 16 * (a // 2 + 1))
                            dve.wait_ge(evacuated[m % NB], CREDIT + 2 * n + m // NB + 1)
                            nc.vector.tensor_add(stage[:, c, j, :], stage[:, c, j, :], add[a % 2][:]).then_inc(gated, 1)
                dve.wait_ge(gain_loaded, CREDIT + 16)
                for t in range(TT):
                    b = t % 2
                    dve.wait_ge(x_loaded[b], CREDIT + 16 * (t // 2 + 1))
                    if t >= 2:
                        dve.wait_ge(y_stored[b], CREDIT + 16 * (t // 2))
                    for h in range(2):
                        m = 2 * t + h
                        dve.wait_ge(acc_full[h], CREDIT + NG * 2 + t + 1)
                        cols = slice(h * CH, (h + 1) * CH)
                        nc.vector.tensor_add(yt[b][:, cols], xt[b][:, cols], acc[m % NB][:]).then_inc(evacuated[m % NB], 1)
                    for h in range(2):
                        m = 2 * t + h
                        dve.wait_ge(evacuated[m % NB], CREDIT + 8 + m // NB + 1)
                    dve.sem_inc(summed, 1)
                    dve.wait_ge(squared, CREDIT + t + 1)
                    nc.vector.tensor_scalar(stat[:, b, 1:2], stat[:, b, 0:1], 1.0 / D, EPS, ALU.mult, ALU.add)\
                        .then_inc(mean_made, 1)
                    dve.wait_ge(root_made, CREDIT + t + 1)
                    nc.vector.reciprocal(stat[:, b, 3:4], stat[:, b, 2:3]).then_inc(rstd_made, 1)
                    dve.wait_ge(rstd_made, CREDIT + t + 1)
                    nc.vector.scalar_tensor_tensor(out=yt[b], in0=yt[b], scalar=stat[:, b, 3:4], in1=gain,
                                                   op0=ALU.mult, op1=ALU.mult).then_inc(normed, 1)

            @block.tensor
            def _(pe):
                def act_ready(s, c, k):
                    pc = (s * NCH + c) * ACT_PCS + k // 2
                    pe.wait_ge(act_lo_made[pc % 2], CREDIT + pc // 2 + 1)

                for n in range(UNITS_F - 2):
                    s, slot = n // 2, n % 2
                    for m in range(NG):
                        c, cb = m // 4, m % 4
                        if n or m >= NB:
                            pe.wait_ge(evacuated[m % NB], CREDIT + 2 * n + m // NB)

                        def before_k(k):
                            if m == 0:
                                pe.wait_ge(w_lo_made, CREDIT + n * KT + k + 1)
                            if slot == 0 and cb == 0:
                                act_ready(s, c, k)

                        t, o = slice(c * CH, (c + 1) * CH), slice(cb * P, (cb + 1) * P)
                        product(nc, pe, acc[m % NB][:], lambda k: w_hi[:, slot, k, o], lambda k: w_lo[:, slot, k, o],
                                lambda k: act_hi[:, k, t], lambda k: act_lo[:, k, t], before_k)\
                            .then_inc(acc_full[slot], 1)
                for t in range(TT):
                    for h in range(2):
                        m = 2 * t + h
                        pe.wait_ge(evacuated[m % NB], CREDIT + 8 + m // NB)

                        def before_k(k):
                            if t == 0:
                                pe.wait_ge(w_lo_made, CREDIT + (4 + h) * KT + k + 1)
                            if h == 0 and t % 4 == 0:
                                act_ready(2, t // 4, k)

                        o = slice(t * P, (t + 1) * P)
                        product(nc, pe, acc[m % NB][:], lambda k: act_hi[:, k, o], lambda k: act_lo[:, k, o],
                                lambda k: w_hi[:, h, k, :], lambda k: w_lo[:, h, k, :], before_k)\
                            .then_inc(acc_full[h], 1)


def encoder_layer(nc, x, w_in, b_if, norm_pre, q_gain, k_gain, w_mo, w_ao, w_out, norm_final, rope, y):
    def scratch(name, *shape):
        return nc.dram_tensor(name, shape, F32, kind="Internal").ap()

    p_feat, p_tok = scratch("p_feat", R_END, T), scratch("p_tok", T, S_END)
    gate_rows = scratch("gate_rows", 4 * HM, T)
    neg_max, floor = scratch("neg_max", HM, NDIR, T), scratch("floor", HM, NDIR, T)
    a_cols = scratch("a_cols", HM, P, NDIR, TT)
    stacks, v_stacks = scratch("stacks", NST, P, T), scratch("v_stacks", T, KVA, P)
    g_mem, g_att = scratch("g_mem", W_M, T), scratch("g_att", W_A, T)
    part, merged = scratch("part", D, T), scratch("merged", D, T)
    project(nc, x, w_in, norm_pre, p_feat, p_tok, gate_rows)
    prepare_gates(nc, gate_rows, b_if, neg_max, floor, a_cols)
    mlstm(nc, p_feat, p_tok, neg_max, floor, a_cols, scratch("inverse", NDIR * CH), g_mem)
    rotate(nc, p_tok, rope, q_gain, k_gain, stacks, v_stacks)
    attend(nc, p_feat, stacks, v_stacks, g_att)
    finish(nc, x, p_feat, g_mem, g_att, w_mo, w_ao, w_out, norm_final, part, merged, y)


def rope_table(np):
    grid_w, half, theta = 64, DA // 4, 10000.0
    pos = np.concatenate([np.arange(n) for n in SEQS])
    freqs = theta ** (-np.arange(0, DA // 2, 2, dtype=np.float32) / np.float32(DA // 2))
    out = np.zeros((T, 2, 2, 2, half), np.float32)
    for axis, at in enumerate((pos // grid_w, pos % grid_w)):
        angle = at.astype(np.float32)[:, None] * freqs.astype(np.float32)
        out[:, 0, axis, :] = np.cos(angle)[:, None]
        out[:, 1, axis, 0], out[:, 1, axis, 1] = -np.sin(angle), np.sin(angle)
    return out.reshape(T, 2 * DA)


def kernel(x_prompt, x_sample, w_in, b_if, norm_pre, q_gain, k_gain, w_mo, w_ao, w_out, norm_final):
    import numpy as np
    import concourse.bacc as bacc
    from concourse.bass_utils import run_bass_kernel_spmd

    a = np.ascontiguousarray
    arrays = {
        "x": a(np.concatenate([np.asarray(x_prompt)[0], np.asarray(x_sample)[0]])),
        "w_in": a(np.asarray(w_in)[0]), "b_if": a(b_if), "norm_pre": a(norm_pre), "q_gain": a(q_gain),
        "k_gain": a(k_gain), "w_mo": a(np.asarray(w_mo)[0]), "w_ao": a(np.asarray(w_ao)[0]),
        "w_out": a(np.asarray(w_out)[0]), "norm_final": a(np.asarray(norm_final)[None, :]),
        "rope": rope_table(np),
    }
    nc = bacc.Bacc("TRN2", target_bir_lowering=False, num_devices=1)
    aps = {n: nc.dram_tensor(n, v.shape, F32, kind="ExternalInput").ap() for n, v in arrays.items()}
    y = nc.dram_tensor("y", (T, D), F32, kind="ExternalOutput").ap()
    encoder_layer(nc, y=y, **aps)
    r = run_bass_kernel_spmd(nc, [arrays], core_ids=[0])
    out = r.results[0]["y"]
    return out[None, 0:SEQS[0]], out[None, SEQS[0]:T]
```

```python
import concourse.bass as bass
from concourse import mybir
from contextlib import ExitStack

F32 = mybir.dt.float32
F32R = mybir.dt.float32r
ALU = mybir.AluOpType
ACT = mybir.ActivationFunctionType
AX = mybir.AxisListType

P = 128
D = 1024
SEQS = (1024, 512)
T = sum(SEQS)
TT = T // P
CH = 512
NCH = T // CH
KT = D // P
HM, DM = 4, 256
HA, KVA, DA = 16, 4, 64
GRP = HA // KVA
EPS = 1e-6
CREDIT = 1
W_M, W_A, W_KV = HM * DM, HA * DA, KVA * DA
C_QM, C_VM, C_OM, C_ZM = 0, 2 * W_M, 3 * W_M, 4 * W_M
C_IF = 5 * W_M
C_QA = C_IF + 4 * HM
C_KVA = C_QA + W_A
C_ZA = C_KVA + 2 * W_KV
C_GM = C_ZA + W_A
R_QM, R_OM, R_ZM, R_ZA, R_GM, R_END = 0, 2 * W_M, 3 * W_M, 4 * W_M, 4 * W_M + W_A, 4 * W_M + W_A + 2 * D
S_QA, S_KVA, S_VM, S_END = 0, W_A, W_A + 2 * W_KV, W_A + 2 * W_KV + W_M

UNIT = 512
CB = UNIT // P
NB = 6
NG = 12
QUADS = NG // 4


class Scope(ExitStack):

    def __init__(self, nc, tag):
        super().__init__()
        self.nc, self.tag, self.used = nc, tag, []
        self.callback(self.clear)

    def clear(self):
        self.nc.clear_and_free_semaphores(self.used)
        self.nc.all_engine_barrier()

    def sb(self, name, shape, dt=F32):
        return self.enter_context(self.nc.sbuf_tensor(f"{self.tag}_{name}", shape, dt))

    def pb(self, name, shape, dt=F32):
        return self.enter_context(self.nc.psum_tensor(f"{self.tag}_{name}", shape, dt))

    def sem(self, name):
        self.used.append(self.nc.alloc_semaphore(f"{self.tag}_{name}"))
        self.nc.gpsimd.sem_inc(self.used[-1], CREDIT)
        return self.used[-1]

    def sems(self, name, n):
        return [self.sem(f"{name}{i}") for i in range(n)]


def make_identity(nc, pool, ident, sem):
    nc.gpsimd.memset(ident[:], 0.0).then_inc(sem, 1)
    pool.wait_ge(sem, CREDIT + 1)
    nc.gpsimd.affine_select(out=ident[:], in_=ident[:], compare_op=ALU.not_equal, fill=1.0,
                            base=0, pattern=[[-1, P]], channel_multiplier=1).then_inc(sem, 1)


class Gemm:

    def __init__(self, sc):
        self.act_hi = sc.sb("act_hi", [P, KT, T], F32R)
        self.act_lo = sc.sb("act_lo", [P, KT, T], F32R)
        self.w_hi = sc.sb("w_hi", [P, 2, KT, UNIT], F32R)
        self.w_lo = sc.sb("w_lo", [P, 2, KT, UNIT], F32R)
        self.raw = sc.sb("raw", [P, KT, UNIT])
        self.stage = sc.sb("stage", [P, QUADS, 4, CH])
        self.acc = [sc.pb(f"acc{b}", [P, CH]) for b in range(NB)]
        self.raw_loaded = sc.sem("raw_loaded")
        self.hi_split = sc.sems("hi_split", 2)
        self.lo_split = sc.sems("lo_split", 2)
        self.acc_full = sc.sems("acc_full", 2)
        self.evacuated = sc.sems("evacuated", NB)
        self.stored = sc.sems("stored", QUADS)


def over_turns(eng, steps, step, count, ticks):
    first, last = (int(f(t for t, _, _ in steps) // ticks) for f in (min, max))
    order = sorted((t % ticks, t // ticks, kind, n) for t, kind, n in steps)

    def ticks_of(i):
        for _, late, kind, n in order:
            turn = i - int(late)
            if not isinstance(turn, int) or 0 <= turn < count:
                step(kind, n, turn)

    start = max(last, 1)
    for i in range(first, start):
        ticks_of(i)
    with eng.Fori(start, count + first) as i:
        ticks_of(i)
    for i in range(count + first, count + last):
        ticks_of(i)


def load_unit(sp, g, w_cols, slot, pair, width=UNIT):
    sp.wait_ge(g.lo_split[1 - slot], CREDIT + KT * (pair + slot))
    sp.dma_start(g.raw[:, :, 0:width], w_cols).then_inc(g.raw_loaded, 16)


def split_hi_unit(nc, dve, g, slot, pair, width=UNIT):
    dve.wait_ge(g.raw_loaded, CREDIT + 16 * (2 * pair + slot + 1))
    dve.wait_ge(g.acc_full[slot], CREDIT + NG * pair)
    for k in range(KT):
        nc.vector.tensor_copy(g.w_hi[:, slot, k, 0:width], g.raw[:, k, 0:width]).then_inc(g.hi_split[slot], 1)


def split_lo_unit(nc, pool, g, slot, pair, width=UNIT):
    for k in range(KT):
        pool.wait_ge(g.hi_split[slot], CREDIT + KT * pair + k + 1)
        nc.gpsimd.tensor_sub(g.w_lo[:, slot, k, 0:width], g.raw[:, k, 0:width],
                             g.w_hi[:, slot, k, 0:width].bitcast(F32)).then_inc(g.lo_split[slot], 1)


def product(nc, pe, out, stat_hi, stat_lo, mov_hi, mov_lo, before_k=None):
    for k in range(KT):
        if before_k:
            before_k(k)
        nc.tensor.matmul(out, stat_hi(k), mov_hi(k), start=(k == 0), stop=False)
        nc.tensor.matmul(out, stat_hi(k), mov_lo(k), start=False, stop=False)
        last = nc.tensor.matmul(out, stat_lo(k), mov_hi(k), start=False, stop=(k == KT - 1))
    return last


def multiply_unit(nc, pe, g, slot, pair, features, groups=NG, before_group=None):
    for n in range(groups):
        b = n % NB
        if before_group:
            before_group(n)
        pe.wait_ge(g.evacuated[b], CREDIT + 2 * (2 * pair + slot) + n // NB)

        def before_k(k, n=n):
            if n == 0:
                pe.wait_ge(g.hi_split[slot], CREDIT + KT * pair + k + 1)
                pe.wait_ge(g.lo_split[slot], CREDIT + KT * pair + k + 1)

        if features:
            c, cb = (n // CB, n % CB) if groups == NG else (n, 0)
            t, m = slice(c * CH, (c + 1) * CH), slice(cb * P, (cb + 1) * P)
            last = product(nc, pe, g.acc[b][:], lambda k: g.w_hi[:, slot, k, m], lambda k: g.w_lo[:, slot, k, m],
                           lambda k: g.act_hi[:, k, t], lambda k: g.act_lo[:, k, t], before_k)
        else:
            t = slice(n * P, (n + 1) * P)
            last = product(nc, pe, g.acc[b][:], lambda k: g.act_hi[:, k, t], lambda k: g.act_lo[:, k, t],
                           lambda k: g.w_hi[:, slot, k, :], lambda k: g.w_lo[:, slot, k, :], before_k)
        last.then_inc(g.acc_full[slot], 1)


def drain_unit(nc, act, g, slot, pair, func, out_quad):
    unit = 2 * pair + slot
    for q in range(QUADS):
        act.wait_ge(g.stored[q], CREDIT + 16 * unit)
        for j in range(4):
            n = 4 * q + j
            act.wait_ge(g.acc_full[slot], CREDIT + NG * pair + n + 1)
            nc.scalar.activation(g.stage[:, q, j, :], g.acc[n % NB][:], func).then_inc(g.evacuated[n % NB], 1)
        for j in range(4):
            n = 4 * q + j
            act.wait_ge(g.evacuated[n % NB], CREDIT + 2 * unit + n // NB + 1)
        act.dma_start(out_quad(q), g.stage[:, q]).then_inc(g.stored[q], 16)


def project(nc, x, w_in, norm_pre, p_feat, p_tok, gate_rows):
    with Scope(nc, "a") as sc:
        g = Gemm(sc)
        gain = sc.sb("gain", [P, D])
        ident = sc.sb("ident", [P, P])
        stat = sc.sb("stat", [P, 3, 4])
        flip = [sc.pb(f"flip{i}", [P, 4, P]) for i in range(2)]
        room = g.stage[:].rearrange("p a b c -> p (a b c)")
        xt = [room[:, j * D:(j + 1) * D] for j in range(3)]
        ht = [room[:, (3 + j) * D:(4 + j) * D] for j in range(3)]
        x_loaded = sc.sems("x_loaded", 3)
        gain_loaded = sc.sem("gain_loaded")
        ident_made = sc.sem("ident_made")
        squared = sc.sem("squared")
        mean_made = sc.sem("mean_made")
        root_made = sc.sem("root_made")
        rstd_made = sc.sem("rstd_made")
        h_made = sc.sem("h_made")
        flipped_a = sc.sem("flipped_a")
        flipped_b = sc.sems("flipped_b", 3)
        act_hi_made = sc.sems("act_hi_made", 2)
        act_lo_made = sc.sems("act_lo_made", 2)
        w_cols = w_in.rearrange("(k p) n -> p k n", p=P)

        feature_runs = [(C_OM, 1, ACT.Sigmoid, R_OM), (C_QM, 2, ACT.Copy, R_QM), (C_ZM, 1, ACT.Silu, R_ZM),
                        (C_ZA, 1, ACT.Silu, R_ZA), (C_GM, 2, ACT.Sigmoid, R_GM)]
        token_runs = [(C_VM, S_VM), (C_QA, S_QA)]
        runs = [(True, *r) for r in feature_runs] + [(False, c, 1, ACT.Copy, s) for c, s in token_runs]

        tile_plan = {"act": [], "dve": []}
        for j in range(3):
            for engine, tick, kind in (("act", 0.0, "square"), ("dve", 0.2, "mean"), ("act", 0.3, "root"),
                                       ("dve", 0.5, "normalise"), ("act", 1.6, "high"), ("dve", 1.75, "low")):
                tile_plan[engine].append((tick + j, kind, j))

        def over_pairs(eng, body):
            pair = 0
            for run in runs:
                if run[2] > 1:
                    with eng.Fori(0, run[2]) as i:
                        body(run, i + pair, i)
                else:
                    body(run, pair, 0)
                pair += run[2]
            return pair

        nc.all_engine_barrier()
        with nc.Block() as block:

            @block.sync
            def _(sp):
                sp.dma_start(gain[:], norm_pre.to_broadcast([P, D])).then_inc(gain_loaded, 16)
                for j in range(3):
                    sp.dma_start(xt[j], x[j * P:(j + 1) * P, :]).then_inc(x_loaded[j], 16)
                sp.dma_start(g.raw[:], w_cols[:, :, runs[0][1]:runs[0][1] + UNIT]).then_inc(g.raw_loaded, 16)
                with sp.Fori(1, TT // 3) as i:
                    for j in range(3):
                        sp.wait_ge(flipped_b[j], CREDIT + i)
                        sp.dma_start(xt[j], x[bass.ds(i * 3 * P + j * P, P), :]).then_inc(x_loaded[j], 16)

                def body(run, pair, i):
                    for slot in range(2):
                        if run is runs[0] and slot == 0:
                            continue
                        load_unit(sp, g, w_cols[:, :, bass.ds(i * 2 * UNIT + run[1] + slot * UNIT, UNIT)], slot, pair)

                last = over_pairs(sp, body)
                load_unit(sp, g, w_cols[:, :, C_KVA:C_KVA + UNIT], 0, last)
                load_unit(sp, g, w_cols[:, :, C_IF:C_IF + P], 1, last, P)

            @block.gpsimd
            def _(pool):
                make_identity(nc, pool, ident, ident_made)
                pool.wait_ge(g.raw_loaded, CREDIT + 16)
                for k in range(KT):
                    nc.gpsimd.tensor_copy(g.w_hi[:, 0, k, :], g.raw[:, k, :]).then_inc(g.hi_split[0], 1)

                def body(run, pair, i):
                    for slot in range(2):
                        split_lo_unit(nc, pool, g, slot, pair)

                last = over_pairs(pool, body)
                split_lo_unit(nc, pool, g, 0, last)
                split_lo_unit(nc, pool, g, 1, last, P)

            @block.vector
            def _(dve):
                def tile_step(kind, j, i):
                    t = i * 3 + j
                    if kind == "mean":
                        dve.wait_ge(squared, CREDIT + t + 1)
                        nc.vector.tensor_scalar(stat[:, j, 1:2], stat[:, j, 0:1], 1.0 / D, EPS, ALU.mult, ALU.add)\
                            .then_inc(mean_made, 1)
                    elif kind == "normalise":
                        dve.wait_ge(root_made, CREDIT + t + 1)
                        nc.vector.reciprocal(stat[:, j, 3:4], stat[:, j, 2:3]).then_inc(rstd_made, 1)
                        dve.wait_ge(rstd_made, CREDIT + t + 1)
                        dve.wait_ge(x_loaded[j], CREDIT + 16 * (i + 1))
                        nc.vector.scalar_tensor_tensor(out=ht[j], in0=xt[j], scalar=stat[:, j, 3:4], in1=gain[:],
                                                       op0=ALU.mult, op1=ALU.mult).then_inc(h_made, 1)
                    elif kind == "low":
                        for half in range(2):
                            dve.wait_ge(act_hi_made[half], CREDIT + t + 1)
                            cols = bass.ds(i * 3 * P + j * P, P)
                            nc.vector.tensor_sub(g.act_lo[:, 4 * half:4 * half + 4, cols], flip[half][:],
                                                 g.act_hi[:, 4 * half:4 * half + 4, cols].bitcast(F32))\
                                .then_inc(act_lo_made[half], 1)

                dve.wait_ge(gain_loaded, CREDIT + 16)
                over_turns(dve, tile_plan["dve"], tile_step, TT // 3, 3)

                def body(run, pair, i):
                    for slot in range(2):
                        if run is runs[0] and slot == 0:
                            continue
                        split_hi_unit(nc, dve, g, slot, pair)

                last = over_pairs(dve, body)
                split_hi_unit(nc, dve, g, 0, last)
                split_hi_unit(nc, dve, g, 1, last, P)

            @block.scalar
            def _(act):
                def tile_step(kind, j, i):
                    t = i * 3 + j
                    if kind == "square":
                        act.wait_ge(x_loaded[j], CREDIT + 16 * (i + 1))
                        act.wait_ge(flipped_b[j], CREDIT + i)
                        nc.scalar.activation(ht[j], xt[j], ACT.Square, accum_out=stat[:, j, 0:1]).then_inc(squared, 1)
                    elif kind == "root":
                        act.wait_ge(mean_made, CREDIT + t + 1)
                        nc.scalar.activation(stat[:, j, 2:3], stat[:, j, 1:2], ACT.Sqrt).then_inc(root_made, 1)
                    elif kind == "high":
                        for half in range(2):
                            if half:
                                act.wait_ge(flipped_b[j], CREDIT + i + 1)
                            else:
                                act.wait_ge(flipped_a, CREDIT + t + 1)
                            nc.scalar.activation(g.act_hi[:, 4 * half:4 * half + 4, bass.ds(i * 3 * P + j * P, P)],
                                                 flip[half][:], ACT.Copy).then_inc(act_hi_made[half], 1)

                over_turns(act, tile_plan["act"], tile_step, TT // 3, 3)

                def body(run, pair, i):
                    features, _, _, func, at = run
                    for slot in range(2):
                        if features:
                            rows = p_feat[bass.ds(i * 2 * UNIT + at + slot * UNIT, UNIT), :]
                            rows = rows.rearrange("(b p) t -> p b t", p=P)
                            drain_unit(nc, act, g, slot, pair, func, lambda q: rows[:, :, q * CH:(q + 1) * CH])
                        else:
                            cols = p_tok[:, at + slot * UNIT:at + (slot + 1) * UNIT]
                            cols = cols.rearrange("(b p) c -> p b c", p=P)
                            drain_unit(nc, act, g, slot, pair, func, lambda q: cols[:, 4 * q:4 * q + 4, :])

                last = over_pairs(act, body)
                cols = p_tok[:, S_KVA:S_VM].rearrange("(b p) c -> p b c", p=P)
                drain_unit(nc, act, g, 0, last, ACT.Copy, lambda q: cols[:, 4 * q:4 * q + 4, :])
                act.wait_ge(g.stored[0], CREDIT + 16 * (2 * last + 1))
                for c in range(NCH):
                    act.wait_ge(g.acc_full[1], CREDIT + NG * last + c + 1)
                    nc.scalar.activation(g.stage[0:4 * HM, 0, c, :], g.acc[c][0:4 * HM, :], ACT.Copy)\
                        .then_inc(g.evacuated[c], 1)
                for c in range(NCH):
                    act.wait_ge(g.evacuated[c], CREDIT + 2 * (2 * last + 1) + 1)
                act.dma_start(gate_rows.rearrange("r (c t) -> r c t", t=CH),
                              g.stage[0:4 * HM, 0, 0:NCH, :]).then_inc(g.stored[0], 16)
                act.wait_ge(g.stored[0], CREDIT + 16 * (2 * last + 2))
                for q in range(1, QUADS):
                    act.wait_ge(g.stored[q], CREDIT + 16 * (2 * last + 1))

            @block.tensor
            def _(pe):
                def transpose_tile(t):
                    pe.wait_ge(h_made, CREDIT + t + 1)
                    for half in range(2):
                        pe.wait_ge(act_lo_made[half], CREDIT + t)
                        for k in range(4):
                            col = (4 * half + k) * P
                            last = nc.tensor.transpose(flip[half][:, k, :], ht[t % 3][:, col:col + P], ident[:])
                        last.then_inc(flipped_b[t % 3] if half else flipped_a, 1)

                def before_group(n):
                    if n < CB:
                        for t in (6 + 2 * n, 7 + 2 * n):
                            if t < TT:
                                transpose_tile(t)
                    if n % CB == 0:
                        for half in range(2):
                            pe.wait_ge(act_lo_made[half], CREDIT + (n // CB + 1) * CH // P)

                pe.wait_ge(ident_made, CREDIT + 2)
                for t in range(6):
                    transpose_tile(t)

                def body(run, pair, i):
                    for slot in range(2):
                        multiply_unit(nc, pe, g, slot, pair, run[0],
                                      before_group=before_group if run is runs[0] and slot == 0 else None)

                last = over_pairs(pe, body)
                multiply_unit(nc, pe, g, 0, last, False)
                multiply_unit(nc, pe, g, 1, last, True, NCH)


NDIR = 2
HALF = 32


def prepare_gates(nc, gate_rows, b_if, neg_max, floor, a_cols):
    with Scope(nc, "g") as sc:
        rows = 2 * HALF
        i_raw, f_raw = sc.sb("i_raw", [rows, T]), sc.sb("f_raw", [rows, T])
        i_bias, f_bias = sc.sb("i_bias", [rows, 1]), sc.sb("f_bias", [rows, 1])
        i_pre, f_pre = sc.sb("i_pre", [rows, T]), sc.sb("f_pre", [rows, T])
        soft = sc.sb("soft", [rows, T])
        ones = sc.sb("ones", [rows, T])
        cum, a_run, m_run, shift = (sc.sb(n, [rows, T]) for n in ("cum", "a_run", "m_run", "shift"))
        a_out, m_out, f_out = (sc.sb(n, [rows, T]) for n in ("a_out", "m_out", "f_out"))
        cols = sc.sb("cols", [P, HM, NDIR, TT])
        ident = sc.sb("ident", [P, P])
        flip = [sc.pb(f"flip{i}", [P, TT // 2, rows]) for i in range(2)]
        ident_made, zeroed, i_loaded, f_loaded, chain, acts = (sc.sem(n) for n in (
            "ident_made", "zeroed", "i_loaded", "f_loaded", "chain", "acts"))
        a_final, m_final, f_final, flipped, cols_made, stored = (sc.sem(n) for n in (
            "a_final", "m_final", "f_final", "flipped", "cols_made", "stored"))
        fwd, bwd = slice(0, HALF), slice(HALF, rows)
        seqs, at = [], 0
        for n in SEQS:
            seqs.append(slice(at, at + n))
            at += n
        src = gate_rows.rearrange("(d g h) t -> d g h t", d=2, g=2)
        b_v = b_if.rearrange("l d g h -> (l d) g h")

        nc.all_engine_barrier()
        with nc.Block() as block:

            @block.sync
            def _(sp):
                sp.wait_ge(zeroed, CREDIT + 4)
                for g, raw, bias, sem in ((1, f_raw, f_bias, f_loaded), (0, i_raw, i_bias, i_loaded)):
                    for d, r in ((0, 0), (1, HALF)):
                        sp.dma_start(raw[r:r + HM, :], src[d, g]).then_inc(sem, 16)
                        sp.dma_start(bias[r:r + HM, :], b_v[d, g].rearrange("(h o) -> h o", o=1)).then_inc(sem, 16)
                sp.wait_ge(m_final, CREDIT + 3)
                for d, r in ((0, HALF), (1, 0)):
                    sp.dma_start(neg_max[:, d, :], m_out[r:r + HM, :]).then_inc(stored, 16)
                sp.wait_ge(f_final, CREDIT + 3)
                for d, r in ((0, HALF), (1, 0)):
                    sp.dma_start(floor[:, d, :], f_out[r:r + HM, :]).then_inc(stored, 16)
                sp.wait_ge(cols_made, CREDIT + 4)
                sp.dma_start(a_cols.rearrange("h p d t -> p h d t"), cols[:]).then_inc(stored, 16)
                sp.wait_ge(stored, CREDIT + 16 * 5)

            @block.gpsimd
            def _(pool):
                for tile in (f_raw, i_bias, f_bias):
                    nc.gpsimd.memset(tile[:], 0.0).then_inc(zeroed, 1)
                make_identity(nc, pool, ident, ident_made)

            @block.vector
            def _(dve):
                done = [0]

                def link(ins):
                    done[0] += 1
                    ins.then_inc(chain, 1)
                    dve.wait_ge(chain, CREDIT + done[0])

                nc.vector.memset(i_raw[:], 0.0).then_inc(zeroed, 1)
                nc.vector.memset(ones[:], 1.0)
                for raw, bias, pre, sem in ((f_raw, f_bias, f_pre, f_loaded), (i_raw, i_bias, i_pre, i_loaded)):
                    dve.wait_ge(sem, CREDIT + 16 * 4)
                    nc.vector.tensor_scalar_add(pre[fwd, :], raw[fwd, :], bias[fwd, :])
                    for s in seqs:
                        last = nc.vector.tensor_scalar_add(pre[bwd, s], raw[bwd, s][:, ::-1], bias[bwd, :])
                    link(last)
                dve.wait_ge(acts, CREDIT + 3)
                link(nc.vector.scalar_tensor_tensor(out=soft[:], in0=f_pre[:], scalar=0.0, in1=soft[:],
                                                    op0=ALU.min, op1=ALU.subtract))
                for s in seqs:
                    last = nc.vector.tensor_tensor_scan(out=cum[:, s], data0=ones[:, s], data1=soft[:, s], initial=0.0,
                                                        op0=ALU.mult, op1=ALU.add)
                link(last)
                link(nc.vector.tensor_sub(a_run[:], i_pre[:], cum[:]))
                for s in seqs:
                    last = nc.vector.tensor_tensor_scan(out=m_run[:, s], data0=a_run[:, s], data1=a_run[:, s],
                                                        initial=0.0, op0=ALU.max, op1=ALU.max)
                link(last)
                link(nc.vector.tensor_add(shift[:], cum[:], m_run[:]))
                nc.vector.tensor_scalar_mul(m_out[fwd, :], m_run[fwd, :], -1.0).then_inc(m_final, 1)
                for s in seqs:
                    nc.vector.tensor_scalar_mul(m_out[bwd, s], m_run[bwd, s][:, ::-1], -1.0).then_inc(m_final, 1)
                for b in range(2):
                    dve.wait_ge(flipped, CREDIT + b + 1)
                    for d, r in ((0, HALF), (1, 0)):
                        nc.vector.tensor_copy(cols[:, :, d, b * TT // 2:(b + 1) * TT // 2],
                                              flip[b][:, :, r:r + HM].rearrange("p t h -> p h t"))\
                            .then_inc(cols_made, 1)

            @block.scalar
            def _(act):
                act.wait_ge(chain, CREDIT + 1)
                nc.scalar.activation(soft[:], f_pre[:], ACT.Abs).then_inc(acts, 1)
                act.wait_ge(acts, CREDIT + 1)
                nc.scalar.activation(soft[:], soft[:], ACT.Exp, scale=-1.0).then_inc(acts, 1)
                act.wait_ge(acts, CREDIT + 2)
                nc.scalar.activation(soft[:], soft[:], ACT.Ln, bias=1.0).then_inc(acts, 1)
                act.wait_ge(chain, CREDIT + 5)
                nc.scalar.activation(a_out[fwd, :], a_run[fwd, :], ACT.Copy).then_inc(a_final, 1)
                for s in seqs:
                    nc.scalar.activation(a_out[bwd, s], a_run[bwd, s][:, ::-1], ACT.Copy).then_inc(a_final, 1)
                act.wait_ge(chain, CREDIT + 7)
                nc.scalar.activation(f_out[fwd, :], shift[fwd, :], ACT.Exp, scale=-1.0).then_inc(f_final, 1)
                for s in seqs:
                    nc.scalar.activation(f_out[bwd, s], shift[bwd, s][:, ::-1], ACT.Exp, scale=-1.0).then_inc(f_final, 1)

            @block.tensor
            def _(pe):
                pe.wait_ge(ident_made, CREDIT + 2)
                pe.wait_ge(a_final, CREDIT + 3)
                for b in range(2):
                    for t in range(TT // 2):
                        tok = (b * TT // 2 + t) * P
                        last = nc.tensor.transpose(flip[b][:, t, :], a_out[:, tok:tok + P], ident[0:rows, 0:rows])
                    last.then_inc(flipped, 1)


CHUNKS = [(0, 8, 0), (0, 8, 4), (8, 4, 8)]
BLK = CH // P
UNITS = sum(n for _, n, _ in CHUNKS)
FIRST = [sum(m for _, m, _ in CHUNKS[:c]) for c in range(NCH + 1)]


def units_of_head():
    return [(c, first + i, (first + i - own if own <= first + i < own + BLK else None), first + i < own)
            for c, (first, n, own) in enumerate(CHUNKS) for i in range(n)]


KQ_PIECES = [("k", 0), ("q", 0), ("k", 1), ("q", 1), ("k", 2), ("q", 2)]
NKQ = len(KQ_PIECES)
KQ_RING = 3
TICKS = UNITS


def head_plan():
    plan = {e: [] for e in ("sp", "pool", "act", "dve", "pe")}

    def at(engine, tick, kind, n):
        plan[engine].append((tick, kind, n))

    units = units_of_head()
    start = [2 + FIRST[c] for c in range(NCH)]
    end = [1 + FIRST[c + 1] for c in range(NCH)]
    for n, (c, s, j, _) in enumerate(units):
        score, value = 2 + n, VALUES_AFTER + n
        if j is not None:
            at("dve", score, "argument", n)
        at("act", score, "decay", n)
        at("pe", score, "scores", n)
        at("dve", score + 0.9, "weigh", n)
        at("pool", score + 1.3, "sum", n)
        at("dve", value - 1.3, "scale", n)
        at("act", value - 1.4, "high", n)
        at("pool" if j is None else "dve", value - 0.6, "low", n)
        at("pe", value, "values", n)
    for c in range(NCH):
        at("dve", start[c] - 1.5, "zero", c)
        for k, (engine, kind) in enumerate((("pe", "den"), ("act", "abs"), ("sp", "move"), ("dve", "invert"),
                                            ("sp", "keep"), ("sp", "spread"))):
            at(engine, end[c] + (2.4, 3.1, 3.1, 4.2, 4.3, 4.9)[k], kind, c)
        out = VALUES_AFTER + FIRST[c + 1] - 1 + 0.4
        at("dve", out, "gate", c)
        at("pool", out + 0.5, "gate", c)
        at("sp", out + 0.7, "store", c)
        at("sp", (19.5, out - 6.0, out - 2.1)[c], "load gates", c)
        at("sp", (-5.5, 2.5, 4.5)[c], "load nmax", c)
        at("sp", (3, 4, 7)[c], "load floor", c)
        at("act", (14.3, 16.8, 20.8)[c], "v high", c)
        at("pool", (14.3, 17.8, 21.8)[c], "v low", c)
        at("sp", (10.7, 14.7, 17.5)[c], "load v", c)
    for m in range(NKQ):
        tick = (0.7, 0.8, 2.3, 6.3, 11.3, 14.3)[m]
        at("act", tick, "kq high", m)
        at("dve", tick + 0.5, "kq low", m)
        at("sp", (-11.3, -6.5, -4.5, 1.5, 3.0, 5.1)[m], "load kq", m)
    return plan


VALUES_AFTER = 16.8


def mlstm(nc, p_feat, p_tok, neg_max, floor, a_cols, inverse, g_mem):
    with Scope(nc, "m") as sc:
        units, plan = units_of_head(), head_plan()
        own_no = {n: k for k, n in enumerate(n for n, u in enumerate(units) if u[2] is not None)}
        OWN = len(own_no)
        half = UNITS // 2
        raw_kq = [sc.sb(f"raw_kq{b}", [P, 2, CH]) for b in range(KQ_RING)]
        raw_v = sc.sb("raw_v", [P, BLK, DM])
        hi = {n: sc.sb(f"hi_{n}", [P, 2, T] if n != "v" else [P, TT, DM], F32R) for n in "qkv"}
        lo = {n: sc.sb(f"lo_{n}", [P, 2, T] if n != "v" else [P, TT, DM], F32R) for n in "qkv"}
        a_col = [sc.sb(f"a_col{c}", [P, NDIR, TT]) for c in range(NCH)]
        nmax = [sc.sb(f"nmax{c}", [P, NDIR, CH]) for c in range(NCH)]
        norm = [sc.sb(f"norm{c}", [P, NDIR, CH]) for c in range(NCH)]
        wsum = [sc.sb(f"wsum{c}", [P, NDIR, CH]) for c in range(NCH)]
        wbuf = sc.sb("wbuf", [P, UNITS, CH])
        wfwd = sc.sb("wfwd", [P, OWN, P])
        dec = [sc.sb(f"dec{b}", [P, BLK + 1, P]) for b in range(2)]
        arg = [sc.sb(f"arg{b}", [P, NDIR, P]) for b in range(2)]
        w_hi = [sc.sb(f"w_hi{b}", [P, CH], F32R) for b in range(2)]
        w_lo = [sc.sb(f"w_lo{b}", [P, CH], F32R) for b in range(2)]
        gate_o, gate_z, out_s = (sc.sb(n, [P, 2, CH]) for n in ("gate_o", "gate_z", "out_s"))
        mask = sc.sb("mask", [P, NDIR, P])
        ones = sc.sb("ones", [P, 1])
        den_row = sc.sb("den_row", [1, NDIR * CH])
        DC = NDIR * CH // P
        den_col = sc.sb("den_col", [P, DC])
        floor_col = [sc.sb(f"floor_col{c}", [P, DC]) for c in range(NCH)]
        scr = [sc.pb(f"scr{b}", [P, CH]) for b in range(4)]
        den = sc.pb("den", [1, NDIR, CH])
        hout = sc.pb("hout", [P, 2, CH])

        mask_made, ones_made = sc.sem("mask_made"), sc.sem("ones_made")
        kq_loaded = sc.sems("kq_loaded", KQ_RING)
        v_loaded = sc.sem("v_loaded")
        nmax_loaded = sc.sems("nmax_loaded", NCH)
        gates_loaded = sc.sem("gates_loaded")
        kq_hi, kq_lo, v_hi, v_lo = (sc.sem(n) for n in ("kq_hi", "kq_lo", "v_hi", "v_lo"))
        scored = sc.sem("scored")
        arg_made = sc.sem("arg_made")
        dec_made = sc.sems("dec_made", 2)
        weighed = sc.sems("weighed", 4)
        wsum_zeroed = sc.sem("wsum_zeroed")
        wsum_step = sc.sem("wsum_step")
        den_full, abs_made, den_moved = (sc.sem(n) for n in ("den_full", "abs_made", "den_moved"))
        floor_loaded = sc.sems("floor_loaded", NCH)
        max_made, inv_made, inv_stored = sc.sem("max_made"), sc.sem("inv_made"), sc.sem("inv_stored")
        norm_spread = sc.sems("norm_spread", NCH)
        scaled_part, scaled = sc.sem("scaled_part"), sc.sem("scaled")
        whi_made, wlo_made = sc.sems("whi_made", 2), sc.sems("wlo_made", 2)
        valued = sc.sems("valued", 2)
        out_read, out_made, out_stored = sc.sem("out_read"), sc.sem("out_made"), sc.sem("out_stored")

        wsum_count, n_w = {}, 0
        for n, (_, _, j, _) in enumerate(units):
            n_w += 1 if j is None else (3 if j < BLK - 1 else 2)
            wsum_count[n] = n_w
        WS = n_w

        def once_more(h):
            return not (isinstance(h, int) and h == 0)

        def piece(n, pc):
            return (slice(None), slice(None), slice(pc * CH, (pc + 1) * CH)) if n != "v" else \
                (slice(None), slice(pc * BLK, (pc + 1) * BLK), slice(None))

        def feat(row, h, c):
            v = p_feat[bass.ds(h * DM + row, DM), c * CH:(c + 1) * CH]
            return v.rearrange("(b p) t -> p b t", p=P)

        nc.all_engine_barrier()
        with nc.Block() as block:

            @block.sync
            def _(sp):
                def step(kind, c, h):
                    t = slice(c * CH, (c + 1) * CH)
                    if kind == "load kq":
                        m, (name, pc) = c, KQ_PIECES[c]
                        if m >= KQ_RING:
                            sp.wait_ge(kq_lo, CREDIT + h * NKQ + m - KQ_RING + 1)
                        elif once_more(h):
                            sp.wait_ge(kq_lo, CREDIT + h * NKQ + m - KQ_RING + 1)
                        sp.dma_start(raw_kq[m % KQ_RING][:], feat(R_QM + (W_M if name == "k" else 0), h, pc))\
                            .then_inc(kq_loaded[m % KQ_RING], 16)
                    elif kind == "load v":
                        v = p_tok[t, bass.ds(h * DM + S_VM, DM)].rearrange("(b p) c -> p b c", p=P)
                        sp.wait_ge(v_lo, CREDIT + h * NCH + c)
                        sp.dma_start(raw_v[:], v).then_inc(v_loaded, 16)
                    elif kind == "load nmax":
                        if once_more(h):
                            for q in range(2):
                                sp.wait_ge(dec_made[q], CREDIT + h * half - half + FIRST[c + 1] // 2)
                        sp.dma_start(nmax[c][:], neg_max[bass.ds(h, 1), :, t].to_broadcast([P, NDIR, CH]))\
                            .then_inc(nmax_loaded[c], 16)
                        sp.dma_start(a_col[c][:], a_cols[bass.ds(h, 1)].rearrange("o p d t -> (o p) d t"))\
                            .then_inc(nmax_loaded[c], 16)
                    elif kind == "load floor":
                        if once_more(h):
                            sp.wait_ge(max_made, CREDIT + h * NCH - NCH + c + 1)
                        for d in range(NDIR):
                            v = floor[bass.ds(h, 1), d, t].rearrange("o (p k) -> (o p) k", k=DC)
                            sp.dma_start(floor_col[c][d * CH // DC:(d + 1) * CH // DC, :], v)\
                                .then_inc(floor_loaded[c], 16)
                    elif kind == "load gates":
                        sp.wait_ge(out_made, CREDIT + h * NCH + c)
                        sp.dma_start(gate_o[:], feat(R_OM, h, c)).then_inc(gates_loaded, 16)
                        sp.dma_start(gate_z[:], feat(R_ZM, h, c)).then_inc(gates_loaded, 16)
                    elif kind == "store":
                        sp.wait_ge(out_made, CREDIT + h * NCH + c + 1)
                        v = g_mem[bass.ds(h * DM, DM), t].rearrange("(b p) t -> p b t", p=P)
                        sp.dma_start(v, out_s[:]).then_inc(out_stored, 16)
                    elif kind == "move":
                        sp.wait_ge(abs_made, CREDIT + h * NCH + c + 1)
                        sp.wait_ge(inv_stored, CREDIT + 16 * (h * NCH + c))
                        sp.dma_start(den_col[:], den_row[:].rearrange("o (p k) -> o p k", k=DC))\
                            .then_inc(den_moved, 16)
                    elif kind == "keep":
                        sp.wait_ge(inv_made, CREDIT + h * NCH + c + 1)
                        if c:
                            sp.wait_ge(norm_spread[c - 1], CREDIT + h * 16 + 16)
                        elif once_more(h):
                            sp.wait_ge(norm_spread[NCH - 1], CREDIT + h * 16)
                        sp.dma_start(inverse.rearrange("(p k) -> p k", k=DC), den_col[:]).then_inc(inv_stored, 16)
                    elif kind == "spread":
                        sp.wait_ge(inv_stored, CREDIT + 16 * (h * NCH + c + 1))
                        if once_more(h):
                            sp.wait_ge(scaled, CREDIT + h * UNITS - (UNITS - FIRST[1] if c == 0 else 0))
                        sp.dma_start(norm[c][:].rearrange("p d t -> p (d t)"),
                                     inverse.rearrange("(o n) -> o n", o=1).to_broadcast([P, NDIR * CH]))\
                            .then_inc(norm_spread[c], 16)

                over_turns(sp, plan["sp"], step, HM, TICKS)
                sp.wait_ge(out_stored, CREDIT + 16 * HM * NCH)

            @block.gpsimd
            def _(pool):
                nc.gpsimd.memset(ones[:], 1.0).then_inc(ones_made, 1)
                nc.gpsimd.memset(mask[:], 0.0).then_inc(mask_made, 1)
                pool.wait_ge(mask_made, CREDIT + 1)
                for d, sign in ((0, 1), (1, -1)):
                    nc.gpsimd.affine_select(out=mask[:, d, :], in_=mask[:, d, :], compare_op=ALU.is_ge, fill=-1e30,
                                            base=0, pattern=[[-sign, P]], channel_multiplier=sign)\
                        .then_inc(mask_made, 1)

                def step(kind, n, h):
                    if kind == "v low":
                        pool.wait_ge(v_hi, CREDIT + h * NCH + n + 1)
                        cut = piece("v", n)
                        nc.gpsimd.tensor_sub(lo["v"][cut], raw_v[:], hi["v"][cut].bitcast(F32)).then_inc(v_lo, 1)
                    elif kind == "sum":
                        c, s, j, fwd = units[n]
                        if n in FIRST:
                            pool.wait_ge(wsum_zeroed, CREDIT + h * NCH + c + 1)
                        pool.wait_ge(weighed[n % 4], CREDIT + h * (UNITS // 4) + n // 4 + 1)
                        if j is None:
                            parts = [(int(fwd), slice(0, CH), wbuf[:, n, :])]
                        else:
                            own, past = slice(j * P, (j + 1) * P), (j + 1) * P
                            parts = [(0, slice(0, past), wbuf[:, n, 0:past]), (1, own, wfwd[:, own_no[n], :])]
                            if past < CH:
                                parts.append((1, slice(past, CH), wbuf[:, n, past:CH]))
                        pool.wait_ge(wsum_step, CREDIT + h * WS + wsum_count[n] - len(parts))
                        for d, dst, src in parts:
                            nc.gpsimd.tensor_add(wsum[c][:, d, dst], wsum[c][:, d, dst], src).then_inc(wsum_step, 1)
                    elif kind == "low":
                        par = n % 2
                        pool.wait_ge(whi_made[par], CREDIT + h * half + n // 2 + 1)
                        pool.wait_ge(valued[par], CREDIT + h * half + n // 2)
                        nc.gpsimd.tensor_sub(w_lo[par][:], wbuf[:, n, :], w_hi[par][:].bitcast(F32))\
                            .then_inc(wlo_made[par], 1)
                    elif kind == "gate":
                        pool.wait_ge(out_read, CREDIT + h * NCH + n + 1)
                        nc.gpsimd.tensor_mul(out_s[:], out_s[:], gate_z[:]).then_inc(out_made, 1)

                over_turns(pool, plan["pool"], step, HM, TICKS)

            @block.scalar
            def _(act):
                def step(kind, n, h):
                    if kind == "kq high":
                        name, pc = KQ_PIECES[n]
                        act.wait_ge(kq_loaded[n % KQ_RING], CREDIT + h * 32 + n // KQ_RING * 16 + 16)
                        if once_more(h):
                            act.wait_ge(scored, CREDIT + h * UNITS - (UNITS - FIRST[2] if pc < 2 else 0))
                        nc.scalar.activation(hi[name][piece(name, pc)], raw_kq[n % KQ_RING][:], ACT.Copy)\
                            .then_inc(kq_hi, 1)
                    elif kind == "v high":
                        act.wait_ge(v_loaded, CREDIT + 16 * (h * NCH + n + 1))
                        if once_more(h):
                            for q in range(2):
                                act.wait_ge(valued[q], CREDIT + h * half - (half - FIRST[2] // 2 if n < 2 else 0))
                        nc.scalar.activation(hi["v"][piece("v", n)], raw_v[:], ACT.Copy).then_inc(v_hi, 1)
                    elif kind == "decay":
                        c, s, j, fwd = units[n]
                        par = n % 2
                        if n in FIRST:
                            act.wait_ge(nmax_loaded[c], CREDIT + h * 32 + 32)
                        if n >= 2 or once_more(h):
                            act.wait_ge(weighed[(n - 2) % 4], CREDIT + h * (UNITS // 4) + (n - 2) // 4 + 1)
                        flat = dec[par][:].rearrange("p b t -> p (b t)")
                        col = a_col[c][:, :, s:s + 1]
                        todo = []
                        if j is None:
                            d = int(fwd)
                            todo.append((flat[:, 0:CH], nmax[c][:, d, :], col[:, d]))
                        else:
                            if j:
                                todo.append((flat[:, 0:j * P], nmax[c][:, 0, 0:j * P], col[:, 0]))
                            if j < BLK - 1:
                                x = slice((j + 1) * P, CH)
                                todo.append((flat[:, x], nmax[c][:, 1, x], col[:, 1]))
                            todo.append((dec[par][:, j::BLK - j, :], arg[par][:], 0.0))
                        for m, (dst, src, bias) in enumerate(todo):
                            if j is not None and m == len(todo) - 1:
                                act.wait_ge(arg_made, CREDIT + h * OWN + own_no[n] + 1)
                            ins = nc.scalar.activation(dst, src, ACT.Exp, bias=bias)
                        ins.then_inc(dec_made[par], 1)
                    elif kind == "abs":
                        act.wait_ge(den_full, CREDIT + h * NCH + n + 1)
                        act.wait_ge(den_moved, CREDIT + 16 * (h * NCH + n))
                        nc.scalar.activation(den_row[:], den[:].rearrange("o d t -> o (d t)"), ACT.Abs)\
                            .then_inc(abs_made, 1)
                    elif kind == "high":
                        par = n % 2
                        act.wait_ge(valued[par], CREDIT + h * half + n // 2)
                        act.wait_ge(scaled, CREDIT + h * UNITS + n + 1)
                        nc.scalar.activation(w_hi[par][:], wbuf[:, n, :], ACT.Copy).then_inc(whi_made[par], 1)

                over_turns(act, plan["act"], step, HM, TICKS)

            @block.vector
            def _(dve):
                def step(kind, n, h):
                    if kind == "kq low":
                        name, pc = KQ_PIECES[n]
                        dve.wait_ge(kq_hi, CREDIT + h * NKQ + n + 1)
                        cut = piece(name, pc)
                        nc.vector.tensor_sub(lo[name][cut], raw_kq[n % KQ_RING][:], hi[name][cut].bitcast(F32))\
                            .then_inc(kq_lo, 1)
                    elif kind == "zero":
                        if once_more(h):
                            dve.wait_ge(den_full, CREDIT + h * NCH - NCH + n + 1)
                        nc.vector.memset(wsum[n][:], 0.0).then_inc(wsum_zeroed, 1)
                    elif kind == "argument":
                        c, s, j, fwd = units[n]
                        par = n % 2
                        dve.wait_ge(nmax_loaded[c], CREDIT + h * 32 + 32)
                        if n >= 2 or once_more(h):
                            dve.wait_ge(dec_made[par], CREDIT + h * half + n // 2)
                        for d in range(NDIR):
                            ins = nc.vector.scalar_tensor_tensor(
                                out=arg[par][:, d, :], in0=nmax[c][:, d, j * P:(j + 1) * P],
                                scalar=a_col[c][:, d, s:s + 1], in1=mask[:, d, :], op0=ALU.add, op1=ALU.min)
                        ins.then_inc(arg_made, 1)
                    elif kind == "weigh":
                        c, s, j, fwd = units[n]
                        par = n % 2
                        if once_more(h):
                            dve.wait_ge(wlo_made[par], CREDIT + h * half - half + n // 2 + 1)
                        dve.wait_ge(scored, CREDIT + h * UNITS + n + 1)
                        dve.wait_ge(dec_made[par], CREDIT + h * half + n // 2 + 1)
                        flat = dec[par][:].rearrange("p b t -> p (b t)")
                        ins = nc.vector.scalar_tensor_tensor(
                            out=wbuf[:, n, :], in0=scr[n % 4][:], scalar=DM ** -0.5, in1=flat[:, 0:CH],
                            op0=ALU.mult, op1=ALU.mult)
                        if j is not None:
                            ins = nc.vector.scalar_tensor_tensor(
                                out=wfwd[:, own_no[n], :], in0=scr[n % 4][:, j * P:(j + 1) * P], scalar=DM ** -0.5,
                                in1=flat[:, CH:], op0=ALU.mult, op1=ALU.mult)
                        ins.then_inc(weighed[n % 4], 1)
                    elif kind == "invert":
                        dve.wait_ge(den_moved, CREDIT + 16 * (h * NCH + n + 1))
                        dve.wait_ge(floor_loaded[n], CREDIT + 32 * h + 32)
                        nc.vector.tensor_max(den_col[:], den_col[:], floor_col[n][:]).then_inc(max_made, 1)
                        dve.wait_ge(max_made, CREDIT + h * NCH + n + 1)
                        nc.vector.reciprocal(den_col[:], den_col[:]).then_inc(inv_made, 1)
                    elif kind == "scale":
                        c, s, j, fwd = units[n]
                        if n in FIRST:
                            dve.wait_ge(norm_spread[c], CREDIT + 16 * h + 16)
                        dve.wait_ge(wsum_step, CREDIT + h * WS + wsum_count[n])
                        w = wbuf[:, n, :]
                        if j is None:
                            nc.vector.tensor_mul(w, w, norm[c][:, int(fwd), :]).then_inc(scaled, 1)
                        else:
                            own, past = slice(j * P, (j + 1) * P), (j + 1) * P
                            fw = wfwd[:, own_no[n], :]
                            if past < CH:
                                nc.vector.tensor_mul(w[:, past:CH], w[:, past:CH], norm[c][:, 1, past:CH])
                            nc.vector.tensor_mul(w[:, 0:past], w[:, 0:past], norm[c][:, 0, 0:past])
                            nc.vector.tensor_mul(fw, fw, norm[c][:, 1, own]).then_inc(scaled_part, 1)
                            dve.wait_ge(scaled_part, CREDIT + h * OWN + own_no[n] + 1)
                            nc.vector.tensor_add(w[:, own], w[:, own], fw).then_inc(scaled, 1)
                    elif kind == "low":
                        par = n % 2
                        dve.wait_ge(whi_made[par], CREDIT + h * half + n // 2 + 1)
                        dve.wait_ge(valued[par], CREDIT + h * half + n // 2)
                        nc.vector.tensor_sub(w_lo[par][:], wbuf[:, n, :], w_hi[par][:].bitcast(F32))\
                            .then_inc(wlo_made[par], 1)
                    elif kind == "gate":
                        dve.wait_ge(valued[1], CREDIT + h * half + FIRST[n + 1] // 2)
                        dve.wait_ge(gates_loaded, CREDIT + 32 * (h * NCH + n + 1))
                        dve.wait_ge(out_stored, CREDIT + 16 * (h * NCH + n))
                        nc.vector.tensor_mul(out_s[:], hout[:], gate_o[:]).then_inc(out_read, 1)

                dve.wait_ge(mask_made, CREDIT + 3)
                over_turns(dve, plan["dve"], step, HM, TICKS)

            @block.tensor
            def _(pe):
                def kq_before(c, s):
                    return {0: 2 if s < BLK else 3, 1: 4, 2: 6}[c]

                def step(kind, n, h):
                    if kind == "scores":
                        c, s, j, fwd = units[n]
                        t, src = slice(c * CH, (c + 1) * CH), slice(s * P, (s + 1) * P)
                        pe.wait_ge(kq_lo, CREDIT + h * NKQ + kq_before(c, s))
                        pe.wait_ge(weighed[n % 4], CREDIT + h * (UNITS // 4) + n // 4)
                        for d in range(2):
                            nc.tensor.matmul(scr[n % 4][:], hi["k"][:, d, src], hi["q"][:, d, t], start=(d == 0), stop=False)
                            nc.tensor.matmul(scr[n % 4][:], hi["k"][:, d, src], lo["q"][:, d, t], start=False, stop=False)
                            ins = nc.tensor.matmul(scr[n % 4][:], lo["k"][:, d, src], hi["q"][:, d, t], start=False, stop=(d == 1))
                        ins.then_inc(scored, 1)
                    elif kind == "den":
                        pe.wait_ge(wsum_step, CREDIT + h * WS + wsum_count[FIRST[n + 1] - 1])
                        pe.wait_ge(abs_made, CREDIT + h * NCH + n)
                        for d in range(NDIR):
                            ins = nc.tensor.matmul(den[:, d, :], ones[:], wsum[n][:, d, :], start=True, stop=True)
                        ins.then_inc(den_full, 1)
                    elif kind == "values":
                        c, s, j, fwd = units[n]
                        par = n % 2
                        first, last = n == FIRST[c], n == FIRST[c + 1] - 1
                        if first:
                            pe.wait_ge(out_read, CREDIT + h * NCH + c)
                        pe.wait_ge(v_lo, CREDIT + h * NCH + s // BLK + 1)
                        pe.wait_ge(wlo_made[par], CREDIT + h * half + n // 2 + 1)
                        for d in range(2):
                            f = slice(d * P, (d + 1) * P)
                            nc.tensor.matmul(hout[:, d, :], hi["v"][:, s, f], w_hi[par][:], start=first, stop=False)
                            nc.tensor.matmul(hout[:, d, :], hi["v"][:, s, f], w_lo[par][:], start=False, stop=False)
                            ins = nc.tensor.matmul(hout[:, d, :], lo["v"][:, s, f], w_hi[par][:], start=False, stop=last)
                        ins.then_inc(valued[par], 1)

                pe.wait_ge(ones_made, CREDIT + 1)
                over_turns(pe, plan["pe"], step, HM, TICKS)


QK = HA + KVA
NST = HA + 2 * KVA


def rotation_plan():
    plan = {e: [] for e in ("sp", "pool", "act", "dve", "pe")}
    for j in range(BLK):
        for engine, tick, kind in (
                ("sp", -0.7, "load"), ("dve", 0.0, "tables"), ("act", 0.0, "square"), ("dve", 0.15, "sum squares"),
                ("act", 0.3, "root"), ("dve", 0.35, "cosine"), ("dve", 0.55, "invert"), ("pool", 0.3, "sine"),
                ("dve", 0.45, "add"), ("pool", 0.85, "normalise"), ("act", 1.1, "high"), ("dve", 1.3, "low"),
                ("pe", 1.5, "transpose"), ("act", 1.6, "empty"), ("dve", 1.8, "empty"), ("sp", 2.0, "store")):
            plan[engine].append((tick + j, kind, j))
    for n in range(2 * CB):
        plan["pe"].append((PRODUCT_AT + n / 2, "product", n))
        plan["dve"].append((PRODUCT_AT + n / 2 + 0.5, "gate", n))
    for slot in range(2):
        done = PRODUCT_AT + 2 * slot + 2
        plan["act"].append((done + 0.6, "store part", slot))
        plan["sp"].append((done + 0.9 - 2 * CB / 2, "load gate", slot))
    for i in range(ACT_PCS):
        plan["sp"].append((-1.0, "load piece", i))
        plan["act"].append((PRODUCT_AT - 0.2, "piece high", i))
        plan["dve" if i % 2 else "pool"].append((PRODUCT_AT - 0.15, "piece low", i))
    return plan


PRODUCT_AT = -0.2
ACT_PCS = KT // 2


def rotate(nc, p_tok, rope, q_gain, k_gain, stacks, v_stacks, p_feat, g_mem, w_mo, part):
    with Scope(nc, "r") as sc:
        x = [sc.sb(f"x{b}", [P, QK + KVA, DA]) for b in range(2)]
        trig = [sc.sb(f"trig{b}", [P, 2, DA]) for b in range(2)]
        sq = [sc.sb(f"sq{b}", [P, QK, DA]) for b in range(2)]
        turn = [sc.sb(f"turn{b}", [P, QK, DA]) for b in range(2)]
        stat = [sc.sb(f"stat{b}", [P, 3, QK]) for b in range(2)]
        tab = [sc.sb(f"tab{b}", [P, 2, 2, DA]) for b in range(2)]
        st = [sc.sb(f"st{b}", [P, NST, 2, DA]) for b in range(2)]
        vst = [sc.sb(f"vst{b}", [P, KVA, 2, DA]) for b in range(2)]
        flat = sc.sb("flat", [P, NST, P])
        gain = sc.sb("gain", [P, 2, 2, DA])
        ident = sc.sb("ident", [P, P])
        BANKS, BY_ACT = NST // 4, NST // 4 - 2
        flip = [sc.pb(f"flip{i}", [P, 4, P]) for i in range(BANKS)]
        w_hi = sc.sb("w_hi", [P, 2, KT, UNIT], F32R)
        w_lo = sc.sb("w_lo", [P, 2, KT, UNIT], F32R)
        act_hi = sc.sb("act_hi", [P, KT, CH], F32R)
        act_lo = sc.sb("act_lo", [P, KT, CH], F32R)
        raw = [sc.sb(f"raw{b}", [P, 2, CH]) for b in range(ACT_PCS)]
        stage = sc.sb("stage", [P, 2, CB, CH])
        acc = [sc.pb(f"acc{b}", [P, CH]) for b in range(2)]
        raw_loaded, piece_hi = sc.sems("raw_loaded", ACT_PCS), sc.sem("piece_hi")
        piece_lo = sc.sems("piece_lo", ACT_PCS)
        acc_full = sc.sem("acc_full")
        evacuated = sc.sems("evacuated", 2)
        gate_loaded, part_stored = sc.sems("gate_loaded", 2), sc.sems("part_stored", 2)
        starts = [p for i in range(ACT_PCS) for p in (("w", 0, i), ("a", 0, i))] + [("w", 1, i) for i in range(ACT_PCS)]
        NSTART = len(starts)
        pool_lo = [n for n, p in enumerate(starts) if p[:2] == ("w", 0)]

        def piece_cut(kind, slot, i, w, a):
            return w[:, slot, 2 * i:2 * i + 2, :] if kind == "w" else a[:, 2 * i:2 * i + 2, :]

        def piece_source(kind, slot, i):
            v = w_mo[:, slot * UNIT:(slot + 1) * UNIT] if kind == "w" else g_mem[:, 0:CH]
            return v[2 * i * P:(2 * i + 2) * P, :].rearrange("(b p) t -> p b t", p=P)

        def pieces_before(c):
            return c + NSTART // ACT_PCS - 1

        ident_made, gain_loaded, gain_step = sc.sem("ident_made"), sc.sem("gain_loaded"), sc.sem("gain_step")
        loaded = sc.sems("loaded", 2)
        squared, summed, eps_added, rooted, rstd_made = (sc.sem(n) for n in (
            "squared", "summed", "eps_added", "rooted", "rstd_made"))
        tab_made, cos_made, sin_made, turned, normed = (sc.sem(n) for n in (
            "tab_made", "cos_made", "sin_made", "turned", "normed"))
        hi_made, stacked, doubled = sc.sem("hi_made"), sc.sem("stacked"), sc.sem("doubled")
        flipped = sc.sems("flipped", BANKS)
        emptied = sc.sems("emptied", BANKS)
        stored = sc.sems("stored", 2)
        halves = "p h (a b c) -> p h a b c"
        plan = rotation_plan()
        q_and_k = ((0, slice(0, HA)), (1, slice(HA, QK)))

        def at_start(i):
            return isinstance(i, int) and i == 0

        nc.all_engine_barrier()
        with nc.Block() as block:

            @block.sync
            def _(sp):
                for n, src in enumerate((q_gain, k_gain)):
                    sp.dma_start(gain[:, n, 0, :], src.to_broadcast([P, DA])).then_inc(gain_loaded, 16)

                def step(kind, j, c):
                    b, t, i = j % 2, c * BLK + j, c * (BLK // 2) + j // 2
                    rows = bass.ds(c * (BLK * P) + j * P, P)
                    if kind == "load":
                        if not at_start(i):
                            sp.wait_ge(stacked, CREDIT + 3 * t - 3)
                        sp.dma_start(x[b][:], p_tok[rows, S_QA:S_VM].rearrange("p (h d) -> p h d", d=DA))\
                            .then_inc(loaded[b], 16)
                        sp.dma_start(trig[b][:], rope[rows].rearrange("p (s d) -> p s d", d=DA)).then_inc(loaded[b], 16)
                    elif kind == "store":
                        sp.wait_ge(emptied[BY_ACT - 1], CREDIT + t + 1)
                        sp.wait_ge(emptied[BANKS - 1], CREDIT + t + 1)
                        sp.dma_start(stacks[:, :, rows].rearrange("n p t -> p n t"), flat[:]).then_inc(stored[b], 16)
                        sp.dma_start(v_stacks[rows], vst[b][:].rearrange("p h s d -> p h (s d)")).then_inc(stored[b], 16)
                    elif kind == "load piece":
                        if not at_start(c):
                            v = g_mem[2 * j * P:(2 * j + 2) * P, bass.ds(c * CH, CH)].rearrange("(b p) t -> p b t", p=P)
                            sp.wait_ge(piece_lo[j], CREDIT + pieces_before(c))
                            sp.dma_start(raw[j][:], v).then_inc(raw_loaded[j], 16)
                    elif kind == "load gate":
                        row = R_GM + j * UNIT
                        sp.wait_ge(part_stored[j], CREDIT + 16 * c)
                        sp.dma_start(stage[:, j], p_feat[row:row + UNIT, bass.ds(c * CH, CH)]
                                     .rearrange("(b p) t -> p b t", p=P)).then_inc(gate_loaded[j], 16)

                over_turns(sp, plan["sp"], step, NCH, BLK)
                for b in range(2):
                    sp.wait_ge(stored[b], CREDIT + 32 * (TT // 2))
                    sp.wait_ge(part_stored[b], CREDIT + 16 * NCH)

            @block.gpsimd
            def _(pool):
                make_identity(nc, pool, ident, ident_made)
                for n in pool_lo:
                    pool.wait_ge(piece_hi, CREDIT + n + 1)
                    nc.gpsimd.tensor_sub(piece_cut(*starts[n], w_lo, act_lo), raw[n % ACT_PCS][:],
                                         piece_cut(*starts[n], w_hi, act_hi).bitcast(F32)).then_inc(piece_lo[n % ACT_PCS], 1)
                pool.wait_ge(gain_loaded, CREDIT + 32)
                for n in range(2):
                    g_in = gain[:, n, 0, :].rearrange("p (a b c) -> p a b c", a=2, b=2)
                    g_out = gain[:, n, 1, :].rearrange("p (a b c) -> p a b c", a=2, b=2)
                    for h in range(2):
                        nc.gpsimd.tensor_copy(g_out[:, :, h, :], g_in[:, :, 1 - h, :]).then_inc(gain_step, 1)

                def step(kind, j, c):
                    b, t, i = j % 2, c * BLK + j, c * (BLK // 2) + j // 2
                    if kind == "sine":
                        pool.wait_ge(tab_made, CREDIT + 4 * t + 4)
                        pool.wait_ge(squared, CREDIT + t + 1)
                        pool.wait_ge(summed, CREDIT + t + 1)
                        xv, sv = x[b][:, 0:QK, :].rearrange(halves, a=2, b=2), sq[b][:].rearrange(halves, a=2, b=2)
                        for n, heads in q_and_k:
                            m = heads.stop - heads.start
                            tv = tab[b][:, n:n + 1, 1, :].rearrange(halves, a=2, b=2)
                            for h in range(2):
                                nc.gpsimd.tensor_mul(sv[:, heads, :, h, :], xv[:, heads, :, 1 - h, :],
                                                     tv[:, :, :, h, :].to_broadcast([P, m, 2, DA // 4]))\
                                    .then_inc(sin_made, 1)
                    elif kind == "normalise":
                        pool.wait_ge(rstd_made, CREDIT + t + 1)
                        pool.wait_ge(turned, CREDIT + t + 1)
                        nc.gpsimd.tensor_mul(turn[b][:], turn[b][:],
                                             stat[b][:, 2, :].rearrange("p (h o) -> p h o", o=1).to_broadcast([P, QK, DA]))\
                            .then_inc(normed, 1)
                    elif kind == "piece low":
                        if not at_start(c):
                            pool.wait_ge(piece_hi, CREDIT + c * ACT_PCS + NSTART - ACT_PCS + j + 1)
                            cut = (slice(None), slice(2 * j, 2 * j + 2), slice(None))
                            nc.gpsimd.tensor_sub(act_lo[cut], raw[j][:], act_hi[cut].bitcast(F32))\
                                .then_inc(piece_lo[j], 1)

                over_turns(pool, plan["pool"], step, NCH, BLK)

            @block.vector
            def _(dve):
                for n, p in enumerate(starts):
                    if n not in pool_lo:
                        dve.wait_ge(piece_hi, CREDIT + n + 1)
                        nc.vector.tensor_sub(piece_cut(*p, w_lo, act_lo), raw[n % ACT_PCS][:],
                                             piece_cut(*p, w_hi, act_hi).bitcast(F32)).then_inc(piece_lo[n % ACT_PCS], 1)
                dve.wait_ge(gain_step, CREDIT + 4)

                def step(kind, j, c):
                    b, t, i = j % 2, c * BLK + j, c * (BLK // 2) + j // 2
                    if kind == "tables":
                        dve.wait_ge(loaded[b], CREDIT + 32 * (i + 1))
                        if not at_start(i):
                            dve.wait_ge(sin_made, CREDIT + 4 * t - 4)
                        for n, s in ((0, DA ** -0.5), (1, 1.0)):
                            for k in range(2):
                                nc.vector.scalar_tensor_tensor(out=tab[b][:, n, k, :], in0=trig[b][:, k, :], scalar=s,
                                                               in1=gain[:, n, k, :], op0=ALU.mult, op1=ALU.mult)\
                                    .then_inc(tab_made, 1)
                    elif kind == "sum squares":
                        dve.wait_ge(squared, CREDIT + t + 1)
                        nc.vector.tensor_reduce(out=stat[b][:, 0, :], in_=sq[b][:], axis=AX.X, op=ALU.add)\
                            .then_inc(summed, 1)
                        dve.wait_ge(summed, CREDIT + t + 1)
                        nc.vector.tensor_scalar(stat[b][:, 1, :], stat[b][:, 0, :], 1.0 / DA, EPS, ALU.mult, ALU.add)\
                            .then_inc(eps_added, 1)
                    elif kind == "cosine":
                        dve.wait_ge(tab_made, CREDIT + 4 * t + 4)
                        if not at_start(i):
                            dve.wait_ge(hi_made, CREDIT + 3 * t - 3)
                        for n, heads in q_and_k:
                            m = heads.stop - heads.start
                            nc.vector.tensor_mul(turn[b][:, heads, :], x[b][:, heads, :],
                                                 tab[b][:, n:n + 1, 0, :].to_broadcast([P, m, DA])).then_inc(cos_made, 1)
                    elif kind == "invert":
                        dve.wait_ge(rooted, CREDIT + t + 1)
                        nc.vector.reciprocal(stat[b][:, 2, :], stat[b][:, 1, :]).then_inc(rstd_made, 1)
                    elif kind == "add":
                        dve.wait_ge(cos_made, CREDIT + 2 * t + 2)
                        dve.wait_ge(sin_made, CREDIT + 4 * t + 4)
                        nc.vector.tensor_add(turn[b][:], turn[b][:], sq[b][:]).then_inc(turned, 1)
                    elif kind == "low":
                        dve.wait_ge(hi_made, CREDIT + 3 * t + 3)
                        nc.vector.tensor_sub(st[b][:, 0:HA, 1, :], turn[b][:, 0:HA, :], st[b][:, 0:HA, 0, :])\
                            .then_inc(stacked, 1)
                        nc.vector.tensor_sub(st[b][:, QK:NST, 0, :], turn[b][:, HA:QK, :], st[b][:, HA:QK, 0, :])\
                            .then_inc(stacked, 1)
                        nc.vector.tensor_sub(vst[b][:, :, 1, :], x[b][:, QK:, :], vst[b][:, :, 0, :]).then_inc(stacked, 1)
                        dve.wait_ge(stacked, CREDIT + 3 * t + 3)
                        nc.vector.tensor_copy(st[b][:, HA:NST, 1, :], st[b][:, HA:NST, 0, :]).then_inc(doubled, 1)
                    elif kind == "empty":
                        for f in range(BY_ACT, BANKS):
                            dve.wait_ge(flipped[f], CREDIT + t + 1)
                            if f == BY_ACT:
                                dve.wait_ge(stored[1 - b], CREDIT + 32 * i + (32 if b else 0))
                            nc.vector.tensor_copy(flat[:, 4 * f:4 * f + 4, :], flip[f][:]).then_inc(emptied[f], 1)
                    elif kind == "piece low":
                        if not at_start(c):
                            dve.wait_ge(piece_hi, CREDIT + c * ACT_PCS + NSTART - ACT_PCS + j + 1)
                            cut = (slice(None), slice(2 * j, 2 * j + 2), slice(None))
                            nc.vector.tensor_sub(act_lo[cut], raw[j][:], act_hi[cut].bitcast(F32))\
                                .then_inc(piece_lo[j], 1)
                    elif kind == "gate":
                        slot, m = j // CB, j % CB
                        dve.wait_ge(gate_loaded[slot], CREDIT + 16 * c + 16)
                        dve.wait_ge(acc_full, CREDIT + c * (2 * CB) + j + 1)
                        nc.vector.tensor_mul(stage[:, slot, m, :], stage[:, slot, m, :], acc[b][:]).then_inc(evacuated[b], 1)

                over_turns(dve, plan["dve"], step, NCH, BLK)

            @block.scalar
            def _(act):
                def load_start(n):
                    act.dma_start(raw[n % ACT_PCS][:], piece_source(*starts[n])).then_inc(raw_loaded[n % ACT_PCS], 16)

                for n in range(ACT_PCS):
                    load_start(n)
                for n, p in enumerate(starts):
                    act.wait_ge(raw_loaded[n % ACT_PCS], CREDIT + 16 * (n // ACT_PCS + 1))
                    nc.scalar.activation(piece_cut(*p, w_hi, act_hi), raw[n % ACT_PCS][:], ACT.Copy).then_inc(piece_hi, 1)
                    if 1 <= n <= NSTART - ACT_PCS:
                        act.wait_ge(piece_lo[(n - 1) % ACT_PCS], CREDIT + (n - 1) // ACT_PCS + 1)
                        load_start(n - 1 + ACT_PCS)

                def step(kind, j, c):
                    b, t, i = j % 2, c * BLK + j, c * (BLK // 2) + j // 2
                    if kind == "square":
                        act.wait_ge(loaded[b], CREDIT + 32 * (i + 1))
                        if not at_start(i):
                            act.wait_ge(turned, CREDIT + t - 1)
                        nc.scalar.activation(sq[b][:], x[b][:, 0:QK, :], ACT.Square).then_inc(squared, 1)
                    elif kind == "root":
                        act.wait_ge(eps_added, CREDIT + t + 1)
                        nc.scalar.activation(stat[b][:, 1, :], stat[b][:, 1, :], ACT.Sqrt).then_inc(rooted, 1)
                    elif kind == "high":
                        act.wait_ge(normed, CREDIT + t + 1)
                        if not at_start(i):
                            act.wait_ge(flipped[BANKS - 1], CREDIT + t - 1)
                        act.wait_ge(stored[b], CREDIT + 32 * i)
                        nc.scalar.activation(st[b][:, 0:HA, 0, :].bitcast(F32R), turn[b][:, 0:HA, :], ACT.Copy)\
                            .then_inc(hi_made, 1)
                        nc.scalar.activation(st[b][:, HA:QK, 0, :].bitcast(F32R), turn[b][:, HA:QK, :], ACT.Copy)\
                            .then_inc(hi_made, 1)
                        nc.scalar.activation(vst[b][:, :, 0, :].bitcast(F32R), x[b][:, QK:, :], ACT.Copy)\
                            .then_inc(hi_made, 1)
                    elif kind == "empty":
                        for f in range(BY_ACT):
                            act.wait_ge(flipped[f], CREDIT + t + 1)
                            if f == 0:
                                act.wait_ge(stored[1 - b], CREDIT + 32 * i + (32 if b else 0))
                            nc.scalar.activation(flat[:, 4 * f:4 * f + 4, :], flip[f][:], ACT.Copy)\
                                .then_inc(emptied[f], 1)
                    elif kind == "piece high":
                        if not at_start(c):
                            act.wait_ge(raw_loaded[j], CREDIT + pieces_before(c) * 16 + 16)
                            act.wait_ge(acc_full, CREDIT + c * (2 * CB))
                            nc.scalar.activation(act_hi[:, 2 * j:2 * j + 2, :], raw[j][:], ACT.Copy).then_inc(piece_hi, 1)
                    elif kind == "store part":
                        for q in range(2):
                            act.wait_ge(evacuated[q], CREDIT + c * CB + 2 * j + 2)
                        act.dma_start(part[j * UNIT:(j + 1) * UNIT, bass.ds(c * CH, CH)]
                                      .rearrange("(b p) t -> p b t", p=P), stage[:, j]).then_inc(part_stored[j], 16)

                over_turns(act, plan["act"], step, NCH, BLK)

            @block.tensor
            def _(pe):
                def step(kind, j, c):
                    b, t, i = j % 2, c * BLK + j, c * (BLK // 2) + j // 2
                    if kind == "product":
                        slot, m = j // CB, slice(j % CB * P, (j % CB + 1) * P)
                        pe.wait_ge(evacuated[b], CREDIT + c * CB + j // 2)

                        def before_k(k):
                            i = k // 2
                            if at_start(c):
                                for n, p in enumerate(starts):
                                    if p[2] == i and (j == 0 and p[1] == 0 or j == CB and p[1] == 1):
                                        pe.wait_ge(piece_lo[n % ACT_PCS], CREDIT + n // ACT_PCS + 1)
                            elif j == 0:
                                pe.wait_ge(piece_lo[i], CREDIT + pieces_before(c) + 1)

                        product(nc, pe, acc[b][:], lambda k: w_hi[:, slot, k, m], lambda k: w_lo[:, slot, k, m],
                                lambda k: act_hi[:, k, :], lambda k: act_lo[:, k, :], before_k).then_inc(acc_full, 1)
                        return
                    pe.wait_ge(doubled, CREDIT + t + 1)
                    pe.wait_ge(stacked, CREDIT + 3 * t + 3)
                    for f in range(BANKS):
                        pe.wait_ge(emptied[f], CREDIT + t)
                        for n in range(4):
                            src = st[b][:, 4 * f + n, :, :].rearrange("p s d -> p (s d)")
                            last = nc.tensor.transpose(flip[f][:, n, :], src, ident[:])
                        last.then_inc(flipped[f], 1)

                pe.wait_ge(ident_made, CREDIT + 2)
                over_turns(pe, plan["pe"], step, NCH, BLK)


NU = TT
HEADS_IT = 4
UIT = NU * HEADS_IT
NCI = HEADS_IT * NCH
FLIPS = 3
QUARTERS = 4


def keys_of(q_tile):
    at = 0
    for n in SEQS:
        if q_tile * P < at + n:
            return at // P, n // P
        at += n


def attention_units():
    units, groups = [], 0
    for hd in range(HEADS_IT):
        for q in range(NU):
            first, n = keys_of(q)
            units.append((hd, q, first, n, list(range(groups, groups + n // 4))))
            groups += n // 4
    return units, groups


def attention_plan():
    plan = {e: [] for e in ("sp", "pool", "act", "dve", "pe")}

    def at(engine, tick, kind, n):
        plan[engine].append((tick, kind, n))

    for m, (_, _, _, _, gs) in enumerate(attention_units()[0]):
        at("pe", m, "scores", m)
        at("dve", m + MAX_AT, "maximum", m)
        at("act", m + EXP_AT, "exponent", m)
        at("dve", m + INV_AT, "invert", m)
        at("pool", m + NORM_AT, "normalise", m)
        at("pe", m + FLIP_AT, "transpose", m)
        for i in range(len(gs)):
            at("act", m + HIGH_AT[i], "high", (m, i))
            at("dve", m + LOW_AT[i], "low", (m, i))
    for ci in range(NCI):
        done = 4 * ci + 3 + FLIP_AT
        for q in range(QUARTERS):
            at("pe", done + VALUE_AT + q, "values", (ci, q))
        at("act", done + FOLD_AT, "fold", ci)
        at("dve", done + ADD_AT, "add", ci)
        at("pool", done + GATE_AT, "gate", ci)
        at("sp", done + 7, "store", ci)
    half = UIT // 2
    for slot in range(2):
        at("sp", (slot - 1) * half + 1, "load q and k", slot)
        at("sp", (slot - 1) * half + FLIP_AT + 7, "load v and gate", slot)
    return plan


MAX_AT, EXP_AT, INV_AT, NORM_AT, FLIP_AT = 0.6, 1.05, 1.7, 2.0, 3.4
HIGH_AT, LOW_AT = (3.9, 3.95), (4.0, 4.05)
VALUE_AT, FOLD_AT, ADD_AT, GATE_AT = 2.0, 5.2, 5.4, 5.65


def attend(nc, p_feat, stacks, v_stacks, g_att):
    with Scope(nc, "t") as sc:
        units, groups = attention_units()
        plan = attention_plan()
        q_t = [sc.sb(f"q{s}", [P, 2, T], F32R) for s in range(2)]
        k_t = [sc.sb(f"k{s}", [P, 2, T], F32R) for s in range(2)]
        v_t = [sc.sb(f"v{s}", [P, TT, P], F32R) for s in range(2)]
        gate = [sc.sb(f"gate{s}", [DA, 2, T]) for s in range(2)]
        prob = [sc.sb(f"prob{r}", [P, SEQS[0]]) for r in range(3)]
        nmax, rsum = sc.sb("nmax", [P, 4]), sc.sb("rsum", [P, 2, 4])
        pt_hi = [sc.sb(f"pt_hi{b}", [P, SEQS[0] // P, CH], F32R) for b in range(2)]
        pt_lo = [sc.sb(f"pt_lo{b}", [P, SEQS[0] // P, CH], F32R) for b in range(2)]
        low = [sc.sb(f"low{b}", [DA, CH]) for b in range(2)]
        att = [sc.sb(f"att{b}", [DA, CH]) for b in range(2)]
        ident = sc.sb("ident", [P, P])
        scr = [sc.pb(f"scr{b}", [P, SEQS[0]]) for b in range(2)]
        flip = [sc.pb(f"flip{b}", [P, 4, P]) for b in range(FLIPS)]
        out = sc.pb("out", [P, CH])

        ident_made = sc.sem("ident_made")
        qk_loaded = sc.sems("qk_loaded", 2)
        vg_loaded = sc.sems("vg_loaded", 2)
        scored = sc.sem("scored")
        max_made = sc.sem("max_made")
        exp_made = sc.sems("exp_made", 2)
        inv_made = sc.sem("inv_made")
        normed = sc.sem("normed")
        flipped = sc.sems("flipped", 3)
        hi_made, lo_made = sc.sems("hi_made", FLIPS), sc.sems("lo_made", FLIPS)
        multiplied = sc.sem("multiplied")
        low_made = sc.sem("low_made")
        summed = sc.sem("summed")
        gated, stored = sc.sem("gated"), sc.sems("stored", 2)

        before, per_slot = [], [0, 0, 0]
        for m, u in enumerate(units):
            before.append(per_slot[m % 3])
            per_slot[m % 3] += len(u[4])

        per_bank = [len(range(b, groups, FLIPS)) for b in range(FLIPS)]

        def place(m, i):
            return (slice(None), slice(4 * i, 4 * i + 4), slice((m % 4) * P, (m % 4 + 1) * P))

        nc.all_engine_barrier()
        with nc.Block() as block:

            @block.sync
            def _(sp):
                def step(kind, n, g):
                    first = isinstance(g, int) and g == 0
                    if kind == "load q and k":
                        s = n
                        if not first:
                            sp.wait_ge(scored, CREDIT + g * UIT - (1 - s) * (UIT // 2))
                        hd = g * HEADS_IT + 2 * s
                        sp.dma_start(q_t[s][:].bitcast(F32), stacks[bass.ds(hd, 2)].rearrange("n p t -> p n t"))\
                            .then_inc(qk_loaded[s], 16)
                        for part in range(2):
                            sp.dma_start(k_t[s][:, part:part + 1, :].bitcast(F32),
                                         stacks[bass.ds(g + HA + part * KVA, 1)].rearrange("n p t -> p n t"))\
                                .then_inc(qk_loaded[s], 16)
                    elif kind == "load v and gate":
                        s = n
                        if not first:
                            sp.wait_ge(gated, CREDIT + g * NCI - (1 - s) * (NCI // 2))
                        v = v_stacks[:, bass.ds(g, 1), :].rearrange("(t p) o d -> p t (o d)", p=P)
                        sp.dma_start(v_t[s][:].bitcast(F32), v).then_inc(vg_loaded[s], 16)
                        rows = p_feat[bass.ds(g * (HEADS_IT * DA) + (R_ZA + 2 * s * DA), 2 * DA), :]
                        sp.dma_start(gate[s][:], rows.rearrange("(n p) t -> p n t", p=DA)).then_inc(vg_loaded[s], 16)
                    elif kind == "store":
                        hd, c = n // NCH, n % NCH
                        sp.wait_ge(gated, CREDIT + g * NCI + n + 1)
                        sp.dma_start(g_att[bass.ds(g * (HEADS_IT * DA) + hd * DA, DA), c * CH:(c + 1) * CH],
                                     att[n % 2][:]).then_inc(stored[n % 2], 16)

                over_turns(sp, plan["sp"], step, KVA, UIT)
                for b in range(2):
                    sp.wait_ge(stored[b], CREDIT + 16 * KVA * NCI // 2)

            @block.gpsimd
            def _(pool):
                make_identity(nc, pool, ident, ident_made)

                def step(kind, n, g):
                    if kind == "normalise":
                        w = units[n][3] * P
                        pool.wait_ge(inv_made, CREDIT + g * UIT + n + 1)
                        nc.gpsimd.tensor_mul(prob[n % 3][:, 0:w], prob[n % 3][:, 0:w],
                                             rsum[:, 1, n % 4:n % 4 + 1].to_broadcast([P, w])).then_inc(normed, 1)
                    elif kind == "gate":
                        hd, c = n // NCH, n % NCH
                        pool.wait_ge(summed, CREDIT + g * NCI + n + 1)
                        nc.gpsimd.tensor_mul(att[n % 2][:], att[n % 2][:],
                                             gate[hd // 2][:, hd % 2, c * CH:(c + 1) * CH]).then_inc(gated, 1)

                over_turns(pool, plan["pool"], step, KVA, UIT)

            @block.vector
            def _(dve):
                def step(kind, n, g):
                    if kind == "maximum":
                        w = units[n][3] * P
                        dve.wait_ge(scored, CREDIT + g * UIT + n + 1)
                        nc.vector.tensor_reduce(out=nmax[:, n % 4:n % 4 + 1], in_=scr[n % 2][:, 0:w], axis=AX.X,
                                                op=ALU.max, negate=True).then_inc(max_made, 1)
                    elif kind == "invert":
                        dve.wait_ge(exp_made[n % 2], CREDIT + g * (UIT // 2) + n // 2 + 1)
                        nc.vector.reciprocal(rsum[:, 1, n % 4:n % 4 + 1], rsum[:, 0, n % 4:n % 4 + 1])\
                            .then_inc(inv_made, 1)
                    elif kind == "low":
                        m, i = n
                        x, b = units[m][4][i], (m // 4) % 2
                        dve.wait_ge(hi_made[x % FLIPS], CREDIT + g * per_bank[x % FLIPS] + x // FLIPS + 1)
                        nc.vector.tensor_sub(pt_lo[b][place(m, i)], flip[x % FLIPS][:],
                                             pt_hi[b][place(m, i)].bitcast(F32)).then_inc(lo_made[x % FLIPS], 1)
                    elif kind == "add":
                        dve.wait_ge(low_made, CREDIT + g * NCI + n + 1)
                        dve.wait_ge(stored[n % 2], CREDIT + 16 * (g * (NCI // 2) + n // 2))
                        if n % (NCI // 2) == 0:
                            dve.wait_ge(vg_loaded[n // (NCI // 2)], CREDIT + 32 * (g + 1))
                        nc.vector.tensor_add(att[n % 2][:], out[0:DA, :], low[n % 2][:])\
                            .then_inc(summed, 1)

                over_turns(dve, plan["dve"], step, KVA, UIT)

            @block.scalar
            def _(act):
                def step(kind, n, g):
                    if kind == "exponent":
                        w = units[n][3] * P
                        act.wait_ge(max_made, CREDIT + g * UIT + n + 1)
                        act.wait_ge(flipped[n % 3], CREDIT + g * per_slot[n % 3] + before[n])
                        if n >= 3 or not (isinstance(g, int) and g == 0):
                            act.wait_ge(inv_made, CREDIT + g * UIT + n - 3)
                        nc.scalar.activation(prob[n % 3][:, 0:w], scr[n % 2][:, 0:w], ACT.Exp,
                                             bias=nmax[:, n % 4:n % 4 + 1], accum_out=rsum[:, 0, n % 4:n % 4 + 1])\
                            .then_inc(exp_made[n % 2], 1)
                    elif kind == "high":
                        m, i = n
                        x, ci = units[m][4][i], m // 4
                        if m % 4 == 0 and i == 0:
                            if ci >= 2 or not (isinstance(g, int) and g == 0):
                                act.wait_ge(multiplied, CREDIT + g * NCI + ci - 1)
                        act.wait_ge(flipped[m % 3], CREDIT + g * per_slot[m % 3] + before[m] + i + 1)
                        nc.scalar.activation(pt_hi[ci % 2][place(m, i)], flip[x % FLIPS][:], ACT.Copy)\
                            .then_inc(hi_made[x % FLIPS], 1)
                    elif kind == "fold":
                        act.wait_ge(multiplied, CREDIT + g * NCI + n + 1)
                        if n >= 2 or not (isinstance(g, int) and g == 0):
                            act.wait_ge(summed, CREDIT + g * NCI + n - 1)
                        nc.scalar.activation(low[n % 2][:], out[DA:P, :], ACT.Copy).then_inc(low_made, 1)

                over_turns(act, plan["act"], step, KVA, UIT)

            @block.tensor
            def _(pe):
                def step(kind, n, g):
                    if kind == "scores":
                        hd, q, first, _, gs = units[n]
                        s = hd // 2
                        if n % (UIT // 2) == 0:
                            pe.wait_ge(qk_loaded[s], CREDIT + 48 * (g + 1))
                        pe.wait_ge(exp_made[n % 2], CREDIT + g * (UIT // 2) + n // 2)
                        for i in range(len(gs)):
                            keys = slice(first * P + i * CH, first * P + (i + 1) * CH)
                            for part in range(2):
                                ins = nc.tensor.matmul(scr[n % 2][:, i * CH:(i + 1) * CH],
                                                       q_t[s][:, hd % 2, q * P:(q + 1) * P],
                                                       k_t[s][:, part, keys], start=(part == 0), stop=(part == 1))
                        ins.then_inc(scored, 1)
                    elif kind == "transpose":
                        pe.wait_ge(normed, CREDIT + g * UIT + n + 1)
                        for i, x in enumerate(units[n][4]):
                            pe.wait_ge(lo_made[x % FLIPS], CREDIT + g * per_bank[x % FLIPS] + x // FLIPS)
                            for j in range(4):
                                ins = nc.tensor.transpose(flip[x % FLIPS][:, j, :],
                                                          prob[n % 3][:, (4 * i + j) * P:(4 * i + j + 1) * P], ident[:])
                            ins.then_inc(flipped[n % 3], 1)
                    elif kind == "values":
                        ci, quarter = n
                        hd = ci // NCH
                        _, _, first, tiles, gs = units[4 * ci + 3]
                        if quarter == 0:
                            y = gs[-1]
                            pe.wait_ge(lo_made[y % FLIPS], CREDIT + g * per_bank[y % FLIPS] + y // FLIPS + 1)
                            pe.wait_ge(summed, CREDIT + g * NCI + ci)
                            if ci % (NCI // 2) == 0:
                                pe.wait_ge(vg_loaded[hd // 2], CREDIT + 32 * (g + 1))
                        for i in range(quarter * tiles // QUARTERS, (quarter + 1) * tiles // QUARTERS):
                            for part, pt in enumerate((pt_hi, pt_lo)):
                                ins = nc.tensor.matmul(out[:], v_t[hd // 2][:, first + i, :], pt[ci % 2][:, i, :],
                                                       start=(i == 0 and part == 0),
                                                       stop=(i == tiles - 1 and part == 1))
                        if quarter == QUARTERS - 1:
                            ins.then_inc(multiplied, 1)

                pe.wait_ge(ident_made, CREDIT + 2)
                over_turns(pe, plan["pe"], step, KVA, UIT)


QBUFS = 3


def finish(nc, x, p_feat, g_att, w_ao, w_out, norm_final, part, y):
    with Scope(nc, "f") as sc:
        act_hi = sc.sb("act_hi", [P, KT, T], F32R)
        act_lo = sc.sb("act_lo", [P, KT, T], F32R)
        w_hi = sc.sb("w_hi", [P, 2, KT, UNIT], F32R)
        w_lo = sc.sb("w_lo", [P, 2, KT, UNIT], F32R)
        raw = sc.sb("raw", [P, KT // 2, UNIT])
        act_raw = [sc.sb(f"act_raw{b}", [P, 2, CH]) for b in range(2)]
        add = sc.sb("add", [P, 2, CH])
        stage = sc.sb("stage", [P, QBUFS, 4, CH])
        stat = sc.sb("stat", [P, 2, 4])
        acc = [sc.pb(f"acc{b}", [P, CH]) for b in range(NB)]
        xt = [a[:].rearrange("p a b -> p (a b)") for a in act_raw]
        yt = [stage[:, 0, 2 * b:2 * b + 2, :].rearrange("p a b -> p (a b)") for b in range(2)]
        gain = add[:].rearrange("p a b -> p (a b)")

        raw_loaded = sc.sem("raw_loaded")
        w_hi_made, w_lo_made = sc.sem("w_hi_made"), sc.sem("w_lo_made")
        act_loaded = sc.sems("act_loaded", 2)
        act_hi_made = sc.sem("act_hi_made")
        act_lo_made = sc.sems("act_lo_made", 2)
        acc_full = sc.sem("acc_full")
        evacuated = sc.sems("evacuated", NB)
        gate_loaded = sc.sems("gate_loaded", QBUFS)
        add_loaded, gated = sc.sems("add_loaded", 2), sc.sem("gated")
        x_loaded, gain_loaded = sc.sems("x_loaded", 2), sc.sem("gain_loaded")
        summed, squared, mean_made, root_made, rstd_made, normed = (sc.sem(n) for n in (
            "summed", "squared", "mean_made", "root_made", "rstd_made", "normed"))
        y_stored = sc.sems("y_stored", 2)
        weights = (w_ao, w_out)
        PER_STAGE = CB * 2 * NCH
        QS = 2 * NCH
        firsts = [(c, slot, j) for c in range(NCH) for slot in range(2) for j in range(CB)]
        seconds = [(t, h) for h in range(2) for t in range(BLK)] + [(t, h) for t in range(BLK, TT) for h in range(2)]
        second_no = {th: len(firsts) + n for n, th in enumerate(seconds)}

        def unit(n, ks=range(KT)):
            return [("w", n, 0, k) for k in ks]

        def chunk(s, c, pieces=range(ACT_PCS)):
            return [("a", s, c, i) for i in pieces]

        lower, upper = range(KT // 2), range(KT // 2, KT)
        splits = (unit(0, lower) + chunk(0, 0, (0, 1)) + unit(0, upper) + chunk(0, 0, (2, 3)) + unit(1)
                  + chunk(0, 1) + chunk(0, 2) + chunk(1, 0) + chunk(1, 1) + unit(2) + unit(3) + chunk(1, 2))

        def fview(ap):
            return ap.rearrange("(b p) t -> p b t", p=P)

        def piece_no(s, c, i):
            return (s * NCH + c) * ACT_PCS + i

        def act_cut(c, i):
            return (slice(None), slice(2 * i, 2 * i + 2), slice(c * CH, (c + 1) * CH))

        def source(s, c, i):
            if s == 0:
                return act_raw[piece_no(s, c, i) % 2][:]
            return stage[:, (2 * c + i // 2) % QBUFS, 2 * (i % 2):2 * (i % 2) + 2, :]

        nc.all_engine_barrier()
        with nc.Block() as block:

            @block.sync
            def _(sp):
                def load_half(n, h):
                    if 2 * n + h > 0:
                        sp.wait_ge(w_lo_made, CREDIT + (2 * n + h) * KT // 2)
                    v = weights[n // 2].rearrange("(k p) n -> p k n", p=P)
                    sp.dma_start(raw[:], v[:, h * KT // 2:(h + 1) * KT // 2, n % 2 * UNIT:(n % 2 + 1) * UNIT])\
                        .then_inc(raw_loaded, 16)

                def load_act(s, c, pieces=range(ACT_PCS)):
                    for i in pieces:
                        pc = piece_no(s, c, i)
                        if pc >= 2:
                            sp.wait_ge(act_lo_made[pc % 2], CREDIT + pc // 2)
                        sp.dma_start(act_raw[pc % 2][:], fview(g_att)[:, 2 * i:2 * i + 2, c * CH:(c + 1) * CH])\
                            .then_inc(act_loaded[pc % 2], 16)

                def load_gate(q):
                    row = R_GM + D + q % 2 * UNIT
                    sp.dma_start(stage[:, q % QBUFS], fview(p_feat[row:row + UNIT, :])[:, :, q // 2 * CH:(q // 2 + 1) * CH])\
                        .then_inc(gate_loaded[q % QBUFS], 16)

                load_half(0, 0)
                load_act(0, 0, (0, 1))
                load_half(0, 1)
                load_act(0, 0, (2, 3))
                load_half(1, 0)
                for q in range(QBUFS):
                    load_gate(q)
                load_half(1, 1)
                load_act(0, 1)
                for q in range(QS):
                    for j in range(4):
                        m = 4 * q + j
                        if m >= 2:
                            sp.wait_ge(gated, CREDIT + m - 1)
                        row = q % 2 * UNIT + j * P
                        sp.dma_start(add[:, m % 2, :], part[row:row + P, q // 2 * CH:(q // 2 + 1) * CH])\
                            .then_inc(add_loaded[m % 2], 16)
                    if q == 0:
                        load_act(0, 2)
                        load_half(2, 0)
                    if q % 2 == 1:
                        for n in (q - 1, q):
                            if n + QBUFS < QS:
                                for i in (2 * (n % 2), 2 * (n % 2) + 1):
                                    pc = piece_no(1, n // 2, i)
                                    sp.wait_ge(act_lo_made[pc % 2], CREDIT + pc // 2 + 1)
                                load_gate(n + QBUFS)
                    if q == 4:
                        load_half(2, 1)
                        load_half(3, 0)
                sp.wait_ge(gated, CREDIT + PER_STAGE)
                sp.dma_start(gain, norm_final.to_broadcast([P, D])).then_inc(gain_loaded, 16)
                load_half(3, 1)
                for t in range(TT):
                    b = t % 2
                    if t < 2:
                        sp.wait_ge(act_lo_made[b], CREDIT + NCH * ACT_PCS // 2)
                    else:
                        sp.wait_ge(squared, CREDIT + t - 1)
                    sp.dma_start(xt[b], x[t * P:(t + 1) * P, :]).then_inc(x_loaded[b], 16)
                    if t:
                        sp.wait_ge(normed, CREDIT + t)
                        sp.dma_start(y[(t - 1) * P:t * P, :], yt[1 - b]).then_inc(y_stored[1 - b], 16)
                sp.wait_ge(normed, CREDIT + TT)
                sp.dma_start(y[(TT - 1) * P:, :], yt[(TT - 1) % 2]).then_inc(y_stored[(TT - 1) % 2], 16)
                for b in range(2):
                    sp.wait_ge(y_stored[b], CREDIT + 16 * TT // 2)

            @block.gpsimd
            def _(pool):
                for kind, s, c, k in splits:
                    if kind == "w":
                        pool.wait_ge(w_hi_made, CREDIT + s * KT + k + 1)
                        cut = (slice(None), s % 2, k, slice(None))
                        nc.gpsimd.tensor_sub(w_lo[cut], raw[:, k % (KT // 2), :], w_hi[cut].bitcast(F32))\
                            .then_inc(w_lo_made, 1)
                    elif (s, c) != (0, 0):
                        pc = piece_no(s, c, k)
                        pool.wait_ge(act_hi_made, CREDIT + pc + 1)
                        nc.gpsimd.tensor_sub(act_lo[act_cut(c, k)], source(s, c, k),
                                             act_hi[act_cut(c, k)].bitcast(F32)).then_inc(act_lo_made[pc % 2], 1)

            @block.scalar
            def _(act):
                for kind, s, c, k in splits:
                    if kind == "w":
                        act.wait_ge(raw_loaded, CREDIT + 16 * (2 * s + k // (KT // 2) + 1))
                        if s >= 2 and k == 0:
                            act.wait_ge(acc_full, CREDIT + PER_STAGE - (CB if s % 2 == 0 else 0))
                        nc.scalar.activation(w_hi[:, s % 2, k, :], raw[:, k % (KT // 2), :], ACT.Copy)\
                            .then_inc(w_hi_made, 1)
                    else:
                        pc = piece_no(s, c, k)
                        if s == 0:
                            act.wait_ge(act_loaded[pc % 2], CREDIT + 16 * (pc // 2 + 1))
                        else:
                            act.wait_ge(gated, CREDIT + 4 * (2 * c + k // 2) + 4)
                            act.wait_ge(acc_full, CREDIT + (c + 1) * 2 * CB)
                        nc.scalar.activation(act_hi[act_cut(c, k)], source(s, c, k), ACT.Copy).then_inc(act_hi_made, 1)
                for t in range(TT):
                    b = t % 2
                    act.wait_ge(summed, CREDIT + t + 1)
                    nc.scalar.activation(xt[b], yt[b], ACT.Square, accum_out=stat[:, b, 0:1]).then_inc(squared, 1)
                    act.wait_ge(mean_made, CREDIT + t + 1)
                    nc.scalar.activation(stat[:, b, 2:3], stat[:, b, 1:2], ACT.Sqrt).then_inc(root_made, 1)

            @block.vector
            def _(dve):
                for i in range(ACT_PCS):
                    dve.wait_ge(act_hi_made, CREDIT + i + 1)
                    nc.vector.tensor_sub(act_lo[act_cut(0, i)], source(0, 0, i), act_hi[act_cut(0, i)].bitcast(F32))\
                        .then_inc(act_lo_made[i % 2], 1)
                for m, (c, slot, j) in enumerate(firsts):
                    qn = m // 4
                    out = stage[:, qn % QBUFS, j, :]
                    dve.wait_ge(gate_loaded[qn % QBUFS], CREDIT + 16 * (qn // QBUFS + 1))
                    dve.wait_ge(acc_full, CREDIT + m + 1)
                    nc.vector.tensor_mul(out, out, acc[m % NB][:]).then_inc(evacuated[m % NB], 1)
                    dve.wait_ge(add_loaded[m % 2], CREDIT + 16 * (m // 2 + 1))
                    dve.wait_ge(evacuated[m % NB], CREDIT + m // NB + 1)
                    nc.vector.tensor_add(out, out, add[:, m % 2, :]).then_inc(gated, 1)
                dve.wait_ge(gain_loaded, CREDIT + 16)
                pc = piece_no(1, 1, ACT_PCS - 1)
                dve.wait_ge(act_lo_made[pc % 2], CREDIT + pc // 2 + 1)
                for t in range(TT):
                    b = t % 2
                    dve.wait_ge(x_loaded[b], CREDIT + 16 * (t // 2 + 1))
                    if t >= 2:
                        dve.wait_ge(y_stored[b], CREDIT + 16 * (t // 2))
                    for h in range(2):
                        m = second_no[t, h]
                        dve.wait_ge(acc_full, CREDIT + m + 1)
                        cols = slice(h * CH, (h + 1) * CH)
                        nc.vector.tensor_add(yt[b][:, cols], xt[b][:, cols], acc[m % NB][:]).then_inc(evacuated[m % NB], 1)
                    for h in range(2):
                        m = second_no[t, h]
                        dve.wait_ge(evacuated[m % NB], CREDIT + m // NB + 1)
                    dve.sem_inc(summed, 1)
                    dve.wait_ge(squared, CREDIT + t + 1)
                    nc.vector.tensor_scalar(stat[:, b, 1:2], stat[:, b, 0:1], 1.0 / D, EPS, ALU.mult, ALU.add)\
                        .then_inc(mean_made, 1)
                    dve.wait_ge(root_made, CREDIT + t + 1)
                    nc.vector.reciprocal(stat[:, b, 3:4], stat[:, b, 2:3]).then_inc(rstd_made, 1)
                    dve.wait_ge(rstd_made, CREDIT + t + 1)
                    nc.vector.scalar_tensor_tensor(out=yt[b], in0=yt[b], scalar=stat[:, b, 3:4], in1=gain,
                                                   op0=ALU.mult, op1=ALU.mult).then_inc(normed, 1)

            @block.tensor
            def _(pe):
                def act_ready(s, c, k):
                    pc = piece_no(s, c, k // 2)
                    pe.wait_ge(act_lo_made[pc % 2], CREDIT + pc // 2 + 1)

                for m, (c, slot, cb) in enumerate(firsts):
                    if m >= NB:
                        pe.wait_ge(evacuated[m % NB], CREDIT + m // NB)

                    def before_k(k):
                        if c == 0 and cb == 0:
                            pe.wait_ge(w_lo_made, CREDIT + slot * KT + k + 1)
                        if slot == 0 and cb == 0:
                            act_ready(0, c, k)

                    t, o = slice(c * CH, (c + 1) * CH), slice(cb * P, (cb + 1) * P)
                    product(nc, pe, acc[m % NB][:], lambda k: w_hi[:, slot, k, o], lambda k: w_lo[:, slot, k, o],
                            lambda k: act_hi[:, k, t], lambda k: act_lo[:, k, t], before_k).then_inc(acc_full, 1)
                for t, h in seconds:
                    m = second_no[t, h]
                    pe.wait_ge(evacuated[m % NB], CREDIT + m // NB)

                    def before_k(k):
                        if t == 0:
                            pe.wait_ge(w_lo_made, CREDIT + (2 + h) * KT + k + 1)
                        if h == 0 and t % BLK == 0:
                            act_ready(1, t // BLK, k)

                    o = slice(t * P, (t + 1) * P)
                    product(nc, pe, acc[m % NB][:], lambda k: act_hi[:, k, o], lambda k: act_lo[:, k, o],
                            lambda k: w_hi[:, h, k, :], lambda k: w_lo[:, h, k, :], before_k).then_inc(acc_full, 1)


def encoder_layer(nc, x, w_in, b_if, norm_pre, q_gain, k_gain, w_mo, w_ao, w_out, norm_final, rope, y):
    def scratch(name, *shape):
        return nc.dram_tensor(name, shape, F32, kind="Internal").ap()

    p_feat, p_tok = scratch("p_feat", R_END, T), scratch("p_tok", T, S_END)
    gate_rows = scratch("gate_rows", 4 * HM, T)
    neg_max, floor = scratch("neg_max", HM, NDIR, T), scratch("floor", HM, NDIR, T)
    a_cols = scratch("a_cols", HM, P, NDIR, TT)
    stacks, v_stacks = scratch("stacks", NST, P, T), scratch("v_stacks", T, KVA, P)
    g_mem, g_att = scratch("g_mem", W_M, T), scratch("g_att", W_A, T)
    part = scratch("part", D, T)
    project(nc, x, w_in, norm_pre, p_feat, p_tok, gate_rows)
    prepare_gates(nc, gate_rows, b_if, neg_max, floor, a_cols)
    mlstm(nc, p_feat, p_tok, neg_max, floor, a_cols, scratch("inverse", NDIR * CH), g_mem)
    rotate(nc, p_tok, rope, q_gain, k_gain, stacks, v_stacks, p_feat, g_mem, w_mo, part)
    attend(nc, p_feat, stacks, v_stacks, g_att)
    finish(nc, x, p_feat, g_att, w_ao, w_out, norm_final, part, y)


def rope_table(np):
    grid_w, half, theta = 64, DA // 4, 10000.0
    pos = np.concatenate([np.arange(n) for n in SEQS])
    freqs = theta ** (-np.arange(0, DA // 2, 2, dtype=np.float32) / np.float32(DA // 2))
    out = np.zeros((T, 2, 2, 2, half), np.float32)
    for axis, at in enumerate((pos // grid_w, pos % grid_w)):
        angle = at.astype(np.float32)[:, None] * freqs.astype(np.float32)
        out[:, 0, axis, :] = np.cos(angle)[:, None]
        out[:, 1, axis, 0], out[:, 1, axis, 1] = -np.sin(angle), np.sin(angle)
    return out.reshape(T, 2 * DA)


def kernel(x_prompt, x_sample, w_in, b_if, norm_pre, q_gain, k_gain, w_mo, w_ao, w_out, norm_final):
    import numpy as np
    import concourse.bacc as bacc
    from concourse.bass_utils import run_bass_kernel_spmd

    a = np.ascontiguousarray
    arrays = {
        "x": a(np.concatenate([np.asarray(x_prompt)[0], np.asarray(x_sample)[0]])),
        "w_in": a(np.asarray(w_in)[0]), "b_if": a(b_if), "norm_pre": a(norm_pre), "q_gain": a(q_gain),
        "k_gain": a(k_gain), "w_mo": a(np.asarray(w_mo)[0]), "w_ao": a(np.asarray(w_ao)[0]),
        "w_out": a(np.asarray(w_out)[0]), "norm_final": a(np.asarray(norm_final)[None, :]),
        "rope": rope_table(np),
    }
    nc = bacc.Bacc("TRN2", target_bir_lowering=False, num_devices=1)
    aps = {n: nc.dram_tensor(n, v.shape, F32, kind="ExternalInput").ap() for n, v in arrays.items()}
    y = nc.dram_tensor("y", (T, D), F32, kind="ExternalOutput").ap()
    encoder_layer(nc, y=y, **aps)
    r = run_bass_kernel_spmd(nc, [arrays], core_ids=[0])
    out = r.results[0]["y"]
    return out[None, 0:SEQS[0]], out[None, SEQS[0]:T]
```
